# Optimizing a Trainium2 kernel written in Bass

```python
import jax, jax.numpy as jnp
from jax import lax
import numpy as np

D_MODEL = 1024
BATCH = 1
SEQ = 512
DEPTH = 2

N_A_LAYERS = DEPTH // 2
N_B_LAYERS = DEPTH - N_A_LAYERS
FOX_HEADS = 16
FOX_HEAD_DIM = D_MODEL // FOX_HEADS
FOX_WIDTH = FOX_HEADS * FOX_HEAD_DIM
FOX_IN_COLS = 3 * FOX_WIDTH + FOX_HEADS
MLA_HEADS = 8
QK_NOPE_DIM = 128
QK_ROPE_DIM = 64
V_HEAD_DIM = 128
Q_LORA_RANK = 384
KV_LORA_RANK = 256
ROPE_BASE = 10000.0
D_FF = 4 * D_MODEL
Q_BLOCK = 128
EPS = 1e-6


def rms_norm(x, g):
    xf = x.astype(jnp.float32)
    y = xf * lax.rsqrt(jnp.mean(xf * xf, axis=-1, keepdims=True) + EPS)
    return (y * g.astype(jnp.float32)).astype(x.dtype)

def sq_relu_mlp(h, w_up, w_down):
    return jnp.square(jax.nn.relu(h @ w_up)) @ w_down

def rope_tables(seq_len, dim):
    inv = 1.0 / (ROPE_BASE ** (jnp.arange(0, dim, 2, dtype=jnp.float32) / dim))
    ang = jnp.arange(seq_len, dtype=jnp.float32)[:, None] * inv[None, :]
    return jnp.cos(ang), jnp.sin(ang)

def apply_rope(t, cos, sin):
    cos = cos.astype(t.dtype)
    sin = sin.astype(t.dtype)
    half = t.shape[-1] // 2
    t1, t2 = t[..., :half], t[..., half:]
    return jnp.concatenate([t1 * cos - t2 * sin, t2 * cos + t1 * sin], axis=-1)

def causal_block_attention(logits_fn, q_parts, v):
    B, S = v.shape[0], v.shape[1]
    nb = S // Q_BLOCK
    blocks = tuple(jnp.moveaxis(t.reshape((B, nb, Q_BLOCK) + t.shape[2:]), 1, 0) for t in q_parts)
    kpos = jnp.arange(S)

    def one_block(args):
        i, qb = args
        logits = logits_fn(qb)
        qpos = i * Q_BLOCK + jnp.arange(Q_BLOCK)
        logits = jnp.where(kpos[None, :] <= qpos[:, None], logits, -jnp.inf)
        p = jax.nn.softmax(logits, axis=-1).astype(v.dtype)
        return jnp.einsum('bhqk,bkhd->bqhd', p, v)

    out = lax.map(one_block, (jnp.arange(nb), blocks))
    return jnp.moveaxis(out, 0, 1).reshape((B, S) + out.shape[3:])

def fox_mixer(h, w_in, b_f, w_out):
    B, S, _ = h.shape
    proj = h @ w_in
    q = proj[..., :FOX_WIDTH].reshape(B, S, FOX_HEADS, FOX_HEAD_DIM)
    k = proj[..., FOX_WIDTH:2 * FOX_WIDTH].reshape(B, S, FOX_HEADS, FOX_HEAD_DIM)
    v = proj[..., 2 * FOX_WIDTH:3 * FOX_WIDTH].reshape(B, S, FOX_HEADS, FOX_HEAD_DIM)
    f_logit = proj[..., 3 * FOX_WIDTH:].astype(jnp.float32) + b_f.astype(jnp.float32)
    cum = jnp.cumsum(jax.nn.log_sigmoid(f_logit), axis=1)
    c_keys = jnp.transpose(cum, (0, 2, 1))
    scale = FOX_HEAD_DIM ** -0.5

    def logits_fn(qb):
        q_blk, c_blk = qb
        s = jnp.einsum('bqhd,bkhd->bhqk', q_blk, k, preferred_element_type=jnp.float32) * scale
        return s + jnp.transpose(c_blk, (0, 2, 1))[..., None] - c_keys[:, :, None, :]

    ctx = causal_block_attention(logits_fn, (q, cum), v)
    return ctx.reshape(B, S, FOX_WIDTH) @ w_out

def mla_shared_kv(stream, kv_norm_g, w_kv_a, kv_a_norm_g, w_kv_b, cos, sin):
    B, S, _ = stream.shape
    src = rms_norm(stream, kv_norm_g)
    kv_a = src @ w_kv_a
    c_kv = rms_norm(kv_a[..., :KV_LORA_RANK], kv_a_norm_g)
    k_rope = apply_rope(kv_a[..., KV_LORA_RANK:], cos, sin)
    kv_b = (c_kv @ w_kv_b).reshape(B, S, MLA_HEADS, QK_NOPE_DIM + V_HEAD_DIM)
    k_nope = kv_b[..., :QK_NOPE_DIM]
    v = kv_b[..., QK_NOPE_DIM:]
    return k_nope, k_rope, v

def mla_mixer(h, w_q_a, q_a_norm_g, w_q_b, w_out, k_nope, k_rope, v, cos, sin):
    B, S, _ = h.shape
    c_q = rms_norm(h @ w_q_a, q_a_norm_g)
    q = (c_q @ w_q_b).reshape(B, S, MLA_HEADS, QK_NOPE_DIM + QK_ROPE_DIM)
    q_nope = q[..., :QK_NOPE_DIM]
    q_rope = apply_rope(q[..., QK_NOPE_DIM:], cos[:, None, :], sin[:, None, :])
    scale = (QK_NOPE_DIM + QK_ROPE_DIM) ** -0.5

    def logits_fn(qb):
        qn, qr = qb
        s = jnp.einsum('bqhd,bkhd->bhqk', qn, k_nope, preferred_element_type=jnp.float32)
        s = s + jnp.einsum('bqhr,bkr->bhqk', qr, k_rope, preferred_element_type=jnp.float32)
        return s * scale

    ctx = causal_block_attention(logits_fn, (q_nope, q_rope), v)
    return ctx.reshape(B, S, MLA_HEADS * V_HEAD_DIM) @ w_out

def first_inputs(seed: int = 0) -> dict:
    key = jax.random.key(seed)
    ks = jax.random.split(key, 24)

    def w(k, shape, fan_in):
        return jax.random.normal(k, shape, jnp.float32) * (fan_in ** -0.5)

    def gain(k, shape):
        return 1.0 + 0.02 * jax.random.normal(k, shape, jnp.float32)

    return {
        "x": jax.random.normal(ks[0], (BATCH, SEQ, D_MODEL), jnp.float32),
        "norm_mix_g": gain(ks[1], (DEPTH, D_MODEL)),
        "norm_ffn_g": gain(ks[2], (DEPTH, D_MODEL)),
        "fox_w_in": w(ks[3], (N_A_LAYERS, D_MODEL, FOX_IN_COLS), D_MODEL),
        "fox_b_f": 1.0 + 0.1 * jax.random.normal(ks[4], (N_A_LAYERS, FOX_HEADS), jnp.float32),
        "fox_w_out": w(ks[5], (N_A_LAYERS, FOX_WIDTH, D_MODEL), FOX_WIDTH),
        "kv_norm_g": gain(ks[6], (D_MODEL,)),
        "mla_w_kv_a": w(ks[7], (D_MODEL, KV_LORA_RANK + QK_ROPE_DIM), D_MODEL),
        "mla_kv_a_norm_g": gain(ks[8], (KV_LORA_RANK,)),
        "mla_w_kv_b": w(ks[9], (KV_LORA_RANK, MLA_HEADS * (QK_NOPE_DIM + V_HEAD_DIM)), KV_LORA_RANK),
        "mla_w_q_a": w(ks[10], (N_B_LAYERS, D_MODEL, Q_LORA_RANK), D_MODEL),
        "mla_q_a_norm_g": gain(ks[11], (N_B_LAYERS, Q_LORA_RANK)),
        "mla_w_q_b": w(ks[12], (N_B_LAYERS, Q_LORA_RANK, MLA_HEADS * (QK_NOPE_DIM + QK_ROPE_DIM)), Q_LORA_RANK),
        "mla_w_out": w(ks[13], (N_B_LAYERS, MLA_HEADS * V_HEAD_DIM, D_MODEL), MLA_HEADS * V_HEAD_DIM),
        "ffn_w_up": w(ks[14], (DEPTH, D_MODEL, D_FF), D_MODEL),
        "ffn_w_down": w(ks[15], (DEPTH, D_FF, D_MODEL), D_FF),
        "final_norm_g": gain(ks[16], (D_MODEL,)),
    }

def first_block(x, norm_mix_g, norm_ffn_g, fox_w_in, fox_b_f, fox_w_out, kv_norm_g,
              mla_w_kv_a, mla_kv_a_norm_g, mla_w_kv_b, mla_w_q_a, mla_q_a_norm_g,
              mla_w_q_b, mla_w_out, ffn_w_up, ffn_w_down, final_norm_g):
    S = x.shape[1]
    cos, sin = rope_tables(S, QK_ROPE_DIM)
    k_nope = k_rope = v_shared = None
    for layer in range(DEPTH):
        h = rms_norm(x, norm_mix_g[layer])
        if layer < N_A_LAYERS:
            x = x + fox_mixer(h, fox_w_in[layer], fox_b_f[layer], fox_w_out[layer])
        else:
            b = layer - N_A_LAYERS
            x = x + mla_mixer(h, mla_w_q_a[b], mla_q_a_norm_g[b], mla_w_q_b[b], mla_w_out[b],
                              k_nope, k_rope, v_shared, cos, sin)
        x = x + sq_relu_mlp(rms_norm(x, norm_ffn_g[layer]), ffn_w_up[layer], ffn_w_down[layer])
        if layer == N_A_LAYERS - 1:
            k_nope, k_rope, v_shared = mla_shared_kv(x, kv_norm_g, mla_w_kv_a, mla_kv_a_norm_g,
                                                     mla_w_kv_b, cos, sin)
    return rms_norm(x, final_norm_g)


DEPTH_2 = 1

N_BRANCH = 4
MIX = D_MODEL // 4
ML_HEADS = 4
ML_DH = MIX // ML_HEADS
ML_CHUNK = 64
GLA_HEADS = 4
GLA_DH = MIX // GLA_HEADS
GLA_RANK = 16
GLA_TAU = 16.0
GLA_CHUNK = 16
CONF_WIDTH = 31
SC_WIDTH = 3
FFN_WIDTH = 3
FFN_HIDDEN = ((8 * D_MODEL // 3 + 255) // 256) * 256

IN_SPLITS = (
    ("ml_q", MIX), ("ml_k", MIX), ("ml_v", MIX), ("ml_o", MIX),
    ("ml_i", ML_HEADS), ("ml_f", ML_HEADS),
    ("gla_q", MIX), ("gla_k", MIX), ("gla_v", MIX), ("gla_r", MIX), ("gla_a", GLA_RANK),
    ("conf", 2 * MIX),
    ("sc", 3 * MIX),
    ("gate", N_BRANCH * D_MODEL),
)
IN_WIDTH = sum(w for _, w in IN_SPLITS)


def rms_norm_2(x, g):
    xf = x.astype(jnp.float32)
    y = xf * lax.rsqrt(jnp.mean(xf * xf, axis=-1, keepdims=True) + EPS)
    return (y * g.astype(jnp.float32)).astype(x.dtype)

def layer_norm(x, g, b):
    xf = x.astype(jnp.float32)
    mu = jnp.mean(xf, axis=-1, keepdims=True)
    xc = xf - mu
    y = xc * lax.rsqrt(jnp.mean(xc * xc, axis=-1, keepdims=True) + EPS)
    return (y * g.astype(jnp.float32) + b.astype(jnp.float32)).astype(x.dtype)

def head_rms_norm(t, g, n_heads):
    Bn, S, H, d = t.shape
    tf = t.astype(jnp.float32)
    y = tf * lax.rsqrt(jnp.mean(tf * tf, axis=-1, keepdims=True) + EPS)
    y = y * g.astype(jnp.float32).reshape(n_heads, d)
    return y.reshape(Bn, S, H * d)

def causal_dwconv(x, w):
    K, C = w.shape
    return lax.conv_general_dilated(
        x, w[:, None, :].astype(x.dtype), window_strides=(1,), padding=[(K - 1, 0)],
        dimension_numbers=("NWC", "WIO", "NWC"), feature_group_count=C)

def split_columns(proj):
    out = {}
    off = 0
    for name, width in IN_SPLITS:
        out[name] = proj[..., off:off + width]
        off += width
    return out

def split_heads(t, n_heads):
    return t.reshape(t.shape[:2] + (n_heads, t.shape[-1] // n_heads))

def to_chunks(t, L):
    Bn, S, H = t.shape[:3]
    t = t.reshape((Bn, S // L, L, H) + t.shape[3:])
    return jnp.moveaxis(t, (1, 3), (0, 2))

def from_chunks(t):
    NC, Bn, H, L = t.shape[:4]
    t = jnp.moveaxis(t, (0, 2), (1, 3))
    return t.reshape((Bn, NC * L, H) + t.shape[4:])

def mlstm_chunked(q, k, v, i_pre, f_pre):
    f32 = jnp.float32
    Bn, S, H, Dk = q.shape
    Dv = v.shape[-1]
    L = ML_CHUNK
    xs = (to_chunks(q.astype(f32) * (Dk ** -0.5), L), to_chunks(k.astype(f32), L),
          to_chunks(v.astype(f32), L), to_chunks(i_pre.astype(f32), L),
          to_chunks(jax.nn.log_sigmoid(f_pre.astype(f32)), L))
    causal = jnp.tril(jnp.ones((L, L), dtype=bool))

    def step(carry, chunk):
        C, n, m = carry
        qc, kc, vc, ic, fc = chunk
        b = jnp.cumsum(fc, axis=-1)
        logD = jnp.where(causal, b[..., :, None] - b[..., None, :] + ic[..., None, :], -jnp.inf)
        g = b + m[..., None]
        mt = jnp.maximum(g, jnp.max(logD, axis=-1))
        w_inter = jnp.exp(g - mt)
        qk = jnp.einsum('bhtd,bhsd->bhts', qc, kc) * jnp.exp(logD - mt[..., None])
        num = (w_inter[..., None] * jnp.einsum('bhtd,bhde->bhte', qc, C)
               + jnp.einsum('bhts,bhse->bhte', qk, vc))
        den = w_inter * jnp.einsum('bhtd,bhd->bht', qc, n) + jnp.sum(qk, axis=-1)
        h = num / jnp.maximum(jnp.abs(den), jnp.exp(-mt))[..., None]
        bL = b[..., -1]
        a = bL[..., None] - b + ic
        m_new = jnp.maximum(bL + m, jnp.max(a, axis=-1))
        w = jnp.exp(a - m_new[..., None])
        decay = jnp.exp(bL + m - m_new)
        C = decay[..., None, None] * C + jnp.einsum('bhs,bhsd,bhse->bhde', w, kc, vc)
        n = decay[..., None] * n + jnp.einsum('bhs,bhsd->bhd', w, kc)
        return (C, n, m_new), h

    init = (jnp.zeros((Bn, H, Dk, Dv), f32), jnp.zeros((Bn, H, Dk), f32), jnp.zeros((Bn, H), f32))
    _, h = lax.scan(step, init, xs)
    return from_chunks(h)

def gla_chunked(q, k, v, log_a):
    f32 = jnp.float32
    Bn, S, H, Dk = q.shape
    Dv = v.shape[-1]
    L = GLA_CHUNK
    xs = (to_chunks(q.astype(f32) * (Dk ** -0.5), L), to_chunks(k.astype(f32), L),
          to_chunks(v.astype(f32), L), to_chunks(log_a.astype(f32), L))
    causal = jnp.tril(jnp.ones((L, L), dtype=bool))

    def step(state, chunk):
        qc, kc, vc, lac = chunk
        b = jnp.cumsum(lac, axis=2)
        bL = b[:, :, -1:, :]
        q_dec = qc * jnp.exp(b)
        attn = jnp.where(causal, jnp.einsum('bhtd,bhsd->bhts', q_dec, kc * jnp.exp(-b)), 0.0)
        o = jnp.einsum('bhtd,bhde->bhte', q_dec, state) + jnp.einsum('bhts,bhse->bhte', attn, vc)
        k_dec = kc * jnp.exp(bL - b)
        state = jnp.exp(bL[:, :, 0, :])[..., None] * state + jnp.einsum('bhsd,bhse->bhde', k_dec, vc)
        return state, o

    _, o = lax.scan(step, jnp.zeros((Bn, H, Dk, Dv), f32), xs)
    return from_chunks(o)

def token_mixer(h, w_in, ml_i_bias, ml_f_bias, ml_norm_g, w_ml_out, gla_w_a2, gla_a_bias,
                gla_norm_g, w_gla_out, conf_dw_w, conf_dw_b, conf_ln_g, conf_ln_b, w_conf_out,
                conf_out_b, sc_dw_w, w_sc_out, merge_gate_b, w_o):
    Bn, S, _ = h.shape
    p = split_columns(h @ w_in)
    ml = mlstm_chunked(split_heads(p["ml_q"], ML_HEADS), split_heads(p["ml_k"], ML_HEADS),
                       split_heads(p["ml_v"], ML_HEADS), p["ml_i"] + ml_i_bias, p["ml_f"] + ml_f_bias)
    ml = head_rms_norm(ml, ml_norm_g, ML_HEADS).astype(h.dtype)
    y_ml = (ml * jax.nn.sigmoid(p["ml_o"])) @ w_ml_out
    log_a = jax.nn.log_sigmoid((p["gla_a"] @ gla_w_a2 + gla_a_bias).astype(jnp.float32)) / GLA_TAU
    gl = gla_chunked(split_heads(p["gla_q"], GLA_HEADS), split_heads(p["gla_k"], GLA_HEADS),
                     split_heads(p["gla_v"], GLA_HEADS), split_heads(log_a, GLA_HEADS))
    gl = head_rms_norm(gl, gla_norm_g, GLA_HEADS).astype(h.dtype)
    y_gla = (gl * jax.nn.silu(p["gla_r"])) @ w_gla_out
    a, g = jnp.split(p["conf"], 2, axis=-1)
    u = causal_dwconv(a * jax.nn.sigmoid(g), conf_dw_w) + conf_dw_b
    u = jax.nn.silu(layer_norm(u, conf_ln_g, conf_ln_b))
    y_conf = u @ w_conf_out + conf_out_b
    bg, cg, xv = jnp.split(p["sc"], 3, axis=-1)
    y_sc = (bg * causal_dwconv(cg * xv, sc_dw_w)) @ w_sc_out
    gates = jax.nn.sigmoid(p["gate"] + merge_gate_b).reshape(Bn, S, N_BRANCH, D_MODEL)
    merged = (gates[:, :, 0] * y_ml + gates[:, :, 1] * y_gla
              + gates[:, :, 2] * y_conf + gates[:, :, 3] * y_sc)
    return merged @ w_o

def conv_ffn(h, w_up, dw_w, w_down):
    u = causal_dwconv(h @ w_up, dw_w)
    a, v = jnp.split(u, 2, axis=-1)
    return (jax.nn.silu(a) * v) @ w_down

def second_inputs(seed: int = 0) -> dict:
    key = jax.random.key(seed)
    keys = list(jax.random.split(key, 40))

    def nrm(shape, scale):
        return jax.random.normal(keys.pop(), shape, jnp.float32) * scale

    L = DEPTH_2
    D = D_MODEL
    return {
        "x": nrm((BATCH, SEQ, D), 1.0),
        "c": nrm((BATCH, D), 1.0),
        "ada_w": nrm((L, D, 6 * D), 0.5 * D ** -0.5),
        "ada_b": nrm((L, 6 * D), 0.02),
        "tm_pre_g": 1.0 + nrm((L, D), 0.05),
        "tm_post_g": 1.0 + nrm((L, D), 0.05),
        "cm_pre_g": 1.0 + nrm((L, D), 0.05),
        "cm_post_g": 1.0 + nrm((L, D), 0.05),
        "w_in": nrm((L, D, IN_WIDTH), D ** -0.5),
        "ml_i_bias": nrm((L, ML_HEADS), 0.1),
        "ml_f_bias": 3.0 + nrm((L, ML_HEADS), 0.5),
        "ml_norm_g": 1.0 + nrm((L, MIX), 0.05),
        "w_ml_out": nrm((L, MIX, D), MIX ** -0.5),
        "gla_w_a2": nrm((L, GLA_RANK, MIX), GLA_RANK ** -0.5),
        "gla_a_bias": nrm((L, MIX), 0.1),
        "gla_norm_g": 1.0 + nrm((L, MIX), 0.05),
        "w_gla_out": nrm((L, MIX, D), MIX ** -0.5),
        "conf_dw_w": nrm((L, CONF_WIDTH, MIX), CONF_WIDTH ** -0.5),
        "conf_dw_b": nrm((L, MIX), 0.02),
        "conf_ln_g": 1.0 + nrm((L, MIX), 0.05),
        "conf_ln_b": nrm((L, MIX), 0.02),
        "w_conf_out": nrm((L, MIX, D), MIX ** -0.5),
        "conf_out_b": nrm((L, D), 0.02),
        "sc_dw_w": nrm((L, SC_WIDTH, MIX), SC_WIDTH ** -0.5),
        "w_sc_out": nrm((L, MIX, D), MIX ** -0.5),
        "merge_gate_b": nrm((L, N_BRANCH * D), 0.02),
        "w_o": nrm((L, D, D), D ** -0.5),
        "ffn_w_up": nrm((L, D, 2 * FFN_HIDDEN), D ** -0.5),
        "ffn_dw_w": nrm((L, FFN_WIDTH, 2 * FFN_HIDDEN), FFN_WIDTH ** -0.5),
        "ffn_w_down": nrm((L, FFN_HIDDEN, D), FFN_HIDDEN ** -0.5),
    }

def second_block(x, c, ada_w, ada_b, tm_pre_g, tm_post_g, cm_pre_g, cm_post_g, w_in, ml_i_bias,
              ml_f_bias, ml_norm_g, w_ml_out, gla_w_a2, gla_a_bias, gla_norm_g, w_gla_out,
              conf_dw_w, conf_dw_b, conf_ln_g, conf_ln_b, w_conf_out, conf_out_b, sc_dw_w,
              w_sc_out, merge_gate_b, w_o, ffn_w_up, ffn_dw_w, ffn_w_down):
    c_act = jax.nn.silu(c)
    for l in range(DEPTH_2):
        mod = (c_act @ ada_w[l] + ada_b[l])[:, None, :]
        sh_t, sc_t, g_t, sh_c, sc_c, g_c = jnp.split(mod, 6, axis=-1)
        h = rms_norm_2(x, tm_pre_g[l]) * (1.0 + sc_t) + sh_t
        y = token_mixer(h, w_in[l], ml_i_bias[l], ml_f_bias[l], ml_norm_g[l], w_ml_out[l],
                        gla_w_a2[l], gla_a_bias[l], gla_norm_g[l], w_gla_out[l], conf_dw_w[l],
                        conf_dw_b[l], conf_ln_g[l], conf_ln_b[l], w_conf_out[l], conf_out_b[l],
                        sc_dw_w[l], w_sc_out[l], merge_gate_b[l], w_o[l])
        x = x + g_t * rms_norm_2(y, tm_post_g[l])
        h = rms_norm_2(x, cm_pre_g[l]) * (1.0 + sc_c) + sh_c
        y = conv_ffn(h, ffn_w_up[l], ffn_dw_w[l], ffn_w_down[l])
        x = x + g_c * rms_norm_2(y, cm_post_g[l])
    return x


def setup_inputs(seed=0):
    out = dict(first_inputs(seed))
    for name, value in second_inputs(seed + 1).items():
        if name != "x":
            out[name + "_2"] = value
    return out


def reference(
    x, norm_mix_g, norm_ffn_g, fox_w_in, fox_b_f, fox_w_out, kv_norm_g, mla_w_kv_a,
    mla_kv_a_norm_g, mla_w_kv_b, mla_w_q_a, mla_q_a_norm_g, mla_w_q_b, mla_w_out, ffn_w_up,
    ffn_w_down, final_norm_g, c_2, ada_w_2, ada_b_2, tm_pre_g_2, tm_post_g_2, cm_pre_g_2,
    cm_post_g_2, w_in_2, ml_i_bias_2, ml_f_bias_2, ml_norm_g_2, w_ml_out_2, gla_w_a2_2,
    gla_a_bias_2, gla_norm_g_2, w_gla_out_2, conf_dw_w_2, conf_dw_b_2, conf_ln_g_2, conf_ln_b_2,
    w_conf_out_2, conf_out_b_2, sc_dw_w_2, w_sc_out_2, merge_gate_b_2, w_o_2, ffn_w_up_2,
    ffn_dw_w_2, ffn_w_down_2,
):
    x = first_block(
        x, norm_mix_g, norm_ffn_g, fox_w_in, fox_b_f, fox_w_out, kv_norm_g, mla_w_kv_a,
        mla_kv_a_norm_g, mla_w_kv_b, mla_w_q_a, mla_q_a_norm_g, mla_w_q_b, mla_w_out, ffn_w_up,
        ffn_w_down, final_norm_g,
    )
    return second_block(
        x, c_2, ada_w_2, ada_b_2, tm_pre_g_2, tm_post_g_2, cm_pre_g_2, cm_post_g_2, w_in_2,
        ml_i_bias_2, ml_f_bias_2, ml_norm_g_2, w_ml_out_2, gla_w_a2_2, gla_a_bias_2,
        gla_norm_g_2, w_gla_out_2, conf_dw_w_2, conf_dw_b_2, conf_ln_g_2, conf_ln_b_2,
        w_conf_out_2, conf_out_b_2, sc_dw_w_2, w_sc_out_2, merge_gate_b_2, w_o_2, ffn_w_up_2,
        ffn_dw_w_2, ffn_w_down_2,
    )


_drawn_inputs = setup_inputs


def setup_inputs(seed=0):
    import zlib

    import numpy as np

    out = dict(_drawn_inputs(seed))
    spreads = {}
    factors = {'norm_mix_g': 3.139,
     'kv_norm_g': 8.0,
     'mla_kv_a_norm_g': 7.94,
     'mla_q_a_norm_g': 8.0,
     'tm_post_g_2': 3.706,
     'cm_pre_g_2': 2.943,
     'cm_post_g_2': 4.022,
     'ml_i_bias_2': 64.0,
     'ml_f_bias_2': 51.592,
     'ml_norm_g_2': 8.0,
     'gla_a_bias_2': 6.506,
     'gla_norm_g_2': 8.0,
     'conf_dw_b_2': 8.0,
     'conf_ln_g_2': 8.0,
     'conf_ln_b_2': 44.5,
     'conf_out_b_2': 30.17,
     'merge_gate_b_2': 8.0}
    for name, (base, spread) in spreads.items():
        noise = np.random.default_rng([zlib.crc32(name.encode()), seed]).standard_normal(out[name].shape)
        drawn = base * np.exp(spread * noise) if base else spread * noise
        out[name] = __import__('jax').numpy.asarray(drawn.astype(out[name].dtype))
    for name, factor in factors.items():
        out[name] = (out[name] * factor).astype(out[name].dtype)
    return out
```

```python
from contextlib import ExitStack

import numpy as np

import concourse.bass as bass
from concourse import mybir

F32 = mybir.dt.float32
F32R = mybir.dt.float32r
BF16 = mybir.dt.bfloat16
I32 = mybir.dt.int32
ACT = mybir.ActivationFunctionType
ALU = mybir.AluOpType
AX_X = mybir.AxisListType.X

P = 128
T = 512
D = 1024
KT = D // P
PANEL = KT * P
QB = T // P
EPS = 1e-6
BIG = 1e30

FOX_HEADS = 16
FOX_DH = D // FOX_HEADS
FOX_PAIRS = FOX_HEADS // 2
FOX_SCALE = FOX_DH ** -0.5
MLA_HEADS = 8
NOPE = 128
ROPE = 64
VDIM = 128
Q_RANK = 384
KV_RANK = 256
QKT = Q_RANK // P
KVKT = KV_RANK // P
MLA_SCALE = (NOPE + ROPE) ** -0.5
ROPE_BASE = 10000.0
D_FF = 4 * D
FF_CHUNKS = D_FF // D

MIX = D // 4
HEADS = 4
DH = MIX // HEADS
GLA_RANK = 16
GLA_TAU = 16.0
GLA_CHUNK = 32
CHUNKS = T // GLA_CHUNK
CONF_W = 31
SC_W = 3
FFN_W = 3
HID = ((8 * D // 3 + 255) // 256) * 256
HID_T = HID // P
BRANCHES = 4
F_ROW, I_ROW, A_ROW = 0, 32, 64

RUNS = (
    ("qkv", 3 * FOX_PAIRS, PANEL),
    ("fox_out", KT, PANEL),
    ("ff_a", 2 * FF_CHUNKS * KT, PANEL),
    ("kva_qa", 3 + QKT, PANEL),
    ("mla", 2 * MLA_HEADS, None),
    ("mla_out", KT, PANEL),
    ("ff_b", 2 * FF_CHUNKS * KT, PANEL),
    ("mix_in", 28, None),
    ("merge", 5 * KT, PANEL),
    ("w_o", KT, PANEL),
    ("ffn2", 2 * HID_T + 3 * KT, None),
)
Q_COLS = QKT * (NOPE + 2 * ROPE)
KV_COLS = KVKT * (NOPE + VDIM)
PANEL0, at = {}, 0
for _name, _n, _w in RUNS:
    PANEL0[_name] = at
    at += _n
N_PANELS = at
FFN2_CHUNKS = (8, 8, HID_T - 16)
FF_ORDER = (("u", 0), ("u", 1), ("d", 0), ("u", 2), ("d", 1), ("u", 3), ("d", 2), ("d", 3))
FFN2_ORDER = (("u", 0), ("u", 1), ("d", 0), ("u", 2), ("d", 1), ("d", 2))

VEC_COLS = (
    ("mix_g0", KT), ("mix_g1", KT), ("ff_g0", KT), ("ff_g1", KT), ("kv_g", KT), ("final_g", KT),
    ("kva_g", KVKT), ("qa_g", QKT), ("ada_b", 6 * KT), ("tm_pre_g", KT), ("tm_post_g", KT),
    ("cm_pre_g", KT), ("cm_post_g", KT), ("ml_g", 2), ("gla_g", 2), ("conf_w", 2 * CONF_W),
    ("conf_b", 2), ("ln_g", 2), ("ln_b", 2), ("conf_out_b", KT), ("sc_w", 2 * SC_W),
    ("gate_b", BRANCHES * KT), ("ffn_w", FFN_W * 2 * HID_T), ("gla_b", 2),
    ("fox_bf", 1), ("ml_bi", 1), ("ml_bf", 1), ("eps", 1), ("eps2", 1), ("one", 1),
)
VEC, at = {}, 0
for _name, _n in VEC_COLS:
    VEC[_name] = at
    at += _n
N_VEC = at


def panels(w):
    k, n = w.shape
    return w.reshape(k // P, P, n // P, P).transpose(2, 1, 0, 3).reshape(-1)


def one_panel(w):
    k, n = w.shape
    return w.reshape(k // P, P, n).transpose(1, 0, 2).reshape(-1)


def lay_out(i):
    f = {k: np.asarray(v) for k, v in i.items()}
    out = {}
    s = []
    w = f["fox_w_in"][0]
    for p in range(FOX_PAIRS):
        for part in range(3):
            s.append(one_panel(w[:, part * D + p * P:part * D + (p + 1) * P]))
    w_f = w[:, 3 * D:]
    s.append(panels(f["fox_w_out"][0]))

    def ffn(layer):
        up, down = f["ffn_w_up"][layer], f["ffn_w_down"][layer]
        for what, c in FF_ORDER:
            s.append(panels(up[:, c * D:(c + 1) * D] if what == "u" else down[c * D:(c + 1) * D]))

    ffn(0)
    w = f["mla_w_kv_a"]
    swapped = np.concatenate([w[:, KV_RANK + ROPE // 2:], w[:, KV_RANK:KV_RANK + ROPE // 2]], axis=1)
    s.append(panels(np.concatenate([w, swapped], axis=1)))
    s.append(panels(f["mla_w_q_a"][0]))
    wq = f["mla_w_q_b"][0].reshape(Q_RANK, MLA_HEADS, NOPE + ROPE)
    wkv = f["mla_w_kv_b"].reshape(KV_RANK, MLA_HEADS, NOPE + VDIM)
    for h in range(MLA_HEADS):
        q = wq[:, h]
        s.append(one_panel(np.concatenate([q, q[:, NOPE + ROPE // 2:], q[:, NOPE:NOPE + ROPE // 2]], axis=1)))
        s.append(one_panel(wkv[:, h]))
    s.append(panels(f["mla_w_out"][0]))
    ffn(1)
    w = f["w_in_2"][0]
    ml, gla = w[:, 0:4 * MIX], w[:, 4 * MIX + 2 * HEADS:8 * MIX + 2 * HEADS]
    w_if = w[:, 4 * MIX:4 * MIX + 2 * HEADS]
    at = 8 * MIX + 2 * HEADS
    w_a = w[:, at:at + GLA_RANK]
    at += GLA_RANK
    conf, sc = w[:, at:at + 2 * MIX], w[:, at + 2 * MIX:at + 5 * MIX]
    gate = w[:, at + 5 * MIX:]
    narrow = np.zeros((D, P), np.float32)
    narrow[:, F_ROW:F_ROW + HEADS], narrow[:, I_ROW:I_ROW + HEADS] = w_if[:, HEADS:], w_if[:, :HEADS]
    narrow[:, A_ROW:A_ROW + GLA_RANK] = w_a
    for half in range(2):
        s.append(one_panel(narrow[half * D // 2:(half + 1) * D // 2]))
    for part in (conf, sc, ml, gla):
        s.append(panels(part))
    for j in range(KT):
        cols = slice(j * P, (j + 1) * P)
        for b in range(BRANCHES):
            s.append(one_panel(gate[:, b * D + j * P:b * D + (j + 1) * P]))
        branch = [f[n][0][:, cols] for n in ("w_ml_out_2", "w_gla_out_2", "w_conf_out_2", "w_sc_out_2")]
        s.append(one_panel(np.concatenate(branch, axis=0)))
    s.append(panels(f["w_o_2"][0]))
    up, down = f["ffn_w_up_2"][0], f["ffn_w_down_2"][0]
    first = np.cumsum((0,) + FFN2_CHUNKS)
    for what, c in FFN2_ORDER:
        if what == "u":
            for j in range(first[c], first[c + 1]):
                s.append(panels(up[:, j * P:(j + 1) * P]))
                s.append(panels(up[:, HID + j * P:HID + (j + 1) * P]))
        else:
            s.append(panels(down[first[c] * P:first[c + 1] * P]))
    out["wstream"] = np.concatenate(s)
    out["wsmall"] = one_panel(w_f).reshape(P, -1)
    out["ada"] = np.ascontiguousarray(f["ada_w_2"][0].T)
    out["gla_a2"] = np.ascontiguousarray(f["gla_w_a2_2"][0])
    out["cvec"] = np.ascontiguousarray(f["c_2"])
    out["xT"] = np.ascontiguousarray(f["x"][0].T.reshape(KT, P, T).transpose(1, 0, 2)).reshape(P, KT * T)

    v = np.zeros((P, N_VEC), np.float32)

    def put(name, x):
        x = np.asarray(x).reshape(-1)
        v[:, VEC[name]:VEC[name] + x.size // P] = x.reshape(-1, P).T

    for name, x in (
        ("mix_g0", f["norm_mix_g"][0]), ("mix_g1", f["norm_mix_g"][1]), ("ff_g0", f["norm_ffn_g"][0]),
        ("ff_g1", f["norm_ffn_g"][1]), ("kv_g", f["kv_norm_g"]), ("final_g", f["final_norm_g"]),
        ("kva_g", f["mla_kv_a_norm_g"]), ("qa_g", f["mla_q_a_norm_g"]), ("ada_b", f["ada_b_2"]),
        ("tm_pre_g", f["tm_pre_g_2"]), ("tm_post_g", f["tm_post_g_2"]), ("cm_pre_g", f["cm_pre_g_2"]),
        ("cm_post_g", f["cm_post_g_2"]), ("ml_g", f["ml_norm_g_2"]), ("gla_g", f["gla_norm_g_2"]),
        ("conf_w", f["conf_dw_w_2"]), ("conf_b", f["conf_dw_b_2"]), ("ln_g", f["conf_ln_g_2"]),
        ("ln_b", f["conf_ln_b_2"]), ("conf_out_b", f["conf_out_b_2"]), ("sc_w", f["sc_dw_w_2"]),
        ("gate_b", f["merge_gate_b_2"]), ("ffn_w", f["ffn_dw_w_2"]), ("gla_b", f["gla_a_bias_2"]),
    ):
        put(name, x)
    v[0:FOX_HEADS, VEC["fox_bf"]] = f["fox_b_f"][0]
    v[I_ROW:I_ROW + HEADS, VEC["ml_bi"]] = f["ml_i_bias_2"][0]
    v[F_ROW:F_ROW + HEADS, VEC["ml_bf"]] = f["ml_f_bias_2"][0]
    v[:, VEC["eps"]] = EPS
    v[:, VEC["eps2"]] = EPS * EPS
    v[:, VEC["one"]] = 1.0
    out["vecs"] = v

    r = np.arange(P)
    out["ident"] = np.eye(P, dtype=np.float32)
    out["mask_q"] = np.where(r[None, :] > r[:, None], BIG, 0.0).astype(np.float32)
    out["mask_k"] = np.where(r[:, None] > r[None, :], -BIG, 0.0).astype(np.float32)
    out["fold"] = (r[:, None] % 64 == r[None, :] % 64).astype(np.float32)
    out["halves"] = (r[:, None] // 64 == r[None, :] // 64).astype(np.float32)
    same = r[:, None] // GLA_CHUNK == r[None, :] // GLA_CHUNK
    out["mask_gla"] = (same & (r[:, None] <= r[None, :])).astype(np.int32)
    out["chunk_start"] = np.tile((np.arange(T) % GLA_CHUNK != 0).astype(np.float32), (P, 1))
    inv = 1.0 / (ROPE_BASE ** (np.arange(0, ROPE, 2, dtype=np.float32) / np.float32(ROPE)))
    ang = np.arange(T, dtype=np.float32)[:, None] * inv[None, :].astype(np.float32)
    cos, sin = np.cos(ang).T.astype(np.float32), np.sin(ang).T.astype(np.float32)
    out["rope"] = np.concatenate([cos, cos, -sin, sin], axis=0)
    sel = np.zeros((HEADS, HEADS * P), np.float32)
    for h in range(HEADS):
        sel[h, h * P:(h + 1) * P] = 1.0
    out["sel"] = sel
    return out


class Steps:

    def __init__(self, sem):
        self.sem, self.count, self.moved = sem, 0, 0

    def mark(self, ins):
        ins.then_inc(self.sem, 1)
        self.count += 1
        return self.moved + self.count

    def enter(self, turn, marks):
        self.start, self.marks = self.count, marks
        self.moved = turn * marks

    def leave(self, turns):
        assert self.count - self.start == self.marks, (self.count - self.start, self.marks)
        self.count = self.start + self.marks * turns
        self.moved = 0


def program(nc, d, out, crow):
    with ExitStack() as ctx:
        def sb(name, shape, dt=F32):
            return ctx.enter_context(nc.sbuf_tensor(name, shape, dt))

        def sem(name):
            return ctx.enter_context(nc.semaphore(name))

        x = sb("x", [P, KT, T])
        b_hi = [sb(f"b_hi{i}", [P, KT, T], F32R) for i in range(3)]
        b_lo = [sb(f"b_lo{i}", [P, KT, T], F32R) for i in range(3)]
        w_raw = [sb(f"w_raw{i}", [P, PANEL]) for i in range(2)]
        w_hi = [sb(f"w_hi{i}", [P, PANEL], F32R) for i in range(2)]
        w_lo = [sb(f"w_lo{i}", [P, PANEL], F32R) for i in range(2)]
        SM = FOX_HEADS
        ws_raw = sb("ws_raw", [P, KT * SM])
        ws_hi = sb("ws_hi", [P, KT * SM], F32R)
        ws_lo = sb("ws_lo", [P, KT * SM], F32R)
        vec = sb("vec", [P, N_VEC])
        ident = sb("ident", [P, P])
        mask_q = sb("mask_q", [P, P])
        ident_b, mask_b = sb("ident_b", [P, P], BF16), sb("mask_b", [P, P], BF16)
        ones_sq = sb("ones_sq", [P, P])
        small = sb("small", [P, 64])
        ARENA = 32
        arena = sb("arena", [P, ARENA, T])
        bank = [ctx.enter_context(nc.psum_tensor(f"bank{i}", [P, T], F32)) for i in range(8)]
        acc = bank[0:2]
        s_bank = bank[2:5]
        t_bank = bank[5:7]
        c_bank = bank[7]

        def ar(i, n=1):
            return arena[:, i:i + n, :].rearrange("p a t -> p (a t)")

        def col(name, k=0):
            return vec[:, VEC[name] + k:VEC[name] + k + 1]

        def cold(name, k):
            return vec[:, bass.ds(k + VEC[name], 1)]

        rstd, std, ssum = ar(0), ar(1), ar(2)
        sq = [ar(3), ar(4)]
        eps = col("eps")
        ff_t = [ar(6), ar(7)]
        ff_s = [ar(8), ar(9)]
        ada_w = [ar(10, 2), ar(12, 2)]
        ada_p = ar(14, 2)
        ada_c = ar(16, 2)
        mod = sb("mod", [P, 6 * KT])
        qa = [[ar(6 + 2 * m + h) for h in range(2)] for m in range(2)]
        ka = [[ar(10 + 2 * m + h) for h in range(2)] for m in range(2)]
        v_t = ar(14)
        v_tok = [ar(15), ar(16)]
        CAUSAL = P * QB * (QB + 1) // 2
        flat = arena[:, 17:27, :].rearrange("p a t -> p (a t)")
        probs = [flat[:, CAUSAL * m:CAUSAL * (m + 1)] for m in range(2)]
        probs_t = [flat[:, CAUSAL * (2 + m):CAUSAL * (3 + m)] for m in range(2)]
        fz = [ar(27 + i)[0:FOX_HEADS, :] for i in range(4)]
        rope, fold_t = ar(27), ar(28)
        rope_q = ar(29)
        k_rope = ar(30)
        rstd_kv = ar(31)
        low = [ar(17 + i) for i in range(QKT + KVKT)]
        kr_raw = ar(22)
        low_sum = ar(23)
        kr_tmp = ar(24)
        halves, mask_k, gla_a2 = ar(5)[:, 0:P], ar(5)[:, P:2 * P], ar(5)[32:32 + GLA_RANK, 2 * P:2 * P + MIX]
        chunk_start = ar(6)
        sel = ar(7)[0:HEADS, :]
        mask_gla = sb("mask_gla", [P, P], I32)
        sq_g, ssum_g, rstd_f = [ar(12), ar(13)], ar(14), ar(31)
        mod_t = [ar(8), ar(9)]
        mod_y = [ar(10), ar(11)]
        conf_a, conf_g = [ar(10), ar(11)], [ar(12), ar(13)]
        sc_b, sc_c, sc_x = [ar(14), ar(15)], [ar(29), ar(30)], [ar(8), ar(9)]
        CONF_PAD, SC_PAD = T + CONF_W - 1, T + SC_W - 1
        pads = arena[:, 24:29, :].rearrange("p a t -> p (a t)")
        conf_pad = pads[:, 0:2 * CONF_PAD]
        sc_pad = pads[:, 2 * CONF_PAD:2 * (CONF_PAD + SC_PAD)]
        conf_u, sc_u = conf_a, sc_c
        ml_q, ml_k, ml_vt, ml_o = [ar(16), ar(17)], [ar(18), ar(19)], [ar(20), ar(21)], [ar(22), ar(23)]
        ml_v = [ar(3), ar(4)]
        gla_q, gla_k, gla_vt, gla_r = [ar(8), ar(9)], [ar(12), ar(13)], [ar(29), ar(30)], [ar(14), ar(15)]
        gla_v = [ar(24), ar(25)]
        gla_a = ar(7)[32:32 + GLA_RANK, :]
        row_z, row_b, row_u = ar(0)[0:HEADS, :], ar(1)[0:HEADS, :], ar(2)[0:HEADS, :]
        u_col = small[:, 32:32 + QB * HEADS]
        ml_w = [pads[:, CAUSAL * m:CAUSAL * (m + 1)] for m in range(2)]
        ml_den, ml_h, ml_s = ar(31), ar(10), ar(11)
        gla_z, gla_t, gla_b = [ar(16), ar(25)], [ar(17), ar(26)], [ar(18), ar(27)]
        gla_e = [[ar(i) for i in (19, 20, 21, 22)], [ar(i) for i in (28, 31, 10, 11)]]
        gla_u, gla_s = [ar(16, 2), ar(25, 2)], [ar(23, 2), ar(3, 2)]
        gla_w = [ar(0), ar(1)]
        gla_decay = [small[:, 0:CHUNKS], small[:, CHUNKS:2 * CHUNKS]]
        gate_bank, branch_bank = s_bank + [c_bank], acc + t_bank
        gate = [[ar(8 + 4 * m + b) for b in range(BRANCHES)] for m in range(2)]
        merged = [ar(5), ar(6)]
        y_at = 16
        hid_a, hid_v = ar(8), ar(9)
        ml_s_std = ar(31)
        rmin, rsum, rinv = small[:, 0:8], small[:, 8:16], small[:, 16:24]

        P_AT = [P * i * (i + 1) // 2 for i in range(QB)]
        T_AT = [0, P * QB, 2 * P * QB, P * (2 * QB - 1)]

        const_in, vec_in, rope_in = sem("const_in"), sem("vec_in"), sem("rope_in")
        X_PARTS = 4
        x_in = [sem(f"x_in{i}") for i in range(X_PARTS)]
        w_in = [sem("w_in0"), sem("w_in1")]
        w_hi_done, w_lo_done = sem("w_hi_done"), sem("w_lo_done")
        ws_hi_done, ws_lo_done = sem("ws_hi_done"), sem("ws_lo_done")
        mm_done, acc_free = sem("mm_done"), sem("acc_free")
        prep_hi, prep_lo = sem("prep_hi"), sem("prep_lo")
        norm_sum, norm_std, norm_rstd = sem("norm_sum"), sem("norm_std"), sem("norm_rstd")
        f_mm, f_free, f_abs, f_ln, f_cum = (sem(n) for n in ("f_mm", "f_free", "f_abs", "f_ln", "f_cum"))
        crow_out, ones_set = sem("crow_out"), sem("ones_set")
        crow_in = [sem("crow_in0"), sem("crow_in1")]
        s_ready, row_min, p_exp, p_ready = (sem(n) for n in ("s_ready", "row_min", "p_exp", "p_ready"))
        t_ready, t_free, pv_done, ctx_hi, ctx_lo = (
            sem(n) for n in ("t_ready", "t_free", "pv_done", "ctx_hi", "ctx_lo"))
        sq_hi, hid_lo = sem("sq_hi"), sem("hid_lo")
        ada_in = [sem("ada_in0"), sem("ada_in1")]
        ada_cin, ada_act, ada_done = sem("ada_cin"), sem("ada_act"), sem("ada_done")
        kr_mm, kr_done = sem("kr_mm"), sem("kr_done")
        ff_sq = sem("ff_sq")
        ada_silu, crow_free, sum_clear = sem("ada_silu"), sem("crow_free"), sem("sum_clear")
        act_step, dve_step = sem("act_step"), sem("dve_step")
        x_done = sem("x_done")
        out_done = sem("out_done")
        const2_in, pads_set = sem("const2_in"), sem("pads_set")
        y_normed = sem("y_normed")
        both_sum, cm_sq, cm_added = sem("both_sum"), sem("cm_sq"), sem("cm_added")
        mod_ready, h_tmp, h_hi, h_lo = (sem(n) for n in ("mod_ready", "h_tmp", "h_hi", "h_lo"))
        mix_free, rows_in = sem("mix_free"), sem("rows_in")
        pad_ready, conv_done = sem("pad_ready"), sem("conv_done")
        ln_mean, ln_dev, ln_sq, ln_var, ln_std, ln_out, ln_act, ln_hi, ln_lo = (
            sem(n) for n in ("ln_mean", "ln_dev", "ln_sq", "ln_var", "ln_std", "ln_out", "ln_act", "ln_hi", "ln_lo"))
        sc_out, sc_hi, sc_lo = sem("sc_out"), sem("sc_hi"), sem("sc_lo")
        row_abs, row_ln, row_u_done, row_max, row_floor, row_em = (
            sem(n) for n in ("row_abs", "row_ln", "row_u_done", "row_max", "row_floor", "row_em"))
        u_turned, u_read, v_turned, v_read = (sem(n) for n in ("u_turned", "u_read", "v_turned", "v_read"))
        d_ready, w_exp, qk_ready, a_ready, head_ctx = (
            sem(n) for n in ("d_ready", "w_exp", "qk_ready", "a_ready", "head_ctx"))
        den_abs, head_h, head_sq, head_sum, head_std, head_out, head_hi, head_lo = (
            sem(n) for n in ("den_abs", "head_h", "head_sq", "head_sum", "head_std", "head_out", "head_hi", "head_lo"))
        gz_ready, gz_in, gz_abs, gz_ln, gz_sum, g_exp, g_scaled = (
            sem(n) for n in ("gz_ready", "gz_in", "gz_abs", "gz_ln", "gz_sum", "g_exp", "g_scaled"))
        gw_set, gs_ready, gs_read, kd_turned, kd_read = (
            sem(n) for n in ("gw_set", "gs_ready", "gs_read", "kd_turned", "kd_read"))
        gu_ready, gu_read, g_state, g_out = (sem(n) for n in ("gu_ready", "gu_read", "g_state", "g_out"))
        gate_done, branch_read, merge_out, merge_hi, merge_lo = (
            sem(n) for n in ("gate_done", "branch_read", "merge_out", "merge_hi", "merge_lo"))
        tap_last, hid_silu, hid_out, hid_hi = (sem(n) for n in ("tap_last", "hid_silu", "hid_out", "hid_hi"))
        N_CONST = 3
        N_CONST2 = 6

        TILE0 = {"qkv": 0, "fox_out": 24, "ff_a": 32, "kva_qa": 96, "mla": 102, "mla_out": 134, "ff_b": 142,
                 "mix_in": 206}
        TILE0["merge"] = TILE0["mix_in"] + 28
        TILE0["w_o"] = TILE0["merge"] + 2 * BRANCHES * KT
        TILE0["ffn2"] = TILE0["w_o"] + KT
        FREE0 = dict(TILE0, w_o=TILE0["mix_in"], ffn2=TILE0["mix_in"] + KT)
        NARROW, CONF, SC, ML, GLA = 0, 2, 6, 12, 20

        HEAD0 = {"fox": 0, "mla": FOX_HEADS}
        CTX0 = {"fox": 0, "mla": FOX_PAIRS}
        T0_MLA = 7 * FOX_PAIRS
        PREP0 = {"fox": 0, "ff_a": KT, "mla": 2 * KT, "ckv": 3 * KT, "cq": 3 * KT + KVKT,
                 "ff_b": 3 * KT + KVKT + QKT}
        PREP0["final"] = PREP0["ff_b"] + KT
        PREP0["mix_y"] = PREP0["final"] + KT
        PREP0["ffn_y"] = PREP0["mix_y"] + KT
        NORM = {"fox": 0, "ff_a": 1, "mla": 2, "ckv": 3, "cq": 4, "ff_b": 5, "x2": 6,
                "final": 7, "mix_y": 8, "cm": 9, "ffn_y": 10}
        HID0 = {"ff_a": 0, "ff_b": FF_CHUNKS * KT, "ffn2": 2 * FF_CHUNKS * KT}
        HID_AT = [sum(FFN2_CHUNKS[:c]) for c in range(len(FFN2_CHUNKS))]
        FFN2_STEPS, first = [], 0
        for what, c in FFN2_ORDER:
            FFN2_STEPS.append((what, c, first))
            first += 2 * FFN2_CHUNKS[c] if what == "u" else KT

        wflat = d["wstream"]

        block = ctx.enter_context(nc.Block())

        def load_x(eng, i):
            w = KT * T // X_PARTS
            eng.dma_start(x[:].rearrange("p k t -> p (k t)")[:, i * w:(i + 1) * w], d["xT"][:, i * w:(i + 1) * w])\
               .then_inc(x_in[i], 16)

        @block.sync
        def _(sp):
            sp.dma_start(vec[:], d["vecs"]).then_inc(vec_in, 16)
            load_x(sp, 1)

            def load(slot, g, at, width):
                if not (isinstance(g, int) and g < 2):
                    sp.wait_ge(w_lo_done, g - 1)
                src = wflat[bass.ds(at, P * width)].rearrange("(p c) -> p c", p=P)
                sp.dma_start(w_raw[slot][:, 0:width], src).then_inc(w_in[slot], 16)

            for s in range(2):
                load(s, s, s * P * PANEL, PANEL)
            sp.dma_start(ws_raw[:], d["wsmall"]).then_inc(const_in, 16)
            sp.dma_start(ident[:], d["ident"]).then_inc(const_in, 16)
            sp.dma_start(mask_q[:], d["mask_q"]).then_inc(const_in, 16)

            def load_run(first, n):
                assert first % 2 == 0 and n % 2 == 0
                with sp.Fori(first // 2, (first + n) // 2) as half:
                    for s in range(2):
                        load(s, 2 * half + s, (2 * half + s) * (P * PANEL), PANEL)

            n_ada, ada0 = 6 * KT, PANEL0["ff_a"] + KT
            load_run(2, ada0 - 2)
            sp.wait_ge(s_ready, 3 * FOX_HEADS)
            with sp.Fori(0, n_ada // 2) as half:
                for s in range(2):
                    load(s, 2 * half + (ada0 + s), (2 * half + (ada0 + s)) * (P * PANEL), PANEL)
                    sp.wait_ge(ada_done, 2 * half + s)
                    sp.dma_start(ada_w[s], d["ada"][bass.ds((2 * half + s) * P, P), :]).then_inc(ada_in[s], 16)
            load_run(ada0 + n_ada, PANEL0["mla"] - ada0 - n_ada)
            base = PANEL0["mla"] * P * PANEL
            with sp.Fori(0, MLA_HEADS) as h:
                load(0, 2 * h + PANEL0["mla"], h * (P * (Q_COLS + KV_COLS)) + base, Q_COLS)
                load(1, 2 * h + (PANEL0["mla"] + 1), h * (P * (Q_COLS + KV_COLS)) + (base + P * Q_COLS), KV_COLS)
            base += MLA_HEADS * P * (Q_COLS + KV_COLS)
            with sp.Fori(0, (PANEL0["mix_in"] - PANEL0["mla_out"]) // 2) as half:
                for s in range(2):
                    load(s, 2 * half + (PANEL0["mla_out"] + s), (2 * half + s) * (P * PANEL) + base, PANEL)
            base += (PANEL0["mix_in"] - PANEL0["mla_out"]) * P * PANEL
            for s in range(2):
                load(s, PANEL0["mix_in"] + s, base + s * (P * PANEL // 2), PANEL // 2)
            base += P * PANEL
            first, last = PANEL0["mix_in"] + 2, N_PANELS - KT
            with sp.Fori(0, (last - first) // 2) as half:
                for s in range(2):
                    load(s, 2 * half + (first + s), (2 * half + s) * (P * PANEL) + base, PANEL)
            base += (last - first) * P * PANEL
            width = FFN2_CHUNKS[-1] * P
            with sp.Fori(0, KT // 2) as half:
                for s in range(2):
                    load(s, 2 * half + (last + s), (2 * half + s) * (P * width) + base, width)
            with sp.Fori(0, KT) as k:
                sp.wait_ge(x_done, k + (2 * KT + 1))
                sp.dma_start(out[:, bass.ds(k * T, T)], x[:, bass.ds(k, 1), :].rearrange("p a t -> p (a t)"))\
                  .then_inc(out_done, 16)
            sp.wait_ge(out_done, 16 * KT)

        @block.gpsimd
        def _(pool):
            pool.memset(fz[1], 1.0).then_inc(ones_set, 1)
            pool.memset(ones_sq[:], 1.0).then_inc(ones_set, 1)
            pool.wait_ge(f_cum, 2)
            pool.wait_ge(ones_set, 2)
            pool.dma_start(crow[:, 0, :], fz[0]).then_inc(crow_out, 16)
            pool.dma_start(crow[:, 1, :], fz[1]).then_inc(crow_out, 16)
            pool.dma_start(crow[:, 2, :], fz[1]).then_inc(crow_out, 16)
            pool.dma_start(crow[:, 3, :], fz[2]).then_inc(crow_out, 16)
            pool.wait_ge(crow_out, 64)

            def rows(p, m):
                for at, dst in ((0, qa), (2, ka)):
                    for h in range(2):
                        src = crow[bass.ds(2 * p + h, 1), at:at + 2, :].rearrange("a r t -> (a r) t")
                        pool.dma_start(dst[m][h][FOX_DH:FOX_DH + 2, :], src).then_inc(crow_in[m], 16)

            rows(0, 0)
            rows(1, 1)
            with pool.Fori(1, FOX_PAIRS // 2) as pp:
                for m in range(2):
                    pool.wait_ge(s_ready, 12 * pp + (6 * m - 6))
                    rows(2 * pp + m, m)
            pool.wait_ge(ctx_lo, FOX_PAIRS)
            pool.dma_start(ada_c, d["cvec"].to_broadcast([P, D])).then_inc(ada_cin, 16)
            pool.wait_ge(ada_done, 6 * KT)
            pool.dma_start(rope, d["rope"]).then_inc(rope_in, 16)
            pool.dma_start(fold_t[:, 0:P], d["fold"]).then_inc(rope_in, 16)

            pool.wait_ge(hid_lo, HID0["ffn2"])
            for dst, name in ((halves, "halves"), (mask_k, "mask_k"), (gla_a2, "gla_a2"), (chunk_start, "chunk_start"),
                              (sel, "sel"), (mask_gla[:], "mask_gla")):
                pool.dma_start(dst, d[name]).then_inc(const2_in, 16)
            for i in range(2):
                pool.memset(conf_pad[:, i * CONF_PAD:i * CONF_PAD + CONF_W - 1], 0.0).then_inc(pads_set, 1)
                pool.memset(sc_pad[:, i * SC_PAD:i * SC_PAD + SC_W - 1], 0.0).then_inc(pads_set, 1)
            pool.wait_ge(head_ctx, HEADS)
            for w in gla_w:
                pool.memset(w, 0.0).then_inc(gw_set, 1)
            for norm in ("mix_y", "ffn_y"):
                pool.wait_ge(norm_rstd, NORM[norm] + 1)
                with pool.Fori(0, KT // 2) as half:
                    y = arena[:, bass.ds(2 * half + (y_at + 1), 1), :].rearrange("p a t -> p (a t)")
                    pool.tensor_tensor(y, y, rstd, ALU.mult).then_inc(y_normed, 1)

        @block.tensor
        def _(pe):
            def products(dst, slot, n, rhs_hi, rhs_lo, at, step, width=P, before_k=None):
                for k in range(n):
                    if before_k is not None:
                        before_k(k)
                    c = at + k * step
                    whi, wlo = w_hi[slot][:, c:c + width], w_lo[slot][:, c:c + width]
                    nc.tensor.matmul(dst, whi, rhs_hi(k), start=(k == 0), stop=False)
                    nc.tensor.matmul(dst, whi, rhs_lo(k), start=False, stop=False)
                    last = nc.tensor.matmul(dst, wlo, rhs_hi(k), start=False, stop=(k == n - 1))
                return last

            def panel_ready(g):
                pe.wait_ge(w_lo_done, g + 1)

            def bank_free(t):
                if not (isinstance(t, int) and t < 2):
                    pe.wait_ge(acc_free, t - 1)

            def tile(g, t, slot, buf, off=0, n=KT, before_k=None, free=None):
                panel_ready(g)
                bank_free(t if free is None else free)
                products(acc[slot][:], slot, n, lambda k: b_hi[buf][:, off + k, :],
                         lambda k: b_lo[buf][:, off + k, :], 0, P, before_k=before_k).then_inc(mm_done, 1)

            def begin(run, s, buf, k0, k1):
                if k0 == 0:
                    panel_ready(PANEL0[run] + s)
                    bank_free(TILE0[run] + s)
                for k in range(k0, k1):
                    pe.wait_ge(ctx_lo, CTX0["fox" if run == "fox_out" else "mla"] + k + 1)
                    whi, wlo = w_hi[s][:, k * P:(k + 1) * P], w_lo[s][:, k * P:(k + 1) * P]
                    nc.tensor.matmul(acc[s][:], whi, b_hi[buf][:, k, :], start=(k == 0), stop=False, skip_group_check=True)
                    nc.tensor.matmul(acc[s][:], whi, b_lo[buf][:, k, :], start=False, stop=False, skip_group_check=True)
                    last = nc.tensor.matmul(acc[s][:], wlo, b_hi[buf][:, k, :], start=False, stop=(k == KT - 1),
                                            skip_group_check=True)
                if k1 == KT:
                    last.then_inc(mm_done, 1)

            def segment(run, first, n, buf, lead=None, before_k=None, depth=KT, begun=False):
                g0, t0, f0 = PANEL0[run] + first, TILE0[run] + first, FREE0[run] + first
                start = 1 if begun else 0
                if lead is not None or before_k is not None:
                    tile(g0, t0, 0, buf, n=depth, before_k=before_k, free=f0)
                    if lead is not None:
                        lead()
                    tile(g0 + 1, t0 + 1, 1, buf, n=depth, free=f0 + 1)
                    start = 1
                with pe.Fori(start, n // 2) as half:
                    for s in range(2):
                        tile(2 * half + (g0 + s), 2 * half + (t0 + s), s, buf, n=depth, free=2 * half + (f0 + s))

            def ready_k(base):
                return lambda k: pe.wait_ge(prep_lo, base + k + 1)

            def sum_squares(norm, prepared, squares=ssum):
                pe.wait_ge(prep_lo, prepared)
                if norm == "fox":
                    pe.wait_ge(ones_set, 2)
                else:
                    pe.wait_ge(norm_std, NORM[norm])
                    pe.wait_ge(ctx_lo, CTX0["mla"] + (MLA_HEADS if NORM[norm] >= NORM["ff_b"] else 0))
                nc.tensor.matmul(c_bank[:], ones_sq[:], squares, start=True, stop=True).then_inc(norm_sum, 1)

            def logits(n, m, h, kind):
                for u, rows in enumerate(((3,), (2,), (1, 0))):
                    if not (isinstance(n, int) and n == 0):
                        pe.wait_ge(p_exp, 3 * n + (u - 2))
                    for qb in rows:
                        w = P * (qb + 1)
                        at = 0 if qb else 2 * P
                        dst = s_bank[u][:, at:at + w]
                        q = slice(P * qb, P * (qb + 1))
                        if kind == "fox":
                            r = FOX_DH + 2
                            nc.tensor.matmul(dst, qa[m][h][0:r, q], ka[m][h][0:r, 0:w], start=(qb != 0), stop=False,
                                             skip_group_check=True)
                        else:
                            nc.tensor.matmul(dst, qa[m][0][:, q], ka[m][0][:, 0:w], start=(qb != 0), stop=False,
                                             skip_group_check=True)
                            nc.tensor.matmul(dst, qa[m][1][:, q], k_rope[:, 0:w], start=False, stop=False,
                                             skip_group_check=True)
                        last = nc.tensor.matmul(s_bank[u][:, at + w - P:at + w], ident_b[:], mask_b[:],
                                                start=False, stop=True, skip_group_check=True)
                    last.then_inc(s_ready, 1)

            def turn_free(c):
                if not (isinstance(c, int) and c < 2):
                    pe.wait_ge(t_free, c - 1)

            def turn_probs(n, m, c, par):
                pe.wait_ge(p_ready, n + 1)
                for u, blocks in enumerate(((0,), (1, 3), (2,))):
                    turn_free(c + u)
                    for kb in blocks:
                        for qb in range(kb, QB):
                            at = T_AT[kb] - T_AT[blocks[0]] + P * (qb - kb)
                            src = probs[m][:, P_AT[qb] + P * kb:P_AT[qb] + P * (kb + 1)]
                            last = nc.tensor.transpose(t_bank[(par + u) % 2][:, at:at + P], src, ident[:])
                    last.then_inc(t_ready, 1)

            def turn_values(t, c, par):
                pe.wait_ge(acc_free, t + 1)
                turn_free(c)
                for kb in range(QB):
                    last = nc.tensor.transpose(t_bank[par][:, P * kb:P * (kb + 1)], v_t[:, P * kb:P * (kb + 1)], ident[:])
                last.then_inc(t_ready, 1)

            def context(n, m, vm, c_end, lo, width, ctx_before):
                pe.wait_ge(t_free, c_end)
                if ctx_before is not None:
                    pe.wait_ge(ctx_lo, ctx_before)
                for kb in range(QB):
                    w = T - P * kb
                    last = nc.tensor.matmul(c_bank[lo:lo + width, P * kb:T],
                                            v_tok[vm][:, P * kb + lo:P * kb + lo + width],
                                            probs_t[m][:, T_AT[kb]:T_AT[kb] + w], start=(kb == 0), stop=(kb == QB - 1))
                last.then_inc(pv_done, 1)

            def fox_tile(g, slot, before_k=None):
                tile(g, g, slot, 0, before_k=before_k)

            def forget_gates():
                pe.wait_ge(const_in, 16 * N_CONST)
                pe.wait_ge(ws_lo_done, 1)
                for k in range(KT):
                    hi, lo = ws_hi[:, k * FOX_HEADS:(k + 1) * FOX_HEADS], ws_lo[:, k * FOX_HEADS:(k + 1) * FOX_HEADS]
                    dst = s_bank[0][0:FOX_HEADS, :]
                    nc.tensor.matmul(dst, hi, b_hi[0][:, k, :], start=(k == 0), stop=False)
                    nc.tensor.matmul(dst, hi, b_lo[0][:, k, :], start=False, stop=False)
                    last = nc.tensor.matmul(dst, lo, b_hi[0][:, k, :], start=False, stop=(k == KT - 1))
                last.then_inc(f_mm, 1)

            def fox_step(pp, m, project=True, attend=True, late=True, start=False):
                p = 2 * pp + m
                c = 7 * p - 6
                par = m
                o = 1 - m
                if project:
                    fox_tile(3 * p, m, ready_k(0) if start else None)
                if start:
                    sum_squares("fox", KT)
                    forget_gates()
                if late:
                    context(2 * p - 3, 1, m, c - 1, FOX_DH, FOX_DH, None)
                if attend:
                    pe.wait_ge(crow_in[o], 64 * pp + 64 * m)
                    pe.wait_ge(acc_free, 3 * p - 1)
                    logits(2 * p - 2, o, 0, "fox")
                if project:
                    fox_tile(3 * p + 1, 1 - m)
                if attend:
                    logits(2 * p - 1, o, 1, "fox")
                    turn_probs(2 * p - 2, 0, c, par)
                if project:
                    fox_tile(3 * p + 2, m)
                if attend:
                    context(2 * p - 2, 0, o, c + 3, 0, FOX_DH, None if isinstance(p, int) and p == 1 else p - 1)
                    turn_probs(2 * p - 1, 1, c + 3, 1 - par)
                if project:
                    turn_values(3 * p + 2, 0 if start else c + 6, par if not start else 0)

            fox_step(0, 0, attend=False, late=False, start=True)
            pe.wait_ge(norm_std, 1)
            fox_step(0, 1, late=False)
            with pe.Fori(1, FOX_PAIRS // 2) as pp:
                fox_step(pp, 0)
                fox_step(pp, 1)
            c, last = 7 * FOX_PAIRS - 6, FOX_HEADS - 1
            context(last - 2, 1, 0, c - 1, FOX_DH, FOX_DH, None)
            pe.wait_ge(crow_in[1], 32 * FOX_PAIRS)
            pe.wait_ge(acc_free, 3 * FOX_PAIRS - 1)
            logits(last - 1, 1, 0, "fox")
            logits(last, 1, 1, "fox")
            begin("fox_out", 0, 1, 0, FOX_PAIRS - 2)
            turn_probs(last - 1, 0, c, 0)
            begin("fox_out", 1, 1, 0, FOX_PAIRS - 2)
            context(last - 1, 0, 1, c + 3, 0, FOX_DH, FOX_PAIRS - 1)
            turn_probs(last, 1, c + 3, 1)
            for s in range(2):
                begin("fox_out", s, 1, FOX_PAIRS - 2, FOX_PAIRS - 1)
            context(last, 1, 1, c + 6, FOX_DH, FOX_DH, None)
            for s in range(2):
                begin("fox_out", s, 1, FOX_PAIRS - 1, FOX_PAIRS)
            segment("fox_out", 0, KT, 1, begun=True)

            def ffn(run, buf, hid, norm):
                for i, (what, c) in enumerate(FF_ORDER):
                    if what == "u":
                        segment(run, i * KT, KT, buf,
                                lead=(lambda: sum_squares(norm, PREP0[norm] + KT)) if i == 0 else None,
                                before_k=ready_k(PREP0[norm]) if i == 0 else None)
                    else:
                        first = HID0[run] + c * KT
                        segment(run, i * KT, KT, hid[c % 2],
                                before_k=lambda k, first=first: pe.wait_ge(hid_lo, first + k + 1))

            ffn("ff_a", 0, (1, 2), "ff_a")

            g0, t0 = PANEL0["kva_qa"], TILE0["kva_qa"]
            tile(g0, t0, 0, 0, before_k=ready_k(PREP0["mla"]))
            sum_squares("mla", PREP0["mla"] + KT)
            for j in range(1, 6):
                tile(g0 + j, t0 + j, j % 2, 0 if j < 3 else 1)
                if j == 3:
                    pe.wait_ge(acc_free, t0 + 3)
                    pe.wait_ge(rope_in, 32)
                    nc.tensor.matmul(s_bank[0][:], fold_t[:, 0:P], kr_raw, start=True, stop=True).then_inc(kr_mm, 1)
                if j == 4:
                    sum_squares("ckv", PREP0["ckv"] + KVKT, low_sum)
            sum_squares("cq", PREP0["cq"] + QKT)

            def mla_step(h, m, project=True, attend=True, late=True):
                g = 2 * h + PANEL0["mla"]
                t = 4 * h + TILE0["mla"]
                n = h + HEAD0["mla"]
                c = 4 * h + (T0_MLA - 6)
                o = 1 - m
                if project:
                    panel_ready(g)
                    for i, at in enumerate((0, NOPE)):
                        bank_free(t + i)
                        products(acc[i][:], 0, QKT, lambda k: b_hi[2][:, k, :], lambda k: b_lo[2][:, k, :],
                                 at, NOPE + 2 * ROPE).then_inc(mm_done, 1)
                if late:
                    turn_probs(n - 2, m, c if project or attend else c - 1, (T0_MLA if project or attend else T0_MLA - 1) % 2)
                if attend:
                    pe.wait_ge(acc_free, t - 1)
                    logits(n - 1, o, 0, "mla")
                if project:
                    panel_ready(g + 1)
                    for i, at in enumerate((0, NOPE)):
                        bank_free(t + 2 + i)
                        products(acc[i][:], 1, KVKT, lambda k: b_hi[2][:, QKT + k, :],
                                 lambda k: b_lo[2][:, QKT + k, :], at, NOPE + VDIM).then_inc(mm_done, 1)
                if late:
                    context(n - 2, m, m, (c if project or attend else c - 1) + 3, 0, VDIM, h + (CTX0["mla"] - 2))
                if project:
                    first = not attend
                    turn_values(t + 3, T0_MLA if first else c + 3, (T0_MLA if first else T0_MLA - 3) % 2)

            mla_step(0, 0, attend=False, late=False)
            pe.wait_ge(norm_std, NORM["cq"] + 1)
            pe.wait_ge(kr_done, 1)
            mla_step(1, 1, late=False)
            with pe.Fori(1, MLA_HEADS // 2) as hh:
                mla_step(2 * hh, 0)
                mla_step(2 * hh + 1, 1)
            n, c = HEAD0["mla"] + MLA_HEADS - 1, T0_MLA + 4 * MLA_HEADS
            turn_probs(n - 1, 0, c - 6, T0_MLA % 2)
            pe.wait_ge(acc_free, TILE0["mla_out"] - 1)
            logits(n, 1, 0, "mla")
            begin("mla_out", 0, 0, 0, MLA_HEADS - 2)
            context(n - 1, 0, 0, c - 3, 0, VDIM, CTX0["mla"] + MLA_HEADS - 2)
            begin("mla_out", 1, 0, 0, MLA_HEADS - 2)
            turn_probs(n, 1, c - 3, (T0_MLA - 1) % 2)
            for s in range(2):
                begin("mla_out", s, 0, MLA_HEADS - 2, MLA_HEADS - 1)
            context(n, 1, 1, c, 0, VDIM, CTX0["mla"] + MLA_HEADS - 1)
            for s in range(2):
                begin("mla_out", s, 0, MLA_HEADS - 1, MLA_HEADS)
            segment("mla_out", 0, KT, 0, begun=True)
            ffn("ff_b", 1, (0, 2), "ff_b")
            pe.wait_ge(both_sum, 1)
            sum_squares("x2", PREP0["final"] + KT, ssum_g)

            g0 = PANEL0["mix_in"]
            for half in range(2):
                panel_ready(g0 + half)
                for k in range(KT // 2):
                    f = half * (KT // 2) + k
                    pe.wait_ge(h_lo, f + 1)
                    whi, wlo = w_hi[half][:, k * P:(k + 1) * P], w_lo[half][:, k * P:(k + 1) * P]
                    nc.tensor.matmul(s_bank[2][:], whi, b_hi[0][:, f, :], start=(f == 0), stop=False)
                    nc.tensor.matmul(s_bank[2][:], whi, b_lo[0][:, f, :], start=False, stop=False)
                    last = nc.tensor.matmul(s_bank[2][:], wlo, b_hi[0][:, f, :], start=False, stop=(f == KT - 1))
                last.then_inc(mm_done, 1)
            sum_squares("final", PREP0["final"] + KT)

            def mix_tile(i, slot):
                panel_ready(i + g0)
                if not (isinstance(i, int) and i < 4):
                    pe.wait_ge(mix_free, i - 3)
                products(acc[slot][:], slot, KT, lambda k: b_hi[0][:, k, :], lambda k: b_lo[0][:, k, :], 0, P)\
                    .then_inc(mm_done, 1)

            for s in range(2):
                mix_tile(2 + s, s)
            with pe.Fori(2, (GLA + 8) // 2) as half:
                for s in range(2):
                    mix_tile(2 * half + s, s)
            pe.wait_ge(mix_free, 26)
            pe.wait_ge(const2_in, 16 * N_CONST2)

            pe.wait_ge(row_u_done, 1)
            for blk in range(QB):
                last = nc.tensor.transpose(s_bank[2][:, HEADS * blk:HEADS * (blk + 1)], row_u[:, P * blk:P * (blk + 1)],
                                           ident[0:HEADS, 0:HEADS])
            last.then_inc(u_turned, 1)
            for src, dst in zip(ml_v + gla_v, t_bank + s_bank[0:2]):
                for blk in range(QB):
                    c = slice(P * blk, P * (blk + 1))
                    last = nc.tensor.transpose(dst[:, c], src[:, c], ident[:])
                last.then_inc(v_turned, 1)

            pe.wait_ge(conv_done, 2)
            for i in range(2):
                last = nc.tensor.matmul(c_bank[:], ones_sq[:], conf_u[i], start=(i == 0), stop=(i == 1))
            last.then_inc(ln_mean, 1)
            pe.wait_ge(ln_sq, 2)
            for i in range(2):
                last = nc.tensor.matmul(c_bank[:], ones_sq[:], ml_v[i], start=(i == 0), stop=(i == 1))
            last.then_inc(ln_var, 1)

            pe.wait_ge(row_max, 1)
            pe.wait_ge(u_read, 1)
            pe.wait_ge(v_read, 4)
            pe.wait_ge(ln_std, 1)

            def log_weights(h):
                if h:
                    pe.wait_ge(w_exp, h)
                nc.tensor.matmul(s_bank[0][:], sel[:, P * h:P * (h + 1)], row_z, start=True, stop=True)
                nc.tensor.matmul(s_bank[1][:], sel[:, P * h:P * (h + 1)], row_z, start=True, stop=False,
                                 skip_group_check=True)
                for blk in range(QB):
                    last = nc.tensor.matmul(s_bank[1][:, P * blk:P * (blk + 1)], ident[:], mask_k[:], start=False,
                                            stop=(blk == QB - 1), skip_group_check=True)
                last.then_inc(d_ready, 1)

            def key_queries(h):
                c, rows = h // 2, slice(DH * (h % 2), DH * (h % 2 + 1))
                if h:
                    pe.wait_ge(a_ready, h)
                for blk, (dst, at) in enumerate(((t_bank[0], 0), (t_bank[1], 0), (s_bank[2], 0), (t_bank[1], T - P))):
                    last = nc.tensor.matmul(dst[:, at:at + T - P * blk], ml_k[c][rows, P * blk:P * (blk + 1)],
                                            ml_q[c][rows, P * blk:T], start=(blk < 3), stop=True, skip_group_check=True)
                last.then_inc(qk_ready, 1)

            def head_sums(h):
                c, m, rows = h // 2, h % 2, slice(DH * (h % 2), DH * (h % 2 + 1))
                pe.wait_ge(a_ready, h + 1)
                if h == 2:
                    pe.wait_ge(head_h, 1)
                for dst, by in ((c_bank, None), (acc[0], ones_sq)):
                    for blk in range(QB):
                        lhs = ones_sq[:, 0:DH] if by is not None else ml_vt[c][:, P * blk + DH * m:P * blk + DH * (m + 1)]
                        last = nc.tensor.matmul(dst[rows, P * blk:T], lhs, ml_w[m][:, T_AT[blk]:T_AT[blk] + T - P * blk],
                                                start=(blk == 0), stop=(blk == QB - 1), skip_group_check=True)
                if m:
                    pe.wait_ge(row_em, 1)
                    if c:
                        pe.wait_ge(head_std, c)
                    at = 2 * c * P + DH
                    last = nc.tensor.matmul(acc[1][:], sel[:, at:at + P], row_b, start=True, stop=True)
                last.then_inc(head_ctx, 1)

            def head_squares(i, src):
                pe.wait_ge(head_sq, i + 1)
                nc.tensor.matmul(acc[1][:], halves[:], src, start=True, stop=True).then_inc(head_sum, 1)

            log_weights(0)
            key_queries(0)
            log_weights(1)
            head_sums(0)
            key_queries(1)
            log_weights(2)
            head_sums(1)
            key_queries(2)
            log_weights(3)
            head_squares(0, ml_s)
            head_sums(2)
            key_queries(3)
            head_sums(3)
            head_squares(1, ml_s)

            for c in range(2):
                nc.tensor.matmul(t_bank[c][:], gla_a2[:, P * c:P * (c + 1)], gla_a, start=True, stop=True)\
                  .then_inc(gz_ready, 1)

            def chunk_weights(c):
                pe.wait_ge(g_scaled, c + 1)
                if c == 0:
                    pe.wait_ge(gz_in, 2)
                else:
                    pe.wait_ge(gs_read, c)
                for m in range(2):
                    rows = slice(DH * m, DH * (m + 1))
                    for blk in range(QB):
                        w = slice(P * blk, P * (blk + 1))
                        last = nc.tensor.matmul(t_bank[m][:, w], gla_e[c][1][rows, w], gla_e[c][0][rows, w],
                                                start=(blk == 0), stop=True, skip_group_check=True)
                last.then_inc(gs_ready, 1)

            def turn_keys(c):
                if c:
                    pe.wait_ge(gu_read, c)
                for blk in range(QB):
                    w = slice(P * blk, P * (blk + 1))
                    last = nc.tensor.transpose(s_bank[2][:, w], gla_e[c][3][:, w], ident[:])
                last.then_inc(kd_turned, 1)

            u_bank = [acc[0], s_bank[0], s_bank[1], s_bank[2]]

            def chunk_states(c):
                pe.wait_ge(kd_read, c + 1)
                for i in range(P // GLA_CHUNK):
                    rows = slice(GLA_CHUNK * i, GLA_CHUNK * (i + 1))
                    for blk in range(QB):
                        w = slice(P * blk, P * (blk + 1))
                        last = nc.tensor.matmul(u_bank[i][:, w], gla_b[c][rows, w], gla_vt[c][rows, w],
                                                start=(blk == 0), stop=True, skip_group_check=True,
                                                tile_position=(GLA_CHUNK * i, 0))
                    last.then_inc(gu_ready, 1)

            def chunk_outputs(c):
                pe.wait_ge(gs_read, c + 1)
                pe.wait_ge(g_state, c + 1)
                if c:
                    pe.wait_ge(head_h, 2 + c)
                for m in range(2):
                    rows = slice(DH * m, DH * (m + 1))
                    for blk in range(QB):
                        w = slice(P * blk, P * (blk + 1))
                        nc.tensor.matmul(c_bank[rows, w], gla_vt[c][:, P * blk + DH * m:P * blk + DH * (m + 1)],
                                         gla_w[m][:, w], start=(blk == 0), stop=False, skip_group_check=True)
                    state = gla_s[c][rows, :].rearrange("p (e n) -> p n e", n=CHUNKS)
                    for i in range(1, CHUNKS):
                        w = slice(GLA_CHUNK * i, GLA_CHUNK * (i + 1))
                        last = nc.tensor.matmul(c_bank[rows, w], state[:, i - 1, :], gla_e[c][2][rows, w], start=False,
                                                stop=(i == CHUNKS - 1), skip_group_check=True)
                last.then_inc(g_out, 1)

            chunk_weights(0)
            turn_keys(0)
            chunk_states(0)
            chunk_weights(1)
            turn_keys(1)
            chunk_outputs(0)
            head_squares(2, gla_e[0][0])
            chunk_states(1)
            chunk_outputs(1)
            head_squares(3, gla_e[1][0])

            g0, t0 = PANEL0["merge"], TILE0["merge"]
            pe.wait_ge(ln_lo, 2)
            pe.wait_ge(sc_lo, 2)

            def merge_tile(j, m):
                for b in range(BRANCHES):
                    slot = (m + b) % 2
                    panel_ready(5 * j + (g0 + b))
                    if not (isinstance(j, int) and j == 0):
                        pe.wait_ge(gate_done, 4 * j + (b - 3))
                    elif b == 3:
                        pe.wait_ge(head_h, 4)
                    products(gate_bank[b][:], slot, KT, lambda k: b_hi[0][:, k, :], lambda k: b_lo[0][:, k, :], 0, P)\
                        .then_inc(mm_done, 1)
                panel_ready(5 * j + (g0 + 4))
                for b in range(BRANCHES):
                    if isinstance(j, int) and j == 0:
                        if b == 0:
                            pe.wait_ge(head_lo, 4)
                    if not (isinstance(j, int) and j == 0):
                        pe.wait_ge(branch_read, 4 * j + (b - 3))
                    products(branch_bank[b][:], m, 2, lambda k: b_hi[1][:, 2 * b + k, :], lambda k: b_lo[1][:, 2 * b + k, :],
                             2 * b * P, P).then_inc(mm_done, 1)

            merge_tile(0, 0)
            merge_tile(1, 1)
            with pe.Fori(1, KT // 2) as jj:
                merge_tile(2 * jj, 0)
                merge_tile(2 * jj + 1, 1)

            pe.wait_ge(branch_read, BRANCHES * (KT - 1) + 1)
            segment("w_o", 0, KT, 2, before_k=lambda k: pe.wait_ge(merge_lo, k + 1))
            sum_squares("mix_y", PREP0["mix_y"] + KT)
            pe.wait_ge(norm_std, NORM["cm"])
            for k in range(KT):
                pe.wait_ge(cm_sq, k + 1)
                last = nc.tensor.matmul(c_bank[:], ones_sq[:], sq[k % 2], start=(k == 0), stop=(k == KT - 1))
                last.then_inc(cm_added if k < KT - 1 else norm_sum, 1)

            for what, c, first in FFN2_STEPS:
                n, at = FFN2_CHUNKS[c], HID0["ffn2"] + HID_AT[c]
                if what == "u":
                    segment("ffn2", first, 2 * n, 0,
                            before_k=(lambda k: pe.wait_ge(h_lo, KT + k + 1)) if c == 0 else None)
                else:
                    segment("ffn2", first, KT, 1 + c % 2, depth=n,
                            before_k=lambda k, at=at: pe.wait_ge(hid_lo, at + k + 1))
            sum_squares("ffn_y", PREP0["ffn_y"] + KT)

        @block.scalar
        def _(act):
            def split(half, slot, width, used):
                act.wait_ge(w_in[slot], 16 * half + 16)
                if used is not None:
                    act.wait_ge(mm_done, used)
                nc.scalar.activation(w_hi[slot][:, 0:width], w_raw[slot][:, 0:width], ACT.Copy).then_inc(w_hi_done, 1)

            def segment(run, first, n, mid, before0, before1, before2=None, fresh=0, width=PANEL, last=1):
                half0, t0 = (PANEL0[run] + first) // 2, TILE0[run] + first
                if fresh < 1:
                    split(half0, 0, width, t0 - last)
                before0()
                if fresh < 2:
                    split(half0, 1, width, t0)
                before1()
                start = 1
                if before2 is not None:
                    split(half0 + 1, 0, width, t0 + 1)
                    before2()
                    mid(0, 0)
                    mid(1, 1)
                    split(half0 + 1, 1, width, t0 + 2)
                    mid(2, 0)
                    start = 2
                else:
                    mid(0, 0)
                with act.Fori(start, n // 2) as half:
                    split(half + half0, 0, width, 2 * half + (t0 - 1))
                    mid(2 * half - 1, 1)
                    split(half + half0, 1, width, 2 * half + t0)
                    mid(2 * half, 0)

            def nothing(*_):
                pass

            def prepare(np, src, tile_free, k, s, gain, dst):
                if tile_free is not None:
                    act.wait_ge(acc_free, tile_free)
                if not (isinstance(np, int) and np < 2):
                    act.wait_ge(prep_lo, np - 1)
                for buf, at, g in zip(dst[0], dst[1], gain):
                    g_col = vec[:, bass.ds(k + VEC[g], 1)]
                    act.activation(b_hi[buf][:, bass.ds(k + at, 1), :].rearrange("p a t -> p (a t)"), src, ACT.Copy,
                                   scale=g_col)
                act.activation(sq[s], src, ACT.Square).then_inc(prep_hi, 1)

            def x_tile(k):
                return x[:, bass.ds(k, 1), :].rearrange("p a t -> p (a t)")

            def prepare_x(norm, t0, gain, dst):
                return lambda j, s: prepare(j + PREP0[norm], x_tile(j), j + (t0 + 1), j, s, gain, dst)

            def root(norm, width, bias=eps):
                if NORM[norm]:
                    act.wait_ge(norm_rstd, NORM[norm])
                act.wait_ge(norm_sum, NORM[norm] + 1)
                act.activation(std, c_bank[:], ACT.Sqrt, bias=bias, scale=1.0 / width).then_inc(norm_std, 1)

            def ready_root():
                act.activation(small[:, 63:64], eps, ACT.Sqrt)

            load_x(act, 0)
            load_x(act, 2)
            load_x(act, 3)
            act.wait_ge(vec_in, 16)
            for k in range(KT):
                if k % (KT // X_PARTS) == 0:
                    act.wait_ge(x_in[k // (KT // X_PARTS)], 16)
                prepare(k, x_tile(k), None, k, k % 2, ("mix_g0",), ((0,), (0,)))
                if k == 1:
                    split(0, 0, PANEL, None)
            act.wait_ge(const_in, 16 * N_CONST)
            act.activation(ws_hi[:], ws_raw[:], ACT.Copy).then_inc(ws_hi_done, 1)
            root("fox", D)

            def exponentials(n, m):
                for u, rows in enumerate(((3,), (2,), (1, 0))):
                    act.wait_ge(row_min, 3 * n + (u + 1))
                    for qb in rows:
                        w = P * (qb + 1)
                        at = 0 if qb else 2 * P
                        c = 4 * m + qb
                        last = act.activation(probs[m][:, P_AT[qb]:P_AT[qb] + w], s_bank[u][:, at:at + w], ACT.Exp,
                                              bias=rmin[:, c:c + 1], scale=-1.0, accum_out=rsum[:, c:c + 1])
                    last.then_inc(p_exp, 1)

            def read_probs(n, m, c, par):
                if not (isinstance(n, int) and n < 2):
                    act.wait_ge(pv_done, n - 1)
                for u, (at, w) in enumerate(((0, T), (T, T), (2 * T, T // 2))):
                    act.wait_ge(t_ready, c + (u + 1))
                    act.activation(probs_t[m][:, at:at + w], t_bank[(par + u) % 2][:, 0:w], ACT.Copy).then_inc(t_free, 1)

            def read_values(m, c, par):
                act.wait_ge(t_ready, c + 1)
                act.activation(v_tok[m], t_bank[par][:], ACT.Copy).then_inc(t_free, 1)

            def read_context(heads, buf, k):
                act.wait_ge(pv_done, heads)
                act.activation(b_hi[buf][:, bass.ds(k, 1), :].rearrange("p a t -> p (a t)"), c_bank[:], ACT.Copy)\
                   .then_inc(ctx_hi, 1)

            def fox_step(pp, m, project=True, attend=True, late=True):
                p = 2 * pp + m
                c = 7 * p - 6

                def split_next(i):
                    split(3 * pp + (3 * m + i) // 2, (m + i) % 2, PANEL,
                          None if not attend and i < 2 else 3 * p + (i - 1))

                if project:
                    split_next(1)
                if not attend:
                    act.wait_ge(f_abs, 1)
                    act.activation(fz[0], fz[3], ACT.Exp, scale=-1.0).then_inc(f_ln, 1)
                    act.wait_ge(f_ln, 1)
                    act.activation(fz[3], fz[0], ACT.Ln, bias=col("one")[0:FOX_HEADS, :]).then_inc(f_ln, 1)
                if late:
                    read_context(2 * p - 2, 1, p - 2)
                if attend:
                    exponentials(2 * p - 2, 0)
                if project:
                    split_next(2)
                if attend:
                    read_probs(2 * p - 2, 0, c, m)
                    exponentials(2 * p - 1, 1)
                if project:
                    split_next(3)
                if attend:
                    read_probs(2 * p - 1, 1, c + 3, 1 - m)
                if project:
                    read_values(m, c + 6 if attend else 0, m)

            fox_step(0, 0, attend=False, late=False)
            fox_step(0, 1, late=False)
            with act.Fori(1, FOX_PAIRS // 2) as pp:
                fox_step(pp, 0)
                fox_step(pp, 1)
            split(PANEL0["fox_out"] // 2, 1, PANEL, TILE0["fox_out"])
            fox_step(FOX_PAIRS // 2, 0, project=False)

            out_a = prepare_x("ff_a", TILE0["fox_out"], ("ff_g0",), ((0,), (0,)))
            segment("fox_out", 0, KT, out_a, nothing, lambda: read_context(2 * FOX_PAIRS, 1, FOX_PAIRS - 1), ready_root,
                    fresh=2)

            def ffn(run, hid, before, norm, last_mid):
                for i, (what, c) in enumerate(FF_ORDER):
                    t0 = TILE0[run] + i * KT

                    def square(j, s, t0=t0, c=c):
                        n = j + (HID0[run] + c * KT)
                        act.wait_ge(acc_free, j + (t0 + 1))
                        if not (isinstance(n, int) and n < 2):
                            act.wait_ge(hid_lo, n - 1)
                        act.activation(ff_s[s], ff_t[s], ACT.Square).then_inc(ff_sq, 1)
                        act.wait_ge(ff_sq, n + 1)
                        act.activation(b_hi[hid[c % 2]][:, bass.ds(j, 1), :].rearrange("p a t -> p (a t)"), ff_s[s],
                                       ACT.Copy).then_inc(sq_hi, 1)

                    mid = square if what == "u" else last_mid if c == FF_CHUNKS - 1 else nothing
                    if i == 0:
                        segment(run, i * KT, KT, mid, lambda: before(KT - 1, 1), nothing, lambda: start(norm))
                    else:
                        segment(run, i * KT, KT, mid, lambda: before(KT - 1, 1), nothing)
                    before = mid
                return before

            def start(norm):
                root(norm, D)
                if norm == "ff_a":
                    act.wait_ge(ada_cin, 16)
                    act.activation(ada_c, ada_c, ACT.Silu).then_inc(ada_silu, 1)
                    ready_root()

            last_a = prepare_x("mla", TILE0["ff_a"] + 7 * KT, ("kv_g", "mix_g1"), ((0, 1), (0, 0)))
            before = ffn("ff_a", (1, 2), out_a, "ff_a", last_a)

            half0, t0 = PANEL0["kva_qa"] // 2, TILE0["kva_qa"]
            split(half0, 0, PANEL, t0 - 1)
            before(KT - 1, 1)
            split(half0, 1, PANEL, t0)
            split(half0 + 1, 0, PANEL, t0 + 1)
            root("mla", D)

            def prepare_low(norm, n, at, tile0):
                for j in range(n):
                    prepare(PREP0[norm] + j, low[at + j], t0 + tile0 + j + 1, j, (PREP0[norm] + j) % 2,
                            ("kva_g" if norm == "ckv" else "qa_g",), ((2,), (at,)))

            for i in range(3, 6):
                split(half0 + i // 2, i % 2, PANEL, t0 + i - 1)
                if i == 3:
                    prepare_low("ckv", KVKT, QKT, 0)
            root("ckv", KV_RANK)
            prepare_low("cq", QKT, 0, 3)
            split(PANEL0["mla"] // 2, 0, Q_COLS, t0 + 5)
            split(PANEL0["mla"] // 2, 1, KV_COLS, t0 + 6)
            root("cq", Q_RANK)

            def mla_step(hh, m, project=True, attend=True, late=True, ahead=True):
                h = 2 * hh + m
                n = h + HEAD0["mla"]
                c = 4 * h + (T0_MLA - 6)
                o = 1 - m
                if late:
                    read_probs(n - 2, m, c if project or attend else c - 1,
                               (T0_MLA if project or attend else T0_MLA - 1) % 2)
                if attend:
                    exponentials(n - 1, o)
                if ahead:
                    split(h + (PANEL0["mla"] // 2 + 1), 0, Q_COLS, 4 * h + (TILE0["mla"] + 2))
                    split(h + (PANEL0["mla"] // 2 + 1), 1, KV_COLS, 4 * h + (TILE0["mla"] + 4))
                if late:
                    read_context(n - 1, 0, h - 2)
                if project:
                    read_values(m, c + 3 if attend else T0_MLA, (T0_MLA - 3) % 2 if attend else T0_MLA % 2)

            mla_step(0, 0, attend=False, late=False)
            mla_step(0, 1, late=False)
            with act.Fori(1, MLA_HEADS // 2 - 1) as hh:
                mla_step(hh, 0)
                mla_step(hh, 1)
            mla_step(MLA_HEADS // 2 - 1, 0)
            mla_step(MLA_HEADS // 2 - 1, 1, ahead=False)
            split(PANEL0["mla_out"] // 2, 0, PANEL, TILE0["mla_out"] - 2)
            split(PANEL0["mla_out"] // 2, 1, PANEL, TILE0["mla_out"])
            mla_step(MLA_HEADS // 2, 0, project=False, ahead=False)
            read_probs(HEAD0["mla"] + MLA_HEADS - 1, 1, T0_MLA + 4 * MLA_HEADS - 3, (T0_MLA - 1) % 2)

            out_b = prepare_x("ff_b", TILE0["mla_out"], ("ff_g1",), ((1,), (0,)))
            segment("mla_out", 0, KT, out_b, nothing,
                    lambda: read_context(HEAD0["mla"] + MLA_HEADS, 0, MLA_HEADS - 1), ready_root, fresh=2)

            def squares_of(norm, src, ready, count):
                def mid(j, s):
                    act.wait_ge(prep_lo, j + (PREP0[norm] - 1))
                    act.wait_ge(ready, j + (count + 1))
                    act.activation(sq[s], src(j), ACT.Square).then_inc(prep_hi, 1)
                return mid

            def y_tile(j):
                return arena[:, bass.ds(j + y_at, 1), :].rearrange("p a t -> p (a t)")

            def last_b(j, s):
                act.wait_ge(prep_lo, j + (PREP0["final"] - 1))
                act.wait_ge(acc_free, j + (TILE0["ff_b"] + 7 * KT + 1))
                act.activation(sq_g[s], x_tile(j), ACT.Square, scale=vec[:, bass.ds(j + VEC["final_g"], 1)])
                act.activation(sq[s], x_tile(j), ACT.Square).then_inc(prep_hi, 1)

            before = ffn("ff_b", (0, 2), out_b, "ff_b", last_b)
            before(KT - 1, 1)
            half0, t0 = PANEL0["mix_in"] // 2, TILE0["mix_in"]
            for s in range(2):
                split(half0, s, PANEL // 2, t0 - 1 + s)
            root("x2", D, col("eps2"))

            act.wait_ge(mod_ready, 1)

            def modulate(n0, shift, scale):
                def work(k, s):
                    act.wait_ge(h_tmp, k + (n0 + 1))
                    if n0 or not isinstance(k, int):
                        act.wait_ge(h_lo, k + (n0 - 1))
                    by = dict(bias=mod[:, bass.ds(k + shift * KT, 1)], scale=mod[:, bass.ds(k + scale * KT, 1)])
                    act.activation(b_hi[0][:, bass.ds(k, 1), :].rearrange("p a t -> p (a t)"), mod_t[s], ACT.Identity, **by)
                    act.activation(mod_y[s], mod_t[s], ACT.Identity, **by).then_inc(h_hi, 1)

                for s in range(2):
                    work(s, s)
                with act.Fori(1, KT // 2) as half:
                    for s in range(2):
                        work(2 * half + s, s)

            modulate(0, 0, 1)
            root("final", D)

            def read(i, dst, func, scale=1.0):
                act.wait_ge(mm_done, t0 + i + 1)
                act.activation(dst, acc[i % 2][:], func, scale=scale).then_inc(mix_free, 1)

            def narrow():
                act.wait_ge(mm_done, t0 + 2)
                f, i = slice(F_ROW, F_ROW + HEADS), slice(I_ROW, I_ROW + HEADS)
                act.activation(row_z, s_bank[2][f, :], ACT.Identity, bias=col("ml_bf")[f, :])
                act.activation(row_u, s_bank[2][i, :], ACT.Identity, bias=col("ml_bi")[i, :])
                act.activation(gla_a, s_bank[2][A_ROW:A_ROW + GLA_RANK, :], ACT.Copy).then_inc(rows_in, 1)

            def log_sigmoid(z, s, one, ready, count, done):
                act.wait_ge(ready, count + 1)
                act.activation(s, s, ACT.Exp, scale=-1.0).then_inc(done, 1)
                act.wait_ge(done, 2 * count + 1)
                act.activation(s, s, ACT.Ln, bias=one).then_inc(done, 1)

            one = col("one")
            plan = ([(dst, ACT.Copy, 1.0) for dst in conf_a] + [(dst, ACT.Sigmoid, 1.0) for dst in conf_g]
                    + [(dst, ACT.Copy, 1.0) for dst in sc_b + sc_c + sc_x]
                    + [(dst, ACT.Copy, DH ** -0.5) for dst in ml_q] + [(dst, ACT.Copy, 1.0) for dst in ml_k + ml_v]
                    + [(dst, ACT.Sigmoid, 1.0) for dst in ml_o]
                    + [(dst, ACT.Copy, DH ** -0.5) for dst in gla_q] + [(dst, ACT.Copy, 1.0) for dst in gla_k + gla_v]
                    + [(dst, ACT.Silu, 1.0) for dst in gla_r])
            for i in range(2, GLA + 8 + 1):
                if i < GLA + 8:
                    split(half0 + i // 2, i % 2, PANEL, t0 + i - 1)
                if i == 2:
                    narrow()
                    continue
                if i == 4:
                    log_sigmoid(row_z, row_b, one[0:HEADS, :], row_abs, 0, row_ln)
                if i == 6:
                    act.wait_ge(row_floor, 1)
                    act.activation(row_b, row_b, ACT.Exp).then_inc(row_em, 1)
                if i - 1 == GLA:
                    act.wait_ge(pad_ready, 4)
                if i - 1 == GLA + 4:
                    act.wait_ge(conv_done, 4)
                if i - 1 == GLA + 6:
                    act.wait_ge(sc_out, 2)
                read(i - 1, *plan[i - 3])
                if i == 23:
                    for j in range(2):
                        act.wait_ge(sc_out, j + 1)
                        act.activation(b_hi[1][:, 6 + j, :], sc_u[j], ACT.Copy).then_inc(sc_hi, 1)
            half0, t0 = PANEL0["merge"] // 2, TILE0["merge"]
            split(half0, 0, PANEL, t0 - 1)
            split(half0, 1, PANEL, t0)

            act.wait_ge(sc_lo, 2)
            for i, (dst, src) in enumerate(zip(ml_vt + gla_vt, t_bank + s_bank[0:2])):
                act.wait_ge(v_turned, i + 1)
                act.activation(dst, src[:], ACT.Copy).then_inc(v_read, 1)

            for i in range(2):
                act.wait_ge(ln_dev, i + 1)
                act.activation(ml_v[i], conf_u[i], ACT.Square).then_inc(ln_sq, 1)
            act.wait_ge(ln_var, 1)
            act.activation(ml_s_std, c_bank[:], ACT.Sqrt, bias=eps, scale=1.0 / MIX).then_inc(ln_std, 1)
            for i in range(2):
                act.wait_ge(ln_out, i + 1)
                act.activation(conf_u[i], conf_u[i], ACT.Silu, bias=col("ln_b", i), scale=col("ln_g", i)).then_inc(ln_act, 1)
                act.wait_ge(ln_act, i + 1)
                act.activation(b_hi[1][:, 4 + i, :], conf_u[i], ACT.Copy).then_inc(ln_hi, 1)

            act.wait_ge(u_read, 1)

            def weights(h):
                m = h % 2
                act.wait_ge(d_ready, h + 1)
                if h >= 2:
                    act.wait_ge(head_ctx, h - 1)
                for blk in range(QB):
                    bias, at = u_col[:, HEADS * blk + h:HEADS * blk + h + 1], T_AT[blk]
                    last = act.activation(ml_w[m][:, at:at + P], s_bank[1][:, P * blk:P * (blk + 1)], ACT.Exp, bias=bias)
                    if blk < QB - 1:
                        act.activation(ml_w[m][:, at + P:at + T - P * blk], s_bank[0][:, P * (blk + 1):T], ACT.Exp, bias=bias)
                last.then_inc(w_exp, 1)

            def floor(c):
                act.wait_ge(head_ctx, 2 * c + 2)
                if c:
                    act.wait_ge(head_h, c)
                act.activation(ml_den, acc[0][:], ACT.Abs).then_inc(den_abs, 1)

            def squares_root(i, src, dst, ready):
                act.wait_ge(ready[0], ready[1])
                act.activation(dst, src, ACT.Square).then_inc(head_sq, 1)
                act.wait_ge(head_sum, i + 1)
                act.activation(dst, acc[1][:], ACT.Sqrt, bias=eps, scale=1.0 / DH).then_inc(head_std, 1)

            def high(i, src):
                act.wait_ge(head_out, i + 1)
                act.activation(b_hi[1][:, i, :], src, ACT.Copy).then_inc(head_hi, 1)

            weights(0)
            weights(1)
            floor(0)
            weights(2)
            squares_root(0, ml_h, ml_s, (head_h, 1))
            weights(3)
            high(0, ml_h)
            floor(1)
            squares_root(1, ml_h, ml_s, (head_h, 2))
            high(1, ml_h)

            act.wait_ge(head_lo, 2)
            for c in range(2):
                act.wait_ge(gz_ready, c + 1)
                act.activation(gla_z[c], t_bank[c][:], ACT.Identity, bias=col("gla_b", c)).then_inc(gz_in, 1)
            for c in range(2):
                log_sigmoid(gla_z[c], gla_t[c], one, gz_abs, c, gz_ln)
            for c in range(2):
                act.wait_ge(gz_sum, c + 1)
                s = 1.0 / GLA_TAU
                b3 = gla_b[c].rearrange("p (n t) -> p n t", t=GLA_CHUNK)
                act.activation(gla_e[c][0], gla_z[c], ACT.Exp, scale=s)
                act.activation(gla_e[c][1], gla_z[c], ACT.Exp, scale=-s)
                act.activation(gla_e[c][2], gla_b[c], ACT.Exp, scale=s)
                act.activation(gla_e[c][3], gla_t[c], ACT.Exp, scale=s)
                act.activation(gla_decay[c], b3[:, :, GLA_CHUNK - 1:GLA_CHUNK].rearrange("p n t -> p (n t)"), ACT.Exp, scale=s)\
                   .then_inc(g_exp, 1)

            def keys_read(c):
                act.wait_ge(kd_turned, c + 1)
                act.activation(gla_b[c], s_bank[2][:], ACT.Copy).then_inc(kd_read, 1)

            def states_read(c):
                n = P // GLA_CHUNK
                for i, u_bank in enumerate((acc[0], s_bank[0], s_bank[1], s_bank[2])):
                    act.wait_ge(gu_ready, n * c + i + 1)
                    for m in range(2):
                        rows = slice(DH * m, DH * (m + 1))
                        to = gla_u[c][rows, :].rearrange("p (e b n) -> p n b e", b=QB, n=n)
                        src = u_bank[rows, :].rearrange("p (b e) -> p b e", b=QB)[:, :, DH * m:DH * (m + 1)]
                        last = act.activation(to[:, i, :, :], src, ACT.Copy)
                last.then_inc(gu_read, 1)

            keys_read(0)
            states_read(0)
            keys_read(1)
            squares_root(2, c_bank[:], gla_e[0][0], (g_out, 1))
            states_read(1)
            high(2, gla_e[0][1])
            squares_root(3, c_bank[:], gla_e[1][0], (g_out, 2))
            high(3, gla_e[1][1])

            def gate_of(j, m, b):
                act.wait_ge(mm_done, 8 * j + (t0 + b + 1))
                if not (isinstance(j, int) and j < 2):
                    act.wait_ge(branch_read, 4 * j + (b - 7))
                act.activation(gate[m][b], gate_bank[b][:], ACT.Sigmoid,
                               bias=vec[:, bass.ds(j + (VEC["gate_b"] + b * KT), 1)]).then_inc(gate_done, 1)

            def merged_high(j, m):
                act.wait_ge(merge_out, j + 1)
                act.activation(b_hi[2][:, bass.ds(j, 1), :].rearrange("p a t -> p (a t)"), merged[m], ACT.Copy)\
                   .then_inc(merge_hi, 1)

            def merge_split(j, m, p):
                half = (5 * j + m + p) // 2 if isinstance(j, int) else None
                used = 8 * j + (t0 + (p - 1 if p >= 2 else 0 if p == 1 else -4))
                return used

            def merge_tile(j, jj, m):
                for p in range(5):
                    i = 5 * m + p
                    first = isinstance(j, int) and j == 0
                    if not (first and p < 2):
                        split(5 * jj + (half0 + i // 2), i % 2, PANEL, merge_split(j, m, p))
                    if p >= 1:
                        gate_of(j, m, p - 1)
                    if p == 1 and not first:
                        merged_high(j - 1, 1 - m)

            merge_tile(0, 0, 0)
            merge_tile(1, 0, 1)
            with act.Fori(1, KT // 2) as jj:
                merge_tile(2 * jj, jj, 0)
                merge_tile(2 * jj + 1, jj, 1)

            square_y = squares_of("mix_y", y_tile, acc_free, FREE0["w_o"])
            segment("w_o", 0, KT, square_y, nothing, lambda: merged_high(KT - 1, 1), last=BRANCHES)
            square_y(KT - 1, 1)
            half0, t0 = PANEL0["ffn2"] // 2, TILE0["ffn2"]
            for s in range(2):
                split(half0, s, PANEL, t0 - 1 + s)
            root("mix_y", D)
            for k in range(KT):
                if k < 2:
                    act.wait_ge(norm_sum, NORM["mix_y"] + 1)
                else:
                    act.wait_ge(cm_added, k - 1)
                act.wait_ge(x_done, KT + k + 1)
                act.activation(sq[k % 2], x[:, k, :], ACT.Square).then_inc(cm_sq, 1)
            root("cm", D)
            modulate(KT, 3, 4)

            lead0 = lead1 = nothing
            fresh = 2
            for what, c, first in FFN2_STEPS:
                n, f0 = FFN2_CHUNKS[c], FREE0["ffn2"] + first
                hid_buf, hid0 = b_hi[1 + c % 2], HID0["ffn2"] + HID_AT[c]
                half0, t0 = (PANEL0["ffn2"] + first) // 2, TILE0["ffn2"] + first
                if what == "u":
                    def tap(j, is_v, t0=t0, hid_j=hid0 - HID0["ffn2"], last=2 * HID_T):
                        act.wait_ge(mm_done, 2 * j + (t0 + is_v + 1))
                        w_at = VEC["ffn_w"] + 2 * last + is_v * HID_T + hid_j
                        if not (isinstance(j, int) and j == 0 and hid_j == 0):
                            act.wait_ge(hid_lo if is_v else hid_out, j + (hid_j + (HID0["ffn2"] if is_v else 0)))
                        act.activation(hid_v if is_v else hid_a, acc[is_v][:], ACT.Copy,
                                       scale=vec[:, bass.ds(j + w_at, 1)]).then_inc(tap_last, 1)

                    def gate_hidden(j, f0=f0, hid_j=HID_AT[c]):
                        act.wait_ge(acc_free, 2 * j + (f0 + 1))
                        act.activation(hid_a, hid_a, ACT.Silu).then_inc(hid_silu, 1)

                    def hidden_high(j, hid_j=HID_AT[c], buf=hid_buf):
                        act.wait_ge(hid_out, j + (hid_j + 1))
                        act.activation(buf[:, bass.ds(j, 1), :].rearrange("p a t -> p (a t)"), hid_v, ACT.Copy)\
                           .then_inc(hid_hi, 1)

                    if not fresh:
                        split(half0, 0, PANEL, t0 - 1)
                    lead0()
                    if not fresh:
                        split(half0, 1, PANEL, t0)
                    lead1()
                    tap(0, 0)
                    with act.Fori(1, n) as j:
                        split(j + half0, 0, PANEL, 2 * j + (t0 - 1))
                        tap(j - 1, 1)
                        gate_hidden(j - 1)
                        split(j + half0, 1, PANEL, 2 * j + t0)
                        hidden_high(j - 1)
                        tap(j, 0)

                    def lead0(n=n, tap=tap, gate_hidden=gate_hidden):
                        tap(n - 1, 1)
                        gate_hidden(n - 1)

                    def lead1(n=n, hidden_high=hidden_high):
                        hidden_high(n - 1)
                    fresh = 0
                else:
                    mid = squares_of("ffn_y", y_tile, acc_free, f0) if c == len(FFN2_CHUNKS) - 1 else nothing
                    segment("ffn2", first, KT, mid, lead0, lead1, width=n * P)

                    def lead0(mid=mid):
                        mid(KT - 1, 1)
                    lead1 = nothing
            lead0()
            root("ffn_y", D)

        @block.vector
        def _(dve):
            steps = Steps(dve_step)

            def split(half, slot, width=PANEL):
                dve.wait_ge(w_hi_done, 2 * half + (slot + 1))
                dve.tensor_tensor(w_lo[slot][:, 0:width], w_raw[slot][:, 0:width], w_hi[slot][:, 0:width].bitcast(F32),
                                  ALU.subtract).then_inc(w_lo_done, 1)

            def segment(run, first, n, evac, post, before0, before1, before2=None, fresh=0, beside=None, width=PANEL):
                half0 = (PANEL0[run] + first) // 2

                def panel(half, s):
                    if not (isinstance(half, int) and half == 0 and s < fresh):
                        split(half + half0, s, width)
                    if beside is not None:
                        beside(2 * half + (first + s), s)

                panel(0, 0)
                before0()
                panel(0, 1)
                before1()
                start = 1
                if before2 is not None:
                    panel(1, 0)
                    before2()
                    evac(0, 0)
                    evac(1, 1)
                    post(0, 0)
                    panel(1, 1)
                    evac(2, 0)
                    post(1, 1)
                    start = 2
                else:
                    evac(0, 0)
                with dve.Fori(start, n // 2) as half:
                    panel(half, 0)
                    evac(2 * half - 1, 1)
                    post(2 * half - 2, 0)
                    panel(half, 1)
                    evac(2 * half, 0)
                    post(2 * half - 1, 1)

            def nothing(*_):
                pass

            def x_tile(k):
                return x[:, bass.ds(k, 1), :].rearrange("p a t -> p (a t)")

            def b_tile(b, k):
                return b[:, bass.ds(k, 1), :].rearrange("p a t -> p (a t)")

            def clear(squares=ssum):
                v = steps.mark(dve.memset(squares, 0.0))
                dve.wait_ge(dve_step, v)

            def prepare(np, src, k, s, gain, dst, squares=ssum):
                dve.wait_ge(prep_hi, np + 1)
                for buf, at, g in zip(dst[0], dst[1], gain):
                    g_col = vec[:, bass.ds(k + VEC[g], 1)]
                    dve.scalar_tensor_tensor(b_tile(b_lo[buf], k + at), src, g_col,
                                             b_tile(b_hi[buf], k + at).bitcast(F32), ALU.mult, ALU.subtract)
                if not (isinstance(np, int) and np == 0):
                    dve.wait_ge(prep_lo, np)
                dve.tensor_tensor(squares, squares, sq[s], ALU.add).then_inc(prep_lo, 1)

            def prepare_x(norm, gain, dst):
                return lambda j, s: prepare(j + PREP0[norm], x_tile(j), j, s, gain, dst)

            def reciprocal_root(norm, dst=rstd):
                dve.wait_ge(norm_std, NORM[norm] + 1)
                dve.reciprocal(dst, std).then_inc(norm_rstd, 1)
                dve.wait_ge(norm_rstd, NORM[norm] + 1)

            def add_to_x(t0):
                def evac(j, s):
                    dve.wait_ge(mm_done, j + (t0 + 1))
                    dve.tensor_tensor(x_tile(j), acc[s][:], x_tile(j), ALU.add).then_inc(acc_free, 1)
                return evac

            dve.wait_ge(vec_in, 16)
            clear()
            for k in range(KT):
                if k % (KT // X_PARTS) == 0:
                    dve.wait_ge(x_in[k // (KT // X_PARTS)], 16)
                prepare(k, x_tile(k), k, k % 2, ("mix_g0",), ((0,), (0,)))
                if k == 1:
                    split(0, 0)
            dve.wait_ge(ws_hi_done, 1)
            dve.wait_ge(const_in, 16 * N_CONST)
            dve.tensor_copy(ident_b[:], ident[:])
            dve.tensor_copy(mask_b[:], mask_q[:])
            dve.tensor_tensor(ws_lo[:], ws_raw[:], ws_hi[:].bitcast(F32), ALU.subtract).then_inc(ws_lo_done, 1)

            def row_minima(n, m):
                for u, rows in enumerate(((3,), (2,), (1, 0))):
                    dve.wait_ge(s_ready, 3 * n + (u + 1))
                    for qb in rows:
                        w = P * (qb + 1)
                        at = 0 if qb else 2 * P
                        c = 4 * m + qb
                        last = dve.tensor_reduce(rmin[:, c:c + 1], s_bank[u][:, at:at + w], AX_X, ALU.min)
                    last.then_inc(row_min, 1)

            def normalise(n, m):
                dve.wait_ge(p_exp, 3 * n + 3)
                v = steps.mark(dve.reciprocal(rinv[:, 4 * m:4 * m + 4], rsum[:, 4 * m:4 * m + 4]))
                dve.wait_ge(dve_step, v)
                for qb in range(QB):
                    part = probs[m][:, P_AT[qb]:P_AT[qb] + P * (qb + 1)]
                    last = dve.tensor_scalar(part, part, rinv[:, 4 * m + qb:4 * m + qb + 1], None, ALU.mult)
                last.then_inc(p_ready, 1)

            def low_context(k, buf, count):
                dve.wait_ge(ctx_hi, count)
                dve.tensor_tensor(b_tile(b_lo[buf], k), c_bank[:], b_tile(b_hi[buf], k).bitcast(F32), ALU.subtract)\
                   .then_inc(ctx_lo, 1)

            def forget_gates():
                dve.wait_ge(f_mm, 1)
                z, s, a = fz[2], fz[3], fz[0]
                v = steps.mark(dve.tensor_tensor(s, s_bank[0][0:FOX_HEADS, :], rstd[0:FOX_HEADS, :], ALU.mult))
                dve.wait_ge(dve_step, v)
                v = steps.mark(dve.tensor_scalar(z, s, col("fox_bf")[0:FOX_HEADS, :], None, ALU.add))
                dve.wait_ge(dve_step, v)
                dve.scalar_tensor_tensor(s, z, -1.0, z, ALU.mult, ALU.max).then_inc(f_abs, 1)

            def sum_forget_gates():
                z, s, a = fz[2], fz[3], fz[0]
                dve.wait_ge(f_ln, 2)
                dve.wait_ge(ones_set, 2)
                v = steps.mark(dve.scalar_tensor_tensor(a, z, 0.0, s, ALU.min, ALU.subtract))
                dve.wait_ge(dve_step, v)
                dve.tensor_tensor_scan(z, fz[1], a, 0.0, ALU.mult, ALU.add).then_inc(f_cum, 1)
                dve.wait_ge(f_cum, 1)
                dve.tensor_scalar(a, z, -1.0, None, ALU.mult).then_inc(f_cum, 1)

            def heads_rows(dst, t, slot, scale):
                dve.wait_ge(mm_done, t + 1)
                for h in range(2):
                    rows = slice(FOX_DH * h, FOX_DH * (h + 1))
                    last = dve.scalar_tensor_tensor(dst[h][0:FOX_DH, :], acc[slot][rows, :], scale, rstd[rows, :],
                                                    ALU.mult, ALU.mult)
                last.then_inc(acc_free, 1)

            def fox_step(pp, m, project=True, attend=True, late=True):
                p = 2 * pp + m
                c = 7 * p - 6
                if project:
                    split(3 * pp + (3 * m + 1) // 2, 1 - m)
                    if not attend:
                        reciprocal_root("fox")
                        clear()
                        forget_gates()
                    heads_rows(qa[m], 3 * p, m, -FOX_SCALE)
                if late:
                    low_context(p - 2, 1, p - 1)
                if attend:
                    row_minima(2 * p - 2, 0)
                if project:
                    split(3 * pp + (3 * m + 2) // 2, m)
                if attend:
                    normalise(2 * p - 2, 0)
                if project:
                    heads_rows(ka[m], 3 * p + 1, 1 - m, 1.0)
                if attend:
                    row_minima(2 * p - 1, 1)
                else:
                    sum_forget_gates()
                if project:
                    split(3 * pp + (3 * m + 3) // 2, 1 - m)
                if attend:
                    normalise(2 * p - 1, 1)
                if project:
                    dve.wait_ge(mm_done, 3 * p + 3)
                    if attend:
                        dve.wait_ge(t_ready, c)
                    dve.tensor_tensor(v_t, acc[m][:], rstd, ALU.mult).then_inc(acc_free, 1)

            fox_step(0, 0, attend=False, late=False)
            fox_step(0, 1, late=False)
            with dve.Fori(1, FOX_PAIRS // 2) as pp:
                steps.enter(pp - 1, 4)
                fox_step(pp, 0)
                fox_step(pp, 1)
            steps.leave(FOX_PAIRS // 2 - 1)
            split(PANEL0["fox_out"] // 2, 1)
            fox_step(FOX_PAIRS // 2, 0, project=False)

            out_a, post_a = add_to_x(TILE0["fox_out"]), prepare_x("ff_a", ("ff_g0",), ((0,), (0,)))
            segment("fox_out", 0, KT, out_a, post_a, nothing, lambda: low_context(FOX_PAIRS - 1, 1, FOX_PAIRS), nothing,
                    fresh=2)

            def ffn(run, hid, evac, post, norm, last_post, beside):
                for i, (what, c) in enumerate(FF_ORDER):
                    t0 = TILE0[run] + i * KT

                    def relu(j, s, t0=t0, c=c):
                        n = j + (HID0[run] + c * KT)
                        dve.wait_ge(mm_done, j + (t0 + 1))
                        if not (isinstance(n, int) and n < 2):
                            dve.wait_ge(ff_sq, n - 1)
                        dve.scalar_tensor_tensor(ff_t[s], acc[s][:], 0.0, rstd, ALU.max, ALU.mult).then_inc(acc_free, 1)

                    def low(j, s, c=c):
                        n = j + (HID0[run] + c * KT)
                        dve.wait_ge(sq_hi, n + 1)
                        dve.tensor_tensor(b_tile(b_lo[hid[c % 2]], j), ff_s[s],
                                          b_tile(b_hi[hid[c % 2]], j).bitcast(F32), ALU.subtract).then_inc(hid_lo, 1)

                    def lead0():
                        evac(KT - 1, 1)
                        post(KT - 2, 0)

                    def lead1():
                        post(KT - 1, 1)
                        if i == 1:
                            clear()
                            if norm == "ff_b":
                                clear(ssum_g)

                    if what == "u":
                        now = relu, low
                    else:
                        now = add_to_x(t0), last_post if c == FF_CHUNKS - 1 else nothing
                    segment(run, i * KT, KT, *now, lead0, lead1, (lambda: reciprocal_root(norm)) if i == 0 else None,
                            beside=beside if 1 <= i < 7 else None)
                    evac, post = now
                return evac, post

            def conditioning(j, s):
                j = j - KT
                if isinstance(j, int) and j == 0:
                    dve.wait_ge(ada_silu, 1)
                dve.wait_ge(ada_in[s], (j - s) * 8 + 16)
                if not (isinstance(j, int) and j == 0):
                    dve.wait_ge(ada_done, j)
                dve.scalar_tensor_tensor(ada_p, ada_w[s], 1.0, ada_c, ALU.mult, ALU.mult,
                                         accum_out=mod[:, bass.ds(j, 1)]).then_inc(ada_done, 1)

            evac, post = ffn("ff_a", (1, 2), out_a, post_a, "ff_a",
                             prepare_x("mla", ("kv_g", "mix_g1"), ((0, 1), (0, 0))), conditioning)

            half0, t0 = PANEL0["kva_qa"] // 2, TILE0["kva_qa"]
            split(half0, 0)
            evac(KT - 1, 1)
            post(KT - 2, 0)
            split(half0, 1)
            post(KT - 1, 1)
            split(half0 + 1, 0)
            reciprocal_root("mla")

            def prepare_low(norm, n, at):
                for j in range(n):
                    prepare(PREP0[norm] + j, low[at + j], j, (PREP0[norm] + j) % 2,
                            ("kva_g" if norm == "ckv" else "qa_g",), ((2,), (at,)), low_sum if norm == "ckv" else ssum)

            for i in range(6):
                if i == 2:
                    clear()
                    clear(low_sum)
                    dve.wait_ge(rope_in, 32)
                if 2 <= i < 5:
                    split(half0 + (i + 1) // 2, (i + 1) % 2)
                if i == 3:
                    prepare_low("ckv", KVKT, QKT)
                if i == 5:
                    reciprocal_root("ckv", rstd_kv)
                dve.wait_ge(mm_done, t0 + i + 1)
                if i == 2:
                    v = steps.mark(dve.tensor_tensor(kr_tmp, rope, rstd, ALU.mult))
                    dve.wait_ge(dve_step, v)
                    dve.tensor_tensor(kr_raw, acc[0][:], kr_tmp, ALU.mult).then_inc(acc_free, 1)
                else:
                    dst = low[QKT + i] if i < 2 else low[i - 3]
                    dve.tensor_tensor(dst, acc[i % 2][:], rstd, ALU.mult).then_inc(acc_free, 1)
            dve.wait_ge(kr_mm, 1)
            dve.tensor_copy(k_rope, s_bank[0][:]).then_inc(kr_done, 1)
            prepare_low("cq", QKT, 0)
            split(PANEL0["mla"] // 2, 0, Q_COLS)
            split(PANEL0["mla"] // 2, 1, KV_COLS)
            reciprocal_root("cq")
            clear()
            v = steps.mark(dve.scalar_tensor_tensor(rope_q, rope, -MLA_SCALE, rstd, ALU.mult, ALU.mult))
            dve.wait_ge(dve_step, v)

            def mla_step(hh, m, project=True, attend=True, late=True, ahead=True):
                h = 2 * hh + m
                n = h + HEAD0["mla"]
                t = 4 * h + TILE0["mla"]
                if project:
                    dve.wait_ge(mm_done, t + 1)
                    dve.scalar_tensor_tensor(qa[m][0], acc[0][:], -MLA_SCALE, rstd, ALU.mult, ALU.mult).then_inc(acc_free, 1)
                    dve.wait_ge(mm_done, t + 2)
                    dve.tensor_tensor(qa[m][1], acc[1][:], rope_q, ALU.mult).then_inc(acc_free, 1)
                if attend:
                    row_minima(n - 1, 1 - m)
                if project:
                    dve.wait_ge(mm_done, t + 3)
                    dve.tensor_tensor(ka[m][0], acc[0][:], rstd_kv, ALU.mult).then_inc(acc_free, 1)
                    dve.wait_ge(mm_done, t + 4)
                    if attend:
                        dve.wait_ge(t_ready, 4 * h + (T0_MLA - 6) if late else T0_MLA + 1)
                    dve.tensor_tensor(v_t, acc[1][:], rstd_kv, ALU.mult).then_inc(acc_free, 1)
                if ahead:
                    split(h + (PANEL0["mla"] // 2 + 1), 0, Q_COLS)
                if attend:
                    normalise(n - 1, 1 - m)
                if ahead:
                    split(h + (PANEL0["mla"] // 2 + 1), 1, KV_COLS)
                if late:
                    low_context(h - 2, 0, h + (CTX0["mla"] - 1))

            mla_step(0, 0, attend=False, late=False)
            mla_step(0, 1, late=False)
            with dve.Fori(1, MLA_HEADS // 2 - 1) as hh:
                steps.enter(hh - 1, 2)
                mla_step(hh, 0)
                mla_step(hh, 1)
            steps.leave(MLA_HEADS // 2 - 2)
            mla_step(MLA_HEADS // 2 - 1, 0)
            mla_step(MLA_HEADS // 2 - 1, 1, ahead=False)
            split(PANEL0["mla_out"] // 2, 0)
            split(PANEL0["mla_out"] // 2, 1)
            mla_step(MLA_HEADS // 2, 0, project=False, ahead=False)

            out_b, post_b = add_to_x(TILE0["mla_out"]), prepare_x("ff_b", ("ff_g1",), ((1,), (0,)))
            segment("mla_out", 0, KT, out_b, post_b, nothing,
                    lambda: low_context(MLA_HEADS - 1, 0, CTX0["mla"] + MLA_HEADS), nothing, fresh=2)

            def add_squares(norm):
                def post(j, s):
                    dve.wait_ge(prep_hi, j + (PREP0[norm] + 1))
                    dve.wait_ge(prep_lo, j + PREP0[norm])
                    dve.tensor_tensor(ssum, ssum, sq[s], ALU.add).then_inc(prep_lo, 1)
                return post

            def y_tile(j):
                return arena[:, bass.ds(j + y_at, 1), :].rearrange("p a t -> p (a t)")

            def add_both(j, s):
                dve.wait_ge(prep_hi, j + (PREP0["final"] + 1))
                dve.wait_ge(prep_lo, j + PREP0["final"])
                dve.tensor_tensor(ssum, ssum, sq[s], ALU.add)
                dve.tensor_tensor(ssum_g, ssum_g, sq_g[s], ALU.add).then_inc(prep_lo, 1)

            evac, post = ffn("ff_b", (0, 2), out_b, post_b, "ff_b", add_both, None)
            evac(KT - 1, 1)
            post(KT - 2, 0)
            post(KT - 1, 1)
            dve.wait_ge(prep_lo, PREP0["final"] + KT)
            dve.scalar_tensor_tensor(ssum_g, ssum, EPS, ssum_g, ALU.mult, ALU.add).then_inc(both_sum, 1)
            half0, t0 = PANEL0["mix_in"] // 2, TILE0["mix_in"]
            for s in range(2):
                split(half0, s, PANEL // 2)

            dve.wait_ge(ada_done, 6 * KT)
            v = steps.mark(dve.tensor_tensor(mod[:], mod[:], vec[:, VEC["ada_b"]:VEC["ada_b"] + 6 * KT], ALU.add))
            dve.wait_ge(dve_step, v)
            for i, gain, plus in ((1, "tm_pre_g", 1.0), (2, "tm_post_g", 0.0), (4, "cm_pre_g", 1.0), (5, "cm_post_g", 0.0)):
                part = mod[:, i * KT:(i + 1) * KT]
                last = dve.scalar_tensor_tensor(part, part, plus, vec[:, VEC[gain]:VEC[gain] + KT], ALU.add, ALU.mult)
            v = steps.mark(last)
            dve.wait_ge(dve_step, v)
            part = mod[:, KT:2 * KT]
            dve.tensor_tensor(part, part, vec[:, VEC["final_g"]:VEC["final_g"] + KT], ALU.mult).then_inc(mod_ready, 1)
            reciprocal_root("x2")

            def modulate(n0, shift, scale):
                def normed(k, s):
                    if n0 or not (isinstance(k, int) and k < 2):
                        dve.wait_ge(h_hi, k + (n0 - 1))
                    dve.tensor_tensor(mod_t[s], x_tile(k), rstd, ALU.mult).then_inc(h_tmp, 1)

                def low(k, s):
                    dve.wait_ge(h_hi, k + (n0 + 1))
                    dve.tensor_tensor(b_tile(b_lo[0], k), mod_y[s], b_tile(b_hi[0], k).bitcast(F32), ALU.subtract)\
                       .then_inc(h_lo, 1)

                normed(0, 0)
                normed(1, 1)
                with dve.Fori(1, KT // 2) as half:
                    for s in range(2):
                        low(2 * half + (s - 2), s)
                        normed(2 * half + s, s)
                for s in range(2):
                    low(KT - 2 + s, s)

            modulate(0, 0, 1)

            def own(ins):
                dve.wait_ge(dve_step, steps.mark(ins))

            def head_gates():
                dve.wait_ge(rows_in, 1)
                dve.scalar_tensor_tensor(row_b, row_z, -1.0, row_z, ALU.mult, ALU.max).then_inc(row_abs, 1)

            def head_rows():
                dve.wait_ge(row_ln, 2)
                own(dve.scalar_tensor_tensor(row_z, row_z, 0.0, row_b, ALU.min, ALU.subtract))
                own(dve.tensor_tensor_scan(row_b, row_z, row_z, 0.0, ALU.add, ALU.min))
                dve.tensor_tensor(row_u, row_u, row_b, ALU.subtract).then_inc(row_u_done, 1)
                dve.wait_ge(row_u_done, 1)
                own(dve.tensor_tensor_scan(row_z, row_u, row_u, 0.0, ALU.max, ALU.max))
                dve.tensor_scalar(row_z, row_z, -1.0, None, ALU.mult).then_inc(row_max, 1)
                dve.wait_ge(row_max, 1)
                dve.tensor_tensor(row_b, row_z, row_b, ALU.subtract).then_inc(row_floor, 1)

            def gated(i):
                dve.wait_ge(mix_free, CONF + 2 + i - 1)
                if i == 0:
                    dve.wait_ge(pads_set, 4)
                at = i * CONF_PAD + CONF_W - 1
                dve.tensor_tensor(conf_pad[:, at:at + T], conf_a[i], conf_g[i], ALU.mult).then_inc(pad_ready, 1)
                dve.wait_ge(pad_ready, i + 1)
                own(dve.tensor_scalar(conf_u[i], conf_pad[:, i * CONF_PAD:i * CONF_PAD + T], col("conf_w", i),
                                      col("conf_b", i), ALU.mult, ALU.add))

            def short(i):
                dve.wait_ge(mix_free, SC + 4 + i - 1)
                at = i * SC_PAD
                dve.tensor_tensor(sc_pad[:, at + SC_W - 1:at + SC_W - 1 + T], sc_c[i], sc_x[i], ALU.mult).then_inc(pad_ready, 1)
                dve.wait_ge(pad_ready, 3 + i)
                own(dve.tensor_scalar(sc_u[i], sc_pad[:, at:at + T], col("sc_w", i), None, ALU.mult))
                for tap in range(1, SC_W):
                    ins = dve.scalar_tensor_tensor(sc_u[i], sc_pad[:, at + tap:at + tap + T], col("sc_w", 2 * tap + i),
                                                   sc_u[i], ALU.mult, ALU.add)
                    if tap < SC_W - 1:
                        own(ins)
                ins.then_inc(conv_done, 1)
                dve.wait_ge(conv_done, i + 1)
                dve.tensor_tensor(sc_u[i], sc_u[i], sc_b[i], ALU.mult).then_inc(sc_out, 1)

            def sc_low(i):
                dve.wait_ge(sc_hi, i + 1)
                dve.tensor_tensor(b_lo[1][:, 6 + i, :], sc_u[i], b_hi[1][:, 6 + i, :].bitcast(F32), ALU.subtract)\
                   .then_inc(sc_lo, 1)

            def finish_x(first):
                for k in (first, first + 1):
                    dve.scalar_tensor_tensor(x[:, k, :], x[:, k, :], col("final_g", k), rstd_f, ALU.mult, ALU.mult)\
                       .then_inc(x_done, 1)

            beside = {2: lambda: reciprocal_root("final", rstd_f), 3: head_gates, 5: head_rows, 8: lambda: finish_x(0), 9: lambda: finish_x(2),
                      10: lambda: finish_x(4), 11: lambda: finish_x(6), 6: lambda: gated(0), 7: lambda: gated(1),
                      12: lambda: short(0), 13: lambda: short(1)}
            for i in range(2, 14):
                split(half0 + i // 2, i % 2)
                if i in beside:
                    beside[i]()
            TAPS = 3
            with dve.Fori(0, (CONF_W - 1) // (2 * TAPS)) as half:
                steps.enter(half, 4 * TAPS)
                for s in range(2):
                    split(half + (half0 + 7), s)
                    for t in range(TAPS):
                        for i in range(2):
                            dve.wait_ge(dve_step, steps.moved + steps.count - 1)
                            at = half * (2 * TAPS) + (1 + TAPS * s + t + i * CONF_PAD)
                            w = half * (4 * TAPS) + (VEC["conf_w"] + 2 * (1 + TAPS * s + t) + i)
                            steps.mark(dve.scalar_tensor_tensor(conf_u[i], conf_pad[:, bass.ds(at, T)],
                                                                vec[:, bass.ds(w, 1)], conf_u[i], ALU.mult, ALU.add))
            steps.leave((CONF_W - 1) // (2 * TAPS))
            dve.wait_ge(dve_step, steps.count)
            dve.sem_inc(conv_done, 2)
            for i in range(2):
                sc_low(i)
            for i in range(24, 28):
                split(half0 + i // 2, i % 2)
            half0, t0 = PANEL0["merge"] // 2, TILE0["merge"]
            split(half0, 0)
            split(half0, 1)

            dve.wait_ge(u_turned, 1)
            dve.tensor_copy(u_col, s_bank[2][:, 0:QB * HEADS]).then_inc(u_read, 1)

            dve.wait_ge(ln_mean, 1)
            for i in range(2):
                dve.scalar_tensor_tensor(conf_u[i], c_bank[:], -1.0 / MIX, conf_u[i], ALU.mult, ALU.add).then_inc(ln_dev, 1)
            dve.wait_ge(ln_std, 1)
            own(dve.reciprocal(ml_s_std, ml_s_std))
            for i in range(2):
                dve.tensor_tensor(conf_u[i], conf_u[i], ml_s_std, ALU.mult).then_inc(ln_out, 1)
            for i in range(2):
                dve.wait_ge(ln_hi, i + 1)
                dve.tensor_tensor(b_lo[1][:, 4 + i, :], conf_u[i], b_hi[1][:, 4 + i, :].bitcast(F32), ALU.subtract)\
                   .then_inc(ln_lo, 1)

            def weigh(h):
                w = ml_w[h % 2]
                dve.wait_ge(qk_ready, h + 1)
                dve.wait_ge(w_exp, h + 1)
                for at, src, n in ((0, t_bank[0], T), (T, t_bank[1], T), (2 * T, s_bank[2], 2 * P)):
                    last = dve.tensor_tensor(w[:, at:at + n], src[:, 0:n], w[:, at:at + n], ALU.mult)
                last.then_inc(a_ready, 1)

            def quotient(c):
                dve.wait_ge(den_abs, c + 1)
                own(dve.tensor_tensor(ml_den, ml_den, acc[1][:], ALU.max))
                own(dve.reciprocal(ml_den, ml_den))
                dve.tensor_tensor(ml_h, c_bank[:], ml_den, ALU.mult).then_inc(head_h, 1)

            def head_norm(i, src, root, dst, gain, gates):
                dve.wait_ge(head_std, i + 1)
                own(dve.reciprocal(root, root))
                if i < 2:
                    own(dve.tensor_tensor(dst, src, root, ALU.mult))
                else:
                    dve.tensor_tensor(dst, src, root, ALU.mult).then_inc(head_h, 1)
                    dve.wait_ge(head_h, i + 1)
                dve.scalar_tensor_tensor(dst, dst, gain, gates, ALU.mult, ALU.mult).then_inc(head_out, 1)
                dve.wait_ge(head_hi, i + 1)
                dve.tensor_tensor(b_lo[1][:, i, :], dst, b_hi[1][:, i, :].bitcast(F32), ALU.subtract).then_inc(head_lo, 1)

            weigh(0)
            weigh(1)
            quotient(0)
            weigh(2)
            head_norm(0, ml_h, ml_s, ml_h, col("ml_g", 0), ml_o[0])
            weigh(3)
            quotient(1)
            head_norm(1, ml_h, ml_s, ml_h, col("ml_g", 1), ml_o[1])

            for c in range(2):
                dve.wait_ge(gz_in, c + 1)
                dve.scalar_tensor_tensor(gla_t[c], gla_z[c], -1.0, gla_z[c], ALU.mult, ALU.max).then_inc(gz_abs, 1)
            for c in range(2):
                dve.wait_ge(gz_ln, 2 * c + 2)
                own(dve.scalar_tensor_tensor(gla_z[c], gla_z[c], 0.0, gla_t[c], ALU.min, ALU.subtract))
                own(dve.tensor_tensor_scan(gla_b[c], chunk_start, gla_z[c], 0.0, ALU.mult, ALU.add))
                b3, z3, t3 = (x_.rearrange("p (n t) -> p n t", t=GLA_CHUNK) for x_ in (gla_b[c], gla_z[c], gla_t[c]))
                half = GLA_CHUNK // 2
                shape = [P, CHUNKS, GLA_CHUNK]
                dve.tensor_tensor(z3, b3, b3[:, :, half - 1:half].to_broadcast(shape), ALU.subtract)
                dve.tensor_tensor(t3, b3[:, :, GLA_CHUNK - 1:GLA_CHUNK].to_broadcast(shape), b3, ALU.subtract)\
                   .then_inc(gz_sum, 1)

            def scaled(c):
                dve.wait_ge(g_exp, c + 1)
                dve.memset(gla_decay[c][:, 0:1], 0.0)
                for e, src in zip(gla_e[c], (gla_q[c], gla_k[c], gla_q[c], gla_k[c])):
                    last = dve.tensor_tensor(e, e, src, ALU.mult)
                last.then_inc(g_scaled, 1)

            def masked(c):
                dve.wait_ge(gs_ready, c + 1)
                dve.wait_ge(gw_set, 2)
                if c:
                    dve.wait_ge(g_out, c)
                for m in range(2):
                    w3, s3 = (x_.rearrange("p (b t) -> p b t", b=QB) for x_ in (gla_w[m], t_bank[m][:]))
                    mask = mask_gla[:].rearrange("p (b t) -> p b t", b=1).to_broadcast([P, QB, P])
                    last = dve.copy_predicated(w3, mask, s3)
                last.then_inc(gs_read, 1)

            def states(c):
                dve.wait_ge(gu_read, c + 1)
                dve.wait_ge(g_scaled, c + 1)
                decay = gla_decay[c].rearrange("p (e n) -> p e n", e=1).to_broadcast([P, DH, CHUNKS])
                own(dve.tensor_copy(gla_s[c].rearrange("p (e n) -> p e n", n=CHUNKS), decay))
                last = dve.tensor_tensor_scan(gla_s[c], gla_s[c], gla_u[c], 0.0, ALU.mult, ALU.add)
                last.then_inc(g_state, 1)

            def gla_norm(c):
                head_norm(2 + c, c_bank[:], gla_e[c][0], gla_e[c][1], col("gla_g", c), gla_r[c])

            scaled(0)
            masked(0)
            scaled(1)
            states(0)
            masked(1)
            gla_norm(0)
            states(1)
            gla_norm(1)

            def branches(j, m):
                for b in range(BRANCHES):
                    dve.wait_ge(mm_done, 8 * j + (t0 + BRANCHES + b + 1))
                    dve.wait_ge(gate_done, 4 * j + (b + 1))
                    if b == 2:
                        bias = vec[:, bass.ds(j + VEC["conf_out_b"], 1)]
                        ins = dve.scalar_tensor_tensor(gate[m][b], branch_bank[b][:], bias, gate[m][b], ALU.add, ALU.mult)
                    else:
                        ins = dve.tensor_tensor(gate[m][b], branch_bank[b][:], gate[m][b], ALU.mult)
                    ins.then_inc(branch_read, 1)
                if not (isinstance(j, int) and j < 2):
                    dve.wait_ge(merge_hi, j - 1)
                dve.wait_ge(branch_read, 4 * j + BRANCHES)
                own(dve.tensor_tensor(merged[m], gate[m][0], gate[m][1], ALU.add))
                own(dve.tensor_tensor(merged[m], merged[m], gate[m][2], ALU.add))
                dve.tensor_tensor(merged[m], merged[m], gate[m][3], ALU.add).then_inc(merge_out, 1)

            def merged_low(j, m):
                dve.wait_ge(merge_hi, j + 1)
                dve.tensor_tensor(b_tile(b_lo[2], j), merged[m], b_tile(b_hi[2], j).bitcast(F32), ALU.subtract)\
                   .then_inc(merge_lo, 1)

            def merge_tile(j, jj, m):
                first = isinstance(j, int) and j == 0
                for p in range(5):
                    i = 5 * m + p
                    if not (first and p < 2):
                        split(5 * jj + (half0 + i // 2), i % 2)
                    if not first and p == 0:
                        branches(j - 1, 1 - m)
                    if not first and p == 1:
                        merged_low(j - 1, 1 - m)

            merge_tile(0, 0, 0)
            merge_tile(1, 0, 1)
            with dve.Fori(1, KT // 2) as jj:
                steps.enter(jj - 1, 4)
                merge_tile(2 * jj, jj, 0)
                merge_tile(2 * jj + 1, jj, 1)
            steps.leave(KT // 2 - 1)

            def keep(t0):
                def evac(j, s):
                    dve.wait_ge(mm_done, j + (t0 + 1))
                    dve.tensor_copy(y_tile(j), acc[s][:]).then_inc(acc_free, 1)
                return evac

            def start_y():
                merged_low(KT - 1, 1)
                clear()

            evac, post = keep(TILE0["w_o"]), add_squares("mix_y")
            segment("w_o", 0, KT, evac, post, lambda: branches(KT - 1, 1), start_y)
            evac(KT - 1, 1)
            post(KT - 2, 0)
            post(KT - 1, 1)
            half0, t0 = PANEL0["ffn2"] // 2, TILE0["ffn2"]
            for s in range(2):
                split(half0, s)
            reciprocal_root("mix_y")

            def add_normed(n0, scale):
                def work(half, s):
                    k = 2 * half + s
                    if s == 0:
                        v = steps.mark(dve.tensor_tensor(y_tile(k), y_tile(k), rstd, ALU.mult))
                        dve.wait_ge(dve_step, v)
                    else:
                        dve.wait_ge(y_normed, half + (n0 + 1))
                    dve.scalar_tensor_tensor(x_tile(k), y_tile(k), mod[:, bass.ds(k + scale * KT, 1)], x_tile(k), ALU.mult,
                                             ALU.add).then_inc(x_done, 1)

                with dve.Fori(0, KT // 2) as half:
                    steps.enter(half, 1)
                    for s in range(2):
                        work(half, s)
                steps.leave(KT // 2)

            add_normed(0, 2)
            reciprocal_root("cm")
            modulate(KT, 3, 4)

            lead0 = lead1 = nothing
            fresh = 2
            for what, c, first in FFN2_STEPS:
                n, f0 = FFN2_CHUNKS[c], FREE0["ffn2"] + first
                half0, t0 = (PANEL0["ffn2"] + first) // 2, TILE0["ffn2"] + first
                if what == "u":
                    def taps(j, is_v, f0=f0, hid_j=HID_AT[c]):
                        dst = hid_v if is_v else hid_a
                        dve.wait_ge(tap_last, 2 * j + (2 * hid_j + is_v + 1))
                        for tap in (1, 0):
                            back = FFN_W - 1 - tap
                            w = vec[:, bass.ds(j + (VEC["ffn_w"] + tap * 2 * HID_T + is_v * HID_T + hid_j), 1)]
                            ins = dve.scalar_tensor_tensor(dst[:, back:T], acc[is_v][:, 0:T - back], w, dst[:, back:T],
                                                           ALU.mult, ALU.add)
                            if tap:
                                own(ins)
                        ins.then_inc(acc_free, 1)

                    def product(j, f0=f0, hid_j=HID_AT[c]):
                        dve.wait_ge(hid_silu, j + (hid_j + 1))
                        dve.wait_ge(acc_free, 2 * j + (f0 + 2))
                        dve.tensor_tensor(hid_v, hid_a, hid_v, ALU.mult).then_inc(hid_out, 1)

                    def hidden_low(j, hid_j=HID_AT[c], buf=1 + c % 2):
                        dve.wait_ge(hid_hi, j + (hid_j + 1))
                        dve.tensor_tensor(b_tile(b_lo[buf], j), hid_v, b_tile(b_hi[buf], j).bitcast(F32), ALU.subtract)\
                           .then_inc(hid_lo, 1)

                    if not fresh:
                        split(half0, 0)
                    lead0()
                    if not fresh:
                        split(half0, 1)
                    lead1()
                    taps(0, 0)
                    with dve.Fori(1, n) as j:
                        steps.enter(j - 1, 2)
                        split(j + half0, 0)
                        taps(j - 1, 1)
                        product(j - 1)
                        split(j + half0, 1)
                        hidden_low(j - 1)
                        taps(j, 0)
                    steps.leave(n - 1)

                    def lead0(n=n, taps=taps, product=product):
                        taps(n - 1, 1)
                        product(n - 1)

                    def lead1(n=n, hidden_low=hidden_low):
                        hidden_low(n - 1)
                    fresh = 0
                else:
                    def add_to_y(j, s, t0=t0):
                        dve.wait_ge(mm_done, j + (t0 + 1))
                        dve.tensor_tensor(y_tile(j), acc[s][:], y_tile(j), ALU.add).then_inc(acc_free, 1)

                    evac = add_to_y if c else keep(t0)
                    post = add_squares("ffn_y") if c == len(FFN2_CHUNKS) - 1 else nothing

                    def start_down(lead1=lead1, c=c):
                        lead1()
                        if c == len(FFN2_CHUNKS) - 1:
                            clear()

                    segment("ffn2", first, KT, evac, post, lead0, start_down, width=n * P)

                    def lead0(evac=evac, post=post):
                        evac(KT - 1, 1)
                        post(KT - 2, 0)

                    def lead1(post=post):
                        post(KT - 1, 1)
            lead0()
            lead1()
            reciprocal_root("ffn_y")
            add_normed(KT // 2, 5)


def kernel(**inputs):
    import concourse.bacc as _bacc
    from concourse.bass_utils import run_bass_kernel_spmd as _run

    laid = lay_out(inputs)
    nc = _bacc.Bacc("TRN2", target_bir_lowering=False, num_devices=1)
    d = {}
    for name, a in laid.items():
        d[name] = nc.dram_tensor(f"in_{name}", a.shape, mybir.dt.from_np(a.dtype), kind="ExternalInput").ap()
    out = nc.dram_tensor("out_xT", (P, KT * T), F32, kind="ExternalOutput").ap()
    crow = nc.dram_tensor("crow", (FOX_HEADS, 4, T), F32, kind="Internal").ap()
    program(nc, d, out, crow)
    r = _run(nc, [{f"in_{name}": a for name, a in laid.items()}], core_ids=[0])
    got = r.results[0]["out_xT"]
    return got.reshape(P, KT, T).transpose(1, 0, 2).reshape(D, T).T.reshape(1, T, D)
```

```python
from contextlib import ExitStack

import numpy as np

import concourse.bass as bass
from concourse import mybir

F32 = mybir.dt.float32
F32R = mybir.dt.float32r
BF16 = mybir.dt.bfloat16
I32 = mybir.dt.int32
ACT = mybir.ActivationFunctionType
ALU = mybir.AluOpType
AX_X = mybir.AxisListType.X

P = 128
T = 512
D = 1024
KT = D // P
PANEL = KT * P
QB = T // P
EPS = 1e-6
BIG = 1e30

FOX_HEADS = 16
FOX_DH = D // FOX_HEADS
FOX_PAIRS = FOX_HEADS // 2
FOX_SCALE = FOX_DH ** -0.5
MLA_HEADS = 8
NOPE = 128
ROPE = 64
VDIM = 128
Q_RANK = 384
KV_RANK = 256
QKT = Q_RANK // P
KVKT = KV_RANK // P
MLA_SCALE = (NOPE + ROPE) ** -0.5
ROPE_BASE = 10000.0
D_FF = 4 * D
FF_CHUNKS = D_FF // D

MIX = D // 4
HEADS = 4
DH = MIX // HEADS
GLA_RANK = 16
GLA_TAU = 16.0
GLA_CHUNK = 32
CHUNKS = T // GLA_CHUNK
CONF_W = 31
SC_W = 3
FFN_W = 3
HID = ((8 * D // 3 + 255) // 256) * 256
HID_T = HID // P
BRANCHES = 4
F_ROW, I_ROW, A_ROW = 0, 32, 64

MIX_T = MIX // P
CONF = 2
SC = CONF + 2 * MIX_T
ML = SC + 3 * MIX_T
GLA = ML + 4 * MIX_T
N_MIX_IN = GLA + 4 * MIX_T

RUNS = (
    ("qkv", 3 * FOX_PAIRS), ("fox_out", KT), ("ff_a", 2 * FF_CHUNKS * KT), ("low", QKT + KVKT + 1),
    ("mla", 2 * MLA_HEADS), ("mla_out", KT), ("ff_b", 2 * FF_CHUNKS * KT), ("mix_in", N_MIX_IN),
    ("merge", (BRANCHES + 1) * KT), ("w_o", KT), ("ffn2", 2 * HID_T + 3 * KT),
)
PANEL0, at = {}, 0
for _name, _n in RUNS:
    PANEL0[_name] = at
    at += _n
N_PANELS = at
Q_COLS = QKT * (NOPE + 2 * ROPE)
KV_COLS = KVKT * (NOPE + VDIM)
FFN2_CHUNKS = (8, 8, HID_T - 16)
FF_ORDER = (("u", 0), ("u", 1), ("d", 0), ("u", 2), ("d", 1), ("u", 3), ("d", 2), ("d", 3))
FFN2_ORDER = (("u", 0), ("u", 1), ("d", 0), ("u", 2), ("d", 1), ("d", 2))

VEC_COLS = (
    ("mix_g0", KT), ("mix_g1", KT), ("ff_g0", KT), ("ff_g1", KT), ("kv_g", KT), ("final_g", KT),
    ("kva_g", KVKT), ("qa_g", QKT), ("ada_b", 6 * KT), ("tm_pre_g", KT), ("tm_post_g", KT),
    ("cm_pre_g", KT), ("cm_post_g", KT), ("ml_g", 2), ("gla_g", 2), ("conf_w", 2 * CONF_W),
    ("conf_b", 2), ("ln_g", 2), ("ln_b", 2), ("conf_out_b", KT), ("sc_w", 2 * SC_W),
    ("gate_b", BRANCHES * KT), ("ffn_w", FFN_W * 2 * HID_T), ("gla_b", 2),
    ("fox_bf", 1), ("ml_bi", 1), ("ml_bf", 1), ("eps", 1), ("eps2", 1), ("one", 1),
)
VEC, at = {}, 0
for _name, _n in VEC_COLS:
    VEC[_name] = at
    at += _n
N_VEC = at


def panels(w):
    k, n = w.shape
    return w.reshape(k // P, P, n // P, P).transpose(2, 1, 0, 3).reshape(-1)


def one_panel(w):
    k, n = w.shape
    return w.reshape(k // P, P, n).transpose(1, 0, 2).reshape(-1)


def lay_out(i):
    f = {k: np.asarray(v) for k, v in i.items()}
    out = {}
    s = []
    w = f["fox_w_in"][0]
    for p in range(FOX_PAIRS):
        for part in range(3):
            s.append(one_panel(w[:, part * D + p * P:part * D + (p + 1) * P]))
    w_f = w[:, 3 * D:]
    s.append(panels(f["fox_w_out"][0]))

    def ffn(layer):
        up, down = f["ffn_w_up"][layer], f["ffn_w_down"][layer]
        for what, c in FF_ORDER:
            s.append(panels(up[:, c * D:(c + 1) * D] if what == "u" else down[c * D:(c + 1) * D]))

    ffn(0)
    w = f["mla_w_kv_a"]
    swapped = np.concatenate([w[:, KV_RANK + ROPE // 2:], w[:, KV_RANK:KV_RANK + ROPE // 2]], axis=1)
    s.append(panels(f["mla_w_q_a"][0]))
    s.append(panels(np.concatenate([w, swapped], axis=1)))
    wq = f["mla_w_q_b"][0].reshape(Q_RANK, MLA_HEADS, NOPE + ROPE)
    wkv = f["mla_w_kv_b"].reshape(KV_RANK, MLA_HEADS, NOPE + VDIM)
    for h in range(MLA_HEADS):
        q = wq[:, h]
        s.append(one_panel(np.concatenate([q, q[:, NOPE + ROPE // 2:], q[:, NOPE:NOPE + ROPE // 2]], axis=1)))
        s.append(one_panel(wkv[:, h]))
    s.append(panels(f["mla_w_out"][0]))
    ffn(1)
    w = f["w_in_2"][0]
    ml, gla = w[:, 0:4 * MIX], w[:, 4 * MIX + 2 * HEADS:8 * MIX + 2 * HEADS]
    w_if = w[:, 4 * MIX:4 * MIX + 2 * HEADS]
    at = 8 * MIX + 2 * HEADS
    w_a = w[:, at:at + GLA_RANK]
    at += GLA_RANK
    conf, sc = w[:, at:at + 2 * MIX], w[:, at + 2 * MIX:at + 5 * MIX]
    gate = w[:, at + 5 * MIX:]
    narrow = np.zeros((D, P), np.float32)
    narrow[:, F_ROW:F_ROW + HEADS], narrow[:, I_ROW:I_ROW + HEADS] = w_if[:, HEADS:], w_if[:, :HEADS]
    narrow[:, A_ROW:A_ROW + GLA_RANK] = w_a
    for half in range(2):
        s.append(one_panel(narrow[half * D // 2:(half + 1) * D // 2]))
    for part in (conf, sc, ml, gla):
        s.append(panels(part))
    for j in range(KT):
        cols = slice(j * P, (j + 1) * P)
        for b in range(BRANCHES):
            s.append(one_panel(gate[:, b * D + j * P:b * D + (j + 1) * P]))
        branch = [f[n][0][:, cols] for n in ("w_ml_out_2", "w_gla_out_2", "w_conf_out_2", "w_sc_out_2")]
        s.append(one_panel(np.concatenate(branch, axis=0)))
    s.append(panels(f["w_o_2"][0]))
    up, down = f["ffn_w_up_2"][0], f["ffn_w_down_2"][0]
    first = np.cumsum((0,) + FFN2_CHUNKS)
    for what, c in FFN2_ORDER:
        if what == "u":
            for j in range(first[c], first[c + 1]):
                s.append(panels(up[:, j * P:(j + 1) * P]))
                s.append(panels(up[:, HID + j * P:HID + (j + 1) * P]))
        else:
            s.append(panels(down[first[c] * P:first[c + 1] * P]))
    out["wstream"] = np.concatenate(s)
    out["wsmall"] = one_panel(w_f).reshape(P, -1)
    out["ada"] = np.ascontiguousarray(f["ada_w_2"][0].T)
    out["gla_a2"] = np.ascontiguousarray(f["gla_w_a2_2"][0])
    out["cvec"] = np.ascontiguousarray(f["c_2"])
    out["xT"] = np.ascontiguousarray(f["x"][0].T.reshape(KT, P, T).transpose(1, 0, 2)).reshape(P, KT * T)

    v = np.zeros((P, N_VEC), np.float32)

    def put(name, x):
        x = np.asarray(x).reshape(-1)
        v[:, VEC[name]:VEC[name] + x.size // P] = x.reshape(-1, P).T

    for name, x in (
        ("mix_g0", f["norm_mix_g"][0]), ("mix_g1", f["norm_mix_g"][1]), ("ff_g0", f["norm_ffn_g"][0]),
        ("ff_g1", f["norm_ffn_g"][1]), ("kv_g", f["kv_norm_g"]), ("final_g", f["final_norm_g"]),
        ("kva_g", f["mla_kv_a_norm_g"]), ("qa_g", f["mla_q_a_norm_g"]), ("ada_b", f["ada_b_2"]),
        ("tm_pre_g", f["tm_pre_g_2"]), ("tm_post_g", f["tm_post_g_2"]), ("cm_pre_g", f["cm_pre_g_2"]),
        ("cm_post_g", f["cm_post_g_2"]), ("ml_g", f["ml_norm_g_2"]), ("gla_g", f["gla_norm_g_2"]),
        ("conf_w", f["conf_dw_w_2"]), ("conf_b", f["conf_dw_b_2"]), ("ln_g", f["conf_ln_g_2"]),
        ("ln_b", f["conf_ln_b_2"]), ("conf_out_b", f["conf_out_b_2"]), ("sc_w", f["sc_dw_w_2"]),
        ("gate_b", f["merge_gate_b_2"]), ("ffn_w", f["ffn_dw_w_2"]), ("gla_b", f["gla_a_bias_2"]),
    ):
        put(name, x)
    v[0:FOX_HEADS, VEC["fox_bf"]] = f["fox_b_f"][0]
    v[I_ROW:I_ROW + HEADS, VEC["ml_bi"]] = f["ml_i_bias_2"][0]
    v[F_ROW:F_ROW + HEADS, VEC["ml_bf"]] = f["ml_f_bias_2"][0]
    v[:, VEC["eps"]] = EPS
    v[:, VEC["eps2"]] = EPS * EPS
    v[:, VEC["one"]] = 1.0
    out["vecs"] = v

    r = np.arange(P)
    out["ident"] = np.eye(P, dtype=np.float32)
    out["mask_q"] = np.where(r[None, :] > r[:, None], BIG, 0.0).astype(np.float32)
    out["mask_low"] = (r[:, None] > r[None, :]).astype(np.int32)
    out["fold"] = (r[:, None] % 64 == r[None, :] % 64).astype(np.float32)
    out["halves"] = (r[:, None] // 64 == r[None, :] // 64).astype(np.float32)
    same = r[:, None] // GLA_CHUNK == r[None, :] // GLA_CHUNK
    out["mask_gla"] = (same & (r[:, None] <= r[None, :])).astype(np.int32)
    out["chunk_start"] = np.tile((np.arange(T) % GLA_CHUNK != 0).astype(np.float32), (P, 1))
    inv = 1.0 / (ROPE_BASE ** (np.arange(0, ROPE, 2, dtype=np.float32) / np.float32(ROPE)))
    ang = np.arange(T, dtype=np.float32)[:, None] * inv[None, :].astype(np.float32)
    cos, sin = np.cos(ang).T.astype(np.float32), np.sin(ang).T.astype(np.float32)
    out["rope"] = np.concatenate([cos, cos, -sin, sin], axis=0)
    sel = np.zeros((HEADS, HEADS * P), np.float32)
    for h in range(HEADS):
        sel[h, h * P:(h + 1) * P] = 1.0
    out["sel"] = sel
    return out


class Steps:

    def __init__(self, sem):
        self.sem, self.count, self.moved = sem, 0, 0

    def mark(self, ins):
        ins.then_inc(self.sem, 1)
        self.count += 1
        return self.moved + self.count

    def enter(self, turn, marks):
        self.start, self.marks = self.count, marks
        self.moved = turn * marks

    def leave(self, turns):
        assert self.count - self.start == self.marks, (self.count - self.start, self.marks)
        self.count = self.start + self.marks * turns
        self.moved = 0


def program(nc, d, out, crow):
    with ExitStack() as ctx:
        def sb(name, shape, dt=F32):
            return ctx.enter_context(nc.sbuf_tensor(name, shape, dt))

        def sem(name):
            return ctx.enter_context(nc.semaphore(name))

        x = sb("x", [P, KT, T])
        b_hi = [sb(f"b_hi{i}", [P, KT, T], F32R) for i in range(3)]
        b_lo = [sb(f"b_lo{i}", [P, KT, T], F32R) for i in range(3)]
        w_raw = [sb(f"w_raw{i}", [P, PANEL]) for i in range(2)]
        w_hi = [sb(f"w_hi{i}", [P, PANEL], F32R) for i in range(2)]
        w_lo = [sb(f"w_lo{i}", [P, PANEL], F32R) for i in range(2)]
        vec = sb("vec", [P, N_VEC])
        ident = sb("ident", [P, P])
        mask_q = sb("mask_q", [P, P])
        ident_b, mask_b = sb("ident_b", [P, P], BF16), sb("mask_b", [P, P], BF16)
        ones_sq = sb("ones_sq", [P, P])
        small = sb("small", [P, 64])
        ARENA = 32
        arena = sb("arena", [P, ARENA, T])
        bank = [ctx.enter_context(nc.psum_tensor(f"bank{i}", [P, T], F32)) for i in range(8)]
        acc = bank[0:2]
        s_bank = bank[2:5]
        t_bank = bank[5:7]
        c_bank = bank[7]

        def ar(i, n=1):
            return arena[:, i:i + n, :].rearrange("p a t -> p (a t)")

        def col(name, k=0):
            return vec[:, VEC[name] + k:VEC[name] + k + 1]

        rstd, std, ssum = ar(0), ar(1), ar(2)
        sq = [ar(3), ar(4)]
        eps = col("eps")
        WS = KT * FOX_HEADS
        ws_raw, ws_hi, ws_lo = ar(5)[:, 0:WS], b_hi[2][:, 0, 0:WS], b_lo[2][:, 0, 0:WS]
        ff_t = [ar(6), ar(7)]
        ff_s = [ar(8), ar(9)]
        ada_w = [ar(10, 2), ar(12, 2)]
        ada_p = ar(14, 2)
        ada_c = ar(16, 2)
        mod = sb("mod", [P, 6 * KT])
        QA_AT, KA_AT = 6, 10
        qa = [[ar(QA_AT + 2 * m + h) for h in range(2)] for m in range(2)]
        ka = [[ar(KA_AT + 2 * m + h) for h in range(2)] for m in range(2)]
        v_t = ar(14)
        v_tok = [ar(15), ar(16)]
        CAUSAL = P * QB * (QB + 1) // 2
        flat = arena[:, 17:27, :].rearrange("p a t -> p (a t)")
        probs = [flat[:, CAUSAL * m:CAUSAL * (m + 1)] for m in range(2)]
        probs_t = [flat[:, CAUSAL * (2 + m):CAUSAL * (3 + m)] for m in range(2)]
        fz = [ar(27 + i)[0:FOX_HEADS, :] for i in range(4)]
        rope, fold_t = ar(27), ar(28)
        rope_q = ar(29)
        k_rope = ar(30)
        rstd_q, rstd_kv = ar(5), ar(31)
        low = [ar(17 + i) for i in range(QKT + KVKT)]
        kr_raw = ar(22)
        low_sum = ar(23)
        kr_tmp = ar(24)
        halves, zeros, gla_a2 = ar(5)[:, 0:P], ar(5)[:, P:2 * P], ar(5)[32:32 + GLA_RANK, 2 * P:2 * P + MIX]
        chunk_start = ar(6)
        sel = ar(7)[0:HEADS, :]
        mask_gla, mask_low = sb("mask_gla", [P, P], I32), sb("mask_low", [P, P], I32)
        sq_g, ssum_g, rstd_f = [ar(12), ar(13)], ar(14), ar(31)
        mod_t = [ar(8 + i) for i in range(4)]
        mod_y = [ar(12 + i) for i in range(4)]
        conf_a, conf_g = [ar(10), ar(11)], [ar(12), ar(13)]
        sc_b, sc_c, sc_x = [ar(14), ar(15)], [ar(29), ar(30)], [ar(8), ar(9)]
        CONF_PAD, SC_PAD = T + CONF_W - 1, T + SC_W - 1
        pads = arena[:, 24:29, :].rearrange("p a t -> p (a t)")
        conf_pad = pads[:, 0:2 * CONF_PAD]
        sc_pad = pads[:, 2 * CONF_PAD:2 * (CONF_PAD + SC_PAD)]
        conf_u, sc_u = conf_a, sc_c
        ml_q, ml_k, ml_vt, ml_o = [ar(16), ar(17)], [ar(18), ar(19)], [ar(20), ar(21)], [ar(22), ar(23)]
        ml_v = [ar(3), ar(4)]
        gla_q, gla_k, gla_vt, gla_r = [ar(8), ar(9)], [ar(12), ar(13)], [ar(10), ar(11)], [ar(14), ar(15)]
        gla_v = ml_v
        gla_a = ar(7)[32:32 + GLA_RANK, :]
        row_z, row_b, row_u = ar(0)[0:HEADS, :], ar(1)[0:HEADS, :], ar(2)[0:HEADS, :]
        u_col = small[:, 32:32 + QB * HEADS]
        ml_w = [pads[:, CAUSAL * m:CAUSAL * (m + 1)] for m in range(2)]
        ml_den, ml_h, ml_s = ar(31), ar(29), ar(30)
        gla_z, gla_t, gla_b = [ar(16), ar(27)], [ar(17), ar(28)], [ar(18), ar(3)]
        gla_e = [[ar(i) for i in (19, 20, 21, 24)], [ar(i) for i in (4, 2, 22, 0)]]
        gla_u, gla_s = [ar(16, 2), ar(27, 2)], [ar(25, 2), ar(29, 2)]
        gla_w = [ar(1), ar(31)]
        gla_decay = [small[:, 0:CHUNKS], small[:, CHUNKS:2 * CHUNKS]]
        u_bank = [acc[0], s_bank[0], s_bank[2], s_bank[1]]
        gate_bank, branch_bank = s_bank + [c_bank], acc + t_bank
        gate = [[ar(8 + 4 * m + b) for b in range(BRANCHES)] for m in range(2)]
        merged = [ar(5), ar(6)]
        first_gate = sb("first_gate", [P, T])[:]

        def gate_at(j, m, b):
            return first_gate if isinstance(j, int) and j == 0 and b == 0 else gate[m][b]

        y_at = 16
        hid_a, hid_v = ar(8), ar(9)
        ml_s_std = ar(31)
        std_col, rstd_col = small[:, 48:48 + QB], small[:, 52:52 + QB]
        rmin, rsum, rinv = small[:, 0:8], small[:, 8:16], small[:, 16:24]

        P_AT = [P * i * (i + 1) // 2 for i in range(QB)]
        T_AT = [0, P * QB, 2 * P * QB, P * (2 * QB - 1)]

        const_in, vec_in, rope_in = sem("const_in"), sem("vec_in"), sem("rope_in")
        X_PARTS = 4
        x_in = [sem(f"x_in{i}") for i in range(X_PARTS)]
        w_in = [sem("w_in0"), sem("w_in1")]
        w_hi_done, w_lo_done = sem("w_hi_done"), sem("w_lo_done")
        ws_hi_done, ws_lo_done = sem("ws_hi_done"), sem("ws_lo_done")
        mm_done, acc_free = sem("mm_done"), sem("acc_free")
        prep_hi, prep_lo = sem("prep_hi"), sem("prep_lo")
        norm_sum, norm_std, norm_rstd = sem("norm_sum"), sem("norm_std"), sem("norm_rstd")
        norm_row, rstd_set = sem("norm_row"), sem("rstd_set")
        f_mm, f_abs, f_ln, f_cum = (sem(n) for n in ("f_mm", "f_abs", "f_ln", "f_cum"))
        crow_out, ones_set = sem("crow_out"), sem("ones_set")
        crow_in = [sem("crow_in0"), sem("crow_in1")]
        s_ready, row_min, p_exp, p_ready = (sem(n) for n in ("s_ready", "row_min", "p_exp", "p_ready"))
        t_ready, t_free, pv_done, ctx_hi, ctx_lo = (
            sem(n) for n in ("t_ready", "t_free", "pv_done", "ctx_hi", "ctx_lo"))
        sq_hi, hid_lo = sem("sq_hi"), sem("hid_lo")
        ada_in = [sem("ada_in0"), sem("ada_in1")]
        ada_cin, ada_silu, ada_done = sem("ada_cin"), sem("ada_silu"), sem("ada_done")
        kr_mm, kr_done = sem("kr_mm"), sem("kr_done")
        ff_sq = sem("ff_sq")
        dve_step = sem("dve_step")
        x_done = sem("x_done")
        start_sq, start_sum = sem("start_sq"), sem("start_sum")
        out_done = sem("out_done")
        const2_in, pads_set = sem("const2_in"), sem("pads_set")
        y_normed = sem("y_normed")
        both_sum, cm_sq, cm_added = sem("both_sum"), sem("cm_sq"), sem("cm_added")
        mod_ready, h_tmp, h_hi, h_lo = (sem(n) for n in ("mod_ready", "h_tmp", "h_hi", "h_lo"))
        mix_free, rows_in = sem("mix_free"), sem("rows_in")
        pad_ready, conv_done = sem("pad_ready"), sem("conv_done")
        ln_mean, ln_dev, ln_sq, ln_var, ln_std, ln_out, ln_act, ln_hi, ln_lo = (
            sem(n) for n in ("ln_mean", "ln_dev", "ln_sq", "ln_var", "ln_std", "ln_out", "ln_act", "ln_hi", "ln_lo"))
        sc_out, sc_hi, sc_lo = sem("sc_out"), sem("sc_hi"), sem("sc_lo")
        row_abs, row_ln, row_u_done, row_max, row_floor, row_em = (
            sem(n) for n in ("row_abs", "row_ln", "row_u_done", "row_max", "row_floor", "row_em"))
        u_turned, u_read, v_turned, v_read = (sem(n) for n in ("u_turned", "u_read", "v_turned", "v_read"))
        d_ready, w_exp, qk_ready, a_ready, head_ctx, floor_ready = (
            sem(n) for n in ("d_ready", "w_exp", "qk_ready", "a_ready", "head_ctx", "floor_ready"))
        den_abs, head_h, head_sq, head_sum, head_std, head_out, head_hi, head_lo = (
            sem(n) for n in ("den_abs", "head_h", "head_sq", "head_sum", "head_std", "head_out", "head_hi", "head_lo"))
        gz_ready, gz_abs, gz_ln, gz_sum, g_exp, g_scaled = (
            sem(n) for n in ("gz_ready", "gz_abs", "gz_ln", "gz_sum", "g_exp", "g_scaled"))
        gw_set, gs_ready, gs_read, kd_turned, kd_read = (
            sem(n) for n in ("gw_set", "gs_ready", "gs_read", "kd_turned", "kd_read"))
        gu_ready, gu_read, g_state, g_out = (sem(n) for n in ("gu_ready", "gu_read", "g_state", "g_out"))
        gate_early, gate_done, branch_read, merge_out, merge_hi, merge_lo = (
            sem(n) for n in ("gate_early", "gate_done", "branch_read", "merge_out", "merge_hi", "merge_lo"))
        tap_last, hid_silu, hid_out, hid_hi = (sem(n) for n in ("tap_last", "hid_silu", "hid_out", "hid_hi"))
        N_CONST = 3
        N_CONST2 = 6

        TILES = {name: n for name, n in RUNS}
        TILES["mla"], TILES["merge"] = 4 * MLA_HEADS, 2 * BRANCHES * KT
        TILE0, before = {}, 0
        for name, _ in RUNS:
            TILE0[name] = before
            before += TILES[name]
        FREE0 = dict(TILE0, w_o=TILE0["mix_in"], ffn2=TILE0["mix_in"] + KT)
        HEAD0 = {"fox": 0, "mla": FOX_HEADS}
        CTX0 = {"fox": 0, "mla": FOX_PAIRS}
        T0_MLA = 7 * FOX_PAIRS
        PREP0 = {"fox": 0, "ff_a": KT, "mla": 2 * KT, "cq": 3 * KT, "ckv": 3 * KT + QKT,
                 "ff_b": 3 * KT + KVKT + QKT}
        PREP0["final"] = PREP0["ff_b"] + KT
        PREP0["mix_y"] = PREP0["final"] + KT
        PREP0["ffn_y"] = PREP0["mix_y"] + KT
        NORM = {"fox": 0, "ff_a": 1, "mla": 2, "cq": 3, "ckv": 4, "ff_b": 5, "x2": 6,
                "final": 7, "mix_y": 8, "cm": 9, "ffn_y": 10}
        BY_TOKEN = ("x2", "mix_y", "ffn_y")
        HID0 = {"ff_a": 0, "ff_b": FF_CHUNKS * KT, "ffn2": 2 * FF_CHUNKS * KT}
        HID_AT = [sum(FFN2_CHUNKS[:c]) for c in range(len(FFN2_CHUNKS))]
        FFN2_STEPS, first = [], 0
        for what, c in FFN2_ORDER:
            FFN2_STEPS.append((what, c, first))
            first += 2 * FFN2_CHUNKS[c] if what == "u" else KT

        wflat = d["wstream"]

        block = ctx.enter_context(nc.Block())

        def load_x(eng, i):
            w = KT * T // X_PARTS
            eng.dma_start(x[:].rearrange("p k t -> p (k t)")[:, i * w:(i + 1) * w], d["xT"][:, i * w:(i + 1) * w])\
               .then_inc(x_in[i], 16)

        @block.sync
        def _(sp):
            sp.dma_start(vec[:], d["vecs"]).then_inc(vec_in, 16)

            def load(slot, g, at, width):
                if not (isinstance(g, int) and g < 2):
                    sp.wait_ge(w_lo_done, g - 1)
                src = wflat[bass.ds(at, P * width)].rearrange("(p c) -> p c", p=P)
                sp.dma_start(w_raw[slot][:, 0:width], src).then_inc(w_in[slot], 16)

            load(0, 0, 0, PANEL)
            sp.dma_start(ws_raw, d["wsmall"]).then_inc(const_in, 16)
            load(1, 1, P * PANEL, PANEL)
            sp.dma_start(ident[:], d["ident"]).then_inc(const_in, 16)
            sp.dma_start(mask_q[:], d["mask_q"]).then_inc(const_in, 16)

            def load_run(first, n):
                assert first % 2 == 0 and n % 2 == 0
                with sp.Fori(first // 2, (first + n) // 2) as half:
                    for s in range(2):
                        load(s, 2 * half + s, (2 * half + s) * (P * PANEL), PANEL)

            n_ada, ada0 = 6 * KT, PANEL0["ff_a"] + KT
            load_run(2, ada0 - 2)
            sp.wait_ge(s_ready, 3 * FOX_HEADS)
            with sp.Fori(0, n_ada // 2) as half:
                for s in range(2):
                    load(s, 2 * half + (ada0 + s), (2 * half + (ada0 + s)) * (P * PANEL), PANEL)
                    sp.wait_ge(ada_done, 2 * half + s)
                    sp.dma_start(ada_w[s], d["ada"][bass.ds((2 * half + s) * P, P), :]).then_inc(ada_in[s], 16)
            load_run(ada0 + n_ada, PANEL0["mla"] - ada0 - n_ada)
            base = PANEL0["mla"] * P * PANEL
            with sp.Fori(0, MLA_HEADS) as h:
                load(0, 2 * h + PANEL0["mla"], h * (P * (Q_COLS + KV_COLS)) + base, Q_COLS)
                load(1, 2 * h + (PANEL0["mla"] + 1), h * (P * (Q_COLS + KV_COLS)) + (base + P * Q_COLS), KV_COLS)
            base += MLA_HEADS * P * (Q_COLS + KV_COLS)
            with sp.Fori(0, (PANEL0["mix_in"] - PANEL0["mla_out"]) // 2) as half:
                for s in range(2):
                    load(s, 2 * half + (PANEL0["mla_out"] + s), (2 * half + s) * (P * PANEL) + base, PANEL)
            base += (PANEL0["mix_in"] - PANEL0["mla_out"]) * P * PANEL
            for s in range(2):
                load(s, PANEL0["mix_in"] + s, base + s * (P * PANEL // 2), PANEL // 2)
            base += P * PANEL
            first, last = PANEL0["mix_in"] + 2, N_PANELS - KT
            with sp.Fori(0, (last - first) // 2) as half:
                for s in range(2):
                    load(s, 2 * half + (first + s), (2 * half + s) * (P * PANEL) + base, PANEL)
            base += (last - first) * P * PANEL
            width = FFN2_CHUNKS[-1] * P
            with sp.Fori(0, KT // 2) as half:
                for s in range(2):
                    load(s, 2 * half + (last + s), (2 * half + s) * (P * width) + base, width)
            with sp.Fori(0, KT) as k:
                sp.wait_ge(x_done, k + (2 * KT + 1))
                sp.dma_start(out[:, bass.ds(k * T, T)], x[:, bass.ds(k, 1), :].rearrange("p a t -> p (a t)"))\
                  .then_inc(out_done, 16)
            sp.wait_ge(out_done, 16 * KT)

        @block.gpsimd
        def _(pool):
            pool.memset(fz[1], 1.0).then_inc(ones_set, 1)
            pool.memset(ones_sq[:], 1.0).then_inc(ones_set, 1)
            pool.wait_ge(ones_set, 2)
            pool.dma_start(crow[:, 1, :], fz[1]).then_inc(crow_out, 16)
            pool.dma_start(crow[:, 2, :], fz[1]).then_inc(crow_out, 16)
            pool.wait_ge(f_cum, 1)
            pool.dma_start(crow[:, 3, :], fz[2]).then_inc(crow_out, 16)
            pool.wait_ge(f_cum, 2)
            pool.dma_start(crow[:, 0, :], fz[0]).then_inc(crow_out, 16)
            pool.wait_ge(crow_out, 64)

            def rows(p, m):
                for at, tiles in ((0, QA_AT), (2, KA_AT)):
                    src = crow[bass.ds(2 * p, 2), at:at + 2, :].rearrange("a r t -> r a t")
                    pool.dma_start(arena[FOX_DH:FOX_DH + 2, tiles + 2 * m:tiles + 2 * m + 2, :], src).then_inc(crow_in[m], 16)

            rows(0, 0)
            rows(1, 1)
            with pool.Fori(1, FOX_PAIRS // 2) as pp:
                for m in range(2):
                    pool.wait_ge(s_ready, 12 * pp + (6 * m - 6))
                    rows(2 * pp + m, m)
            pool.wait_ge(ctx_lo, FOX_PAIRS)
            pool.dma_start(ada_c, d["cvec"].to_broadcast([P, D])).then_inc(ada_cin, 16)
            pool.wait_ge(ada_done, 6 * KT)
            pool.dma_start(rope, d["rope"]).then_inc(rope_in, 16)
            pool.dma_start(fold_t[:, 0:P], d["fold"]).then_inc(rope_in, 16)

            pool.wait_ge(hid_lo, HID0["ffn2"])
            for dst, name in ((halves, "halves"), (mask_low[:], "mask_low"), (gla_a2, "gla_a2"), (chunk_start, "chunk_start"),
                              (sel, "sel"), (mask_gla[:], "mask_gla")):
                pool.dma_start(dst, d[name]).then_inc(const2_in, 16)
            pool.memset(zeros, 0.0).then_inc(pads_set, 1)
            for i in range(2):
                pool.memset(conf_pad[:, i * CONF_PAD:i * CONF_PAD + CONF_W - 1], 0.0).then_inc(pads_set, 1)
                pool.memset(sc_pad[:, i * SC_PAD:i * SC_PAD + SC_W - 1], 0.0).then_inc(pads_set, 1)
            pool.wait_ge(head_h, 2)
            for w in gla_w:
                pool.memset(w, 0.0).then_inc(gw_set, 1)
            for i in range(2):
                pool.wait_ge(rstd_set, i + 1)
                with pool.Fori(0, KT // 2) as half:
                    y = arena[:, bass.ds(2 * half + (y_at + 1), 1), :].rearrange("p a t -> p (a t)")
                    pool.tensor_tensor(y, y, rstd, ALU.mult).then_inc(y_normed, 1)

        @block.tensor
        def _(pe):
            def products(dst, slot, n, rhs_hi, rhs_lo, at, step, width=P, before_k=None):
                for k in range(n):
                    if before_k is not None:
                        before_k(k)
                    c = at + k * step
                    whi, wlo = w_hi[slot][:, c:c + width], w_lo[slot][:, c:c + width]
                    nc.tensor.matmul(dst, whi, rhs_hi(k), start=(k == 0), stop=False)
                    nc.tensor.matmul(dst, whi, rhs_lo(k), start=False, stop=False)
                    last = nc.tensor.matmul(dst, wlo, rhs_hi(k), start=False, stop=(k == n - 1))
                return last

            def panel_ready(g):
                pe.wait_ge(w_lo_done, g + 1)

            def bank_free(t):
                if not (isinstance(t, int) and t < 2):
                    pe.wait_ge(acc_free, t - 1)

            def tile(g, t, slot, buf, n=KT, before_k=None, free=None):
                panel_ready(g)
                bank_free(t if free is None else free)
                products(acc[slot][:], slot, n, lambda k: b_hi[buf][:, k, :],
                         lambda k: b_lo[buf][:, k, :], 0, P, before_k=before_k).then_inc(mm_done, 1)

            def begin(run, s, buf, k0, k1):
                if k0 == 0:
                    panel_ready(PANEL0[run] + s)
                    bank_free(TILE0[run] + s)
                for k in range(k0, k1):
                    pe.wait_ge(ctx_lo, CTX0["fox" if run == "fox_out" else "mla"] + k + 1)
                    whi, wlo = w_hi[s][:, k * P:(k + 1) * P], w_lo[s][:, k * P:(k + 1) * P]
                    nc.tensor.matmul(acc[s][:], whi, b_hi[buf][:, k, :], start=(k == 0), stop=False, skip_group_check=True)
                    nc.tensor.matmul(acc[s][:], whi, b_lo[buf][:, k, :], start=False, stop=False, skip_group_check=True)
                    last = nc.tensor.matmul(acc[s][:], wlo, b_hi[buf][:, k, :], start=False, stop=(k == KT - 1),
                                            skip_group_check=True)
                if k1 == KT:
                    last.then_inc(mm_done, 1)

            def segment(run, first, n, buf, lead=None, before_k=None, depth=KT, begun=False):
                g0, t0, f0 = PANEL0[run] + first, TILE0[run] + first, FREE0[run] + first
                start = 1 if begun else 0
                if lead is not None or before_k is not None:
                    tile(g0, t0, 0, buf, n=depth, before_k=before_k, free=f0)
                    if lead is not None:
                        lead()
                    tile(g0 + 1, t0 + 1, 1, buf, n=depth, free=f0 + 1)
                    start = 1
                with pe.Fori(start, n // 2) as half:
                    for s in range(2):
                        tile(2 * half + (g0 + s), 2 * half + (t0 + s), s, buf, n=depth, free=2 * half + (f0 + s))

            def ready_k(base):
                return lambda k: pe.wait_ge(prep_lo, base + k + 1)

            def sum_squares(norm, prepared, squares=ssum):
                pe.wait_ge(prep_lo, prepared)
                if norm == "fox":
                    pe.wait_ge(ones_set, 2)
                else:
                    pe.wait_ge(norm_std, NORM[norm])
                    pe.wait_ge(ctx_lo, CTX0["mla"] + (MLA_HEADS if NORM[norm] >= NORM["ff_b"] else 0))
                if norm in BY_TOKEN:
                    sum_by_token(squares).then_inc(norm_sum, 1)
                    rstd_row(norm)
                else:
                    nc.tensor.matmul(c_bank[:], ones_sq[:], squares, start=True, stop=True).then_inc(norm_sum, 1)

            def sum_by_token(squares):
                for blk in range(QB):
                    last = nc.tensor.matmul(c_bank[:, blk:blk + 1], squares[:, P * blk:P * (blk + 1)], ones_sq[:, 0:1],
                                            start=(blk == 0), stop=True, skip_group_check=True)
                return last

            def rstd_row(norm):
                pe.wait_ge(norm_rstd, NORM[norm] + 1)
                for blk in range(QB):
                    last = nc.tensor.matmul(c_bank[:, P * blk:P * (blk + 1)], rstd_col[:, blk:blk + 1].to_broadcast([P, P]),
                                            ident[:], start=(blk == 0), stop=True, skip_group_check=True)
                last.then_inc(norm_row, 1)

            def logits(n, m, h, kind):
                for u, rows in enumerate(((3,), (2,), (1, 0))):
                    if not (isinstance(n, int) and n == 0):
                        pe.wait_ge(p_exp, 3 * n + (u - 2))
                    for qb in rows:
                        w = P * (qb + 1)
                        at = 0 if qb else 2 * P
                        dst = s_bank[u][:, at:at + w]
                        q = slice(P * qb, P * (qb + 1))
                        if kind == "fox":
                            r = FOX_DH + 2
                            nc.tensor.matmul(dst, qa[m][h][0:r, q], ka[m][h][0:r, 0:w], start=(qb != 0), stop=False,
                                             skip_group_check=True)
                        else:
                            nc.tensor.matmul(dst, qa[m][0][:, q], ka[m][0][:, 0:w], start=(qb != 0), stop=False,
                                             skip_group_check=True)
                            nc.tensor.matmul(dst, qa[m][1][:, q], k_rope[:, 0:w], start=False, stop=False,
                                             skip_group_check=True)
                        last = nc.tensor.matmul(s_bank[u][:, at + w - P:at + w], ident_b[:], mask_b[:],
                                                start=False, stop=True, skip_group_check=True)
                    last.then_inc(s_ready, 1)

            def turn_free(c):
                if not (isinstance(c, int) and c < 2):
                    pe.wait_ge(t_free, c - 1)

            def turn_probs(n, m, c, par):
                pe.wait_ge(p_ready, n + 1)
                for u, blocks in enumerate(((0,), (1, 3), (2,))):
                    turn_free(c + u)
                    for kb in blocks:
                        for qb in range(kb, QB):
                            at = T_AT[kb] - T_AT[blocks[0]] + P * (qb - kb)
                            src = probs[m][:, P_AT[qb] + P * kb:P_AT[qb] + P * (kb + 1)]
                            last = nc.tensor.transpose(t_bank[(par + u) % 2][:, at:at + P], src, ident[:])
                    last.then_inc(t_ready, 1)

            def turn_values(t, c, par):
                pe.wait_ge(acc_free, t + 1)
                turn_free(c)
                for kb in range(QB):
                    last = nc.tensor.transpose(t_bank[par][:, P * kb:P * (kb + 1)], v_t[:, P * kb:P * (kb + 1)], ident[:])
                last.then_inc(t_ready, 1)

            def context(n, m, vm, c_end, lo, width, ctx_before):
                pe.wait_ge(t_free, c_end)
                if ctx_before is not None:
                    pe.wait_ge(ctx_lo, ctx_before)
                for kb in range(QB):
                    w = T - P * kb
                    last = nc.tensor.matmul(c_bank[lo:lo + width, P * kb:T],
                                            v_tok[vm][:, P * kb + lo:P * kb + lo + width],
                                            probs_t[m][:, T_AT[kb]:T_AT[kb] + w], start=(kb == 0), stop=(kb == QB - 1))
                last.then_inc(pv_done, 1)

            def fox_tile(g, slot, before_k=None):
                tile(g, g, slot, 0, before_k=before_k)

            def forget_gates():
                pe.wait_ge(const_in, 16 * N_CONST)
                pe.wait_ge(ws_lo_done, 1)
                for k in range(KT):
                    hi, lo = ws_hi[:, k * FOX_HEADS:(k + 1) * FOX_HEADS], ws_lo[:, k * FOX_HEADS:(k + 1) * FOX_HEADS]
                    dst = s_bank[0][0:FOX_HEADS, :]
                    nc.tensor.matmul(dst, hi, b_hi[0][:, k, :], start=(k == 0), stop=False)
                    nc.tensor.matmul(dst, hi, b_lo[0][:, k, :], start=False, stop=False)
                    last = nc.tensor.matmul(dst, lo, b_hi[0][:, k, :], start=False, stop=(k == KT - 1))
                last.then_inc(f_mm, 1)

            def fox_step(pp, m, project=True, attend=True, late=True, start=False):
                p = 2 * pp + m
                c = 7 * p - 6
                par = m
                o = 1 - m
                if project:
                    fox_tile(3 * p, m, ready_k(0) if start else None)
                if start:
                    forget_gates()
                    pe.wait_ge(start_sum, KT)
                    sum_squares("fox", KT)
                if late:
                    context(2 * p - 3, 1, m, c - 1, FOX_DH, FOX_DH, None)
                if attend:
                    pe.wait_ge(crow_in[o], 32 * pp + 32 * m)
                    pe.wait_ge(acc_free, 3 * p - 1)
                    logits(2 * p - 2, o, 0, "fox")
                if project:
                    fox_tile(3 * p + 1, 1 - m)
                if attend:
                    logits(2 * p - 1, o, 1, "fox")
                    turn_probs(2 * p - 2, 0, c, par)
                if project:
                    fox_tile(3 * p + 2, m)
                if attend:
                    context(2 * p - 2, 0, o, c + 3, 0, FOX_DH, None if isinstance(p, int) and p == 1 else p - 1)
                    turn_probs(2 * p - 1, 1, c + 3, 1 - par)
                if project:
                    turn_values(3 * p + 2, 0 if start else c + 6, par if not start else 0)

            fox_step(0, 0, attend=False, late=False, start=True)
            pe.wait_ge(norm_std, 1)
            fox_step(0, 1, late=False)
            with pe.Fori(1, FOX_PAIRS // 2) as pp:
                fox_step(pp, 0)
                fox_step(pp, 1)
            c, last = 7 * FOX_PAIRS - 6, FOX_HEADS - 1
            context(last - 2, 1, 0, c - 1, FOX_DH, FOX_DH, None)
            pe.wait_ge(crow_in[1], 16 * FOX_PAIRS)
            pe.wait_ge(acc_free, 3 * FOX_PAIRS - 1)
            logits(last - 1, 1, 0, "fox")
            logits(last, 1, 1, "fox")
            begin("fox_out", 0, 1, 0, FOX_PAIRS - 2)
            turn_probs(last - 1, 0, c, 0)
            begin("fox_out", 1, 1, 0, FOX_PAIRS - 2)
            context(last - 1, 0, 1, c + 3, 0, FOX_DH, FOX_PAIRS - 1)
            turn_probs(last, 1, c + 3, 1)
            for s in range(2):
                begin("fox_out", s, 1, FOX_PAIRS - 2, FOX_PAIRS - 1)
            context(last, 1, 1, c + 6, FOX_DH, FOX_DH, None)
            for s in range(2):
                begin("fox_out", s, 1, FOX_PAIRS - 1, FOX_PAIRS)
            segment("fox_out", 0, KT, 1, begun=True)

            def ffn(run, buf, hid, norm):
                for i, (what, c) in enumerate(FF_ORDER):
                    if what == "u":
                        segment(run, i * KT, KT, buf,
                                lead=(lambda: sum_squares(norm, PREP0[norm] + KT)) if i == 0 else None,
                                before_k=ready_k(PREP0[norm]) if i == 0 else None)
                    else:
                        first = HID0[run] + c * KT
                        segment(run, i * KT, KT, hid[c % 2],
                                before_k=lambda k, first=first: pe.wait_ge(hid_lo, first + k + 1))

            ffn("ff_a", 0, (1, 2), "ff_a")

            g0, t0 = PANEL0["low"], TILE0["low"]
            tile(g0, t0, 0, 0, before_k=ready_k(PREP0["mla"]))
            sum_squares("mla", PREP0["mla"] + KT)
            for j in range(1, QKT + KVKT + 1):
                tile(g0 + j, t0 + j, j % 2, 0 if j < QKT else 1)
            sum_squares("cq", PREP0["cq"] + QKT)

            def rope_keys():
                pe.wait_ge(acc_free, t0 + QKT + KVKT + 1)
                pe.wait_ge(rope_in, 32)
                nc.tensor.matmul(s_bank[0][:], fold_t[:, 0:P], kr_raw, start=True, stop=True).then_inc(kr_mm, 1)

            def mla_step(h, m, project=True, attend=True, late=True):
                g = 2 * h + PANEL0["mla"]
                t = 4 * h + TILE0["mla"]
                n = h + HEAD0["mla"]
                c = 4 * h + (T0_MLA - 6)
                o = 1 - m
                if project:
                    panel_ready(g)
                    for i, at in enumerate((0, NOPE)):
                        bank_free(t + i)
                        products(acc[i][:], 0, QKT, lambda k: b_hi[2][:, k, :], lambda k: b_lo[2][:, k, :],
                                 at, NOPE + 2 * ROPE).then_inc(mm_done, 1)
                if project and not attend:
                    sum_squares("ckv", PREP0["ckv"] + KVKT, low_sum)
                    rope_keys()
                if late:
                    turn_probs(n - 2, m, c if project or attend else c - 1, (T0_MLA if project or attend else T0_MLA - 1) % 2)
                if attend:
                    pe.wait_ge(acc_free, t - 1)
                    logits(n - 1, o, 0, "mla")
                if project:
                    panel_ready(g + 1)
                    for i, at in enumerate((0, NOPE)):
                        bank_free(t + 2 + i)
                        products(acc[i][:], 1, KVKT, lambda k: b_hi[2][:, QKT + k, :],
                                 lambda k: b_lo[2][:, QKT + k, :], at, NOPE + VDIM).then_inc(mm_done, 1)
                if late:
                    context(n - 2, m, m, (c if project or attend else c - 1) + 3, 0, VDIM, h + (CTX0["mla"] - 2))
                if project:
                    first = not attend
                    turn_values(t + 3, T0_MLA if first else c + 3, (T0_MLA if first else T0_MLA - 3) % 2)

            mla_step(0, 0, attend=False, late=False)
            pe.wait_ge(norm_std, NORM["ckv"] + 1)
            pe.wait_ge(kr_done, 1)
            mla_step(1, 1, late=False)
            with pe.Fori(1, MLA_HEADS // 2) as hh:
                mla_step(2 * hh, 0)
                mla_step(2 * hh + 1, 1)
            n, c = HEAD0["mla"] + MLA_HEADS - 1, T0_MLA + 4 * MLA_HEADS
            turn_probs(n - 1, 0, c - 6, T0_MLA % 2)
            pe.wait_ge(acc_free, TILE0["mla_out"] - 1)
            logits(n, 1, 0, "mla")
            begin("mla_out", 0, 0, 0, MLA_HEADS - 2)
            context(n - 1, 0, 0, c - 3, 0, VDIM, CTX0["mla"] + MLA_HEADS - 2)
            begin("mla_out", 1, 0, 0, MLA_HEADS - 2)
            turn_probs(n, 1, c - 3, (T0_MLA - 1) % 2)
            for s in range(2):
                begin("mla_out", s, 0, MLA_HEADS - 2, MLA_HEADS - 1)
            context(n, 1, 1, c, 0, VDIM, CTX0["mla"] + MLA_HEADS - 1)
            for s in range(2):
                begin("mla_out", s, 0, MLA_HEADS - 1, MLA_HEADS)
            segment("mla_out", 0, KT, 0, begun=True)
            ffn("ff_b", 1, (0, 2), "ff_b")
            pe.wait_ge(both_sum, 1)
            sum_squares("x2", PREP0["final"] + KT, ssum_g)

            g0 = PANEL0["mix_in"]
            for half in range(2):
                panel_ready(g0 + half)
                for k in range(KT // 2):
                    f = half * (KT // 2) + k
                    pe.wait_ge(h_lo, f + 1)
                    whi, wlo = w_hi[half][:, k * P:(k + 1) * P], w_lo[half][:, k * P:(k + 1) * P]
                    nc.tensor.matmul(s_bank[2][:], whi, b_hi[0][:, f, :], start=(f == 0), stop=False)
                    nc.tensor.matmul(s_bank[2][:], whi, b_lo[0][:, f, :], start=False, stop=False)
                    last = nc.tensor.matmul(s_bank[2][:], wlo, b_hi[0][:, f, :], start=False, stop=(f == KT - 1))
                last.then_inc(mm_done, 1)
            sum_squares("final", PREP0["final"] + KT)

            def mix_tile(i, slot):
                panel_ready(i + g0)
                if not (isinstance(i, int) and i < 4):
                    pe.wait_ge(mix_free, i - 3)
                products(acc[slot][:], slot, KT, lambda k: b_hi[0][:, k, :], lambda k: b_lo[0][:, k, :], 0, P)\
                    .then_inc(mm_done, 1)

            for s in range(2):
                mix_tile(2 + s, s)
            with pe.Fori(2, GLA // 2) as half:
                for s in range(2):
                    mix_tile(2 * half + s, s)

            def turn_rows():
                pe.wait_ge(row_u_done, 1)
                for blk in range(QB):
                    last = nc.tensor.transpose(s_bank[2][:, HEADS * blk:HEADS * (blk + 1)], row_u[:, P * blk:P * (blk + 1)],
                                               ident[0:HEADS, 0:HEADS])
                last.then_inc(u_turned, 1)

            def turn_mixed(read, src, dst):
                pe.wait_ge(mix_free, read)
                for v, to in zip(src, dst):
                    for blk in range(QB):
                        c = slice(P * blk, P * (blk + 1))
                        last = nc.tensor.transpose(to[:, c], v[:, c], ident[:])
                    last.then_inc(v_turned, 1)

            def feature_sum(src, ready, count, done):
                pe.wait_ge(ready, count)
                for i in range(2):
                    last = nc.tensor.matmul(c_bank[:], ones_sq[:], src[i], start=(i == 0), stop=(i == 1))
                last.then_inc(done, 1)

            def log_weights(h):
                if h:
                    pe.wait_ge(w_exp, h)
                else:
                    pe.wait_ge(row_max, 1)
                    pe.wait_ge(const2_in, 16 * N_CONST2)
                nc.tensor.matmul(s_bank[0][:], sel[:, P * h:P * (h + 1)], row_z, start=True, stop=True).then_inc(d_ready, 1)

            def key_queries(h):
                c, rows = h // 2, slice(DH * (h % 2), DH * (h % 2 + 1))
                if h:
                    pe.wait_ge(a_ready, h)
                else:
                    pe.wait_ge(u_read, 1)
                    pe.wait_ge(v_read, 2)
                for blk, (dst, at) in enumerate(((t_bank[0], 0), (t_bank[1], 0), (s_bank[2], 0), (t_bank[1], T - P))):
                    last = nc.tensor.matmul(dst[:, at:at + T - P * blk], ml_k[c][rows, P * blk:P * (blk + 1)],
                                            ml_q[c][rows, P * blk:T], start=(blk < 3), stop=True, skip_group_check=True)
                last.then_inc(qk_ready, 1)

            def head_sums(h):
                c, m, rows = h // 2, h % 2, slice(DH * (h % 2), DH * (h % 2 + 1))
                pe.wait_ge(a_ready, h + 1)
                if h == 0:
                    pe.wait_ge(ln_std, 1)
                if h == 2:
                    pe.wait_ge(head_h, 1)
                for dst in (c_bank, s_bank[1]):
                    for blk in range(QB):
                        lhs = ml_vt[c][:, P * blk + DH * m:P * blk + DH * (m + 1)] if dst is c_bank else ones_sq[:, 0:DH]
                        last = nc.tensor.matmul(dst[rows, P * blk:T], lhs, ml_w[m][:, T_AT[blk]:T_AT[blk] + T - P * blk],
                                                start=(blk == 0), stop=(blk == QB - 1), skip_group_check=True)
                last.then_inc(head_ctx, 1)

            def floors(c):
                pe.wait_ge(den_abs, c + 1)
                pe.wait_ge(row_em, 1)
                at = 2 * c * P + DH
                nc.tensor.matmul(s_bank[1][:], sel[:, at:at + P], row_b, start=True, stop=True).then_inc(floor_ready, 1)

            def head_squares(i, src, dst):
                pe.wait_ge(head_sq, i + 1)
                nc.tensor.matmul(dst[:], halves[:], src, start=True, stop=True).then_inc(head_sum, 1)

            mix_tile(GLA, 0)
            turn_rows()
            turn_mixed(ML + 4, ml_v, t_bank)
            feature_sum(conf_u, conv_done, 4, ln_mean)
            mix_tile(GLA + 1, 1)
            feature_sum(ml_v, ln_sq, 2, ln_var)
            log_weights(0)
            key_queries(0)
            mix_tile(GLA + 2, 0)
            log_weights(1)
            head_sums(0)
            key_queries(1)
            mix_tile(GLA + 3, 1)
            log_weights(2)
            head_sums(1)
            key_queries(2)
            mix_tile(GLA + 4, 0)
            floors(0)
            log_weights(3)
            mix_tile(GLA + 5, 1)
            head_sums(2)
            key_queries(3)
            mix_tile(GLA + 6, 0)
            pe.wait_ge(w_exp, HEADS)
            head_squares(0, ml_s, s_bank[0])
            head_sums(3)
            for c in range(2):
                nc.tensor.matmul(t_bank[c][:], gla_a2[:, P * c:P * (c + 1)], gla_a, start=True, stop=True)\
                  .then_inc(gz_ready, 1)
            floors(1)
            mix_tile(GLA + 7, 1)

            g0, t0 = PANEL0["merge"], TILE0["merge"]

            def gate_tile(j, m, b):
                panel_ready(5 * j + (g0 + b))
                if not (isinstance(j, int) and j == 0):
                    pe.wait_ge(gate_done, 4 * j + (b - 3))
                elif b == 3:
                    pe.wait_ge(head_h, 4)
                elif b == 0:
                    pe.wait_ge(head_std, 1)
                else:
                    pe.wait_ge(gu_read, 2)
                products(gate_bank[b][:], (m + b) % 2, KT, lambda k: b_hi[0][:, k, :], lambda k: b_lo[0][:, k, :], 0, P)\
                    .then_inc(mm_done, 1)

            gate_tile(0, 0, 0)

            turn_mixed(GLA + 6, gla_v, acc)

            def chunk_weights(c):
                pe.wait_ge(g_scaled, c + 1)
                if c == 0:
                    pe.wait_ge(gz_abs, 2)
                else:
                    pe.wait_ge(gs_read, c)
                for m in range(2):
                    rows = slice(DH * m, DH * (m + 1))
                    for blk in range(QB):
                        w = slice(P * blk, P * (blk + 1))
                        last = nc.tensor.matmul(t_bank[m][:, w], gla_e[c][1][rows, w], gla_e[c][0][rows, w],
                                                start=(blk == 0), stop=True, skip_group_check=True)
                last.then_inc(gs_ready, 1)

            def turn_keys(c):
                if c:
                    pe.wait_ge(gu_read, c)
                for blk in range(QB):
                    w = slice(P * blk, P * (blk + 1))
                    last = nc.tensor.transpose(s_bank[2][:, w], gla_e[c][3][:, w], ident[:])
                last.then_inc(kd_turned, 1)

            def chunk_states(c):
                pe.wait_ge(kd_read, c + 1)
                for i in range(P // GLA_CHUNK):
                    if u_bank[i] is s_bank[1] and c == 0:
                        pe.wait_ge(head_h, 2)
                    rows = slice(GLA_CHUNK * i, GLA_CHUNK * (i + 1))
                    for blk in range(QB):
                        w = slice(P * blk, P * (blk + 1))
                        last = nc.tensor.matmul(u_bank[i][:, w], gla_b[c][rows, w], gla_vt[c][rows, w],
                                                start=(blk == 0), stop=True, skip_group_check=True,
                                                tile_position=(GLA_CHUNK * i, 0))
                    last.then_inc(gu_ready, 1)

            def chunk_outputs(c):
                pe.wait_ge(gs_read, c + 1)
                pe.wait_ge(g_state, c + 1)
                if c:
                    pe.wait_ge(head_h, 2 + c)
                for m in range(2):
                    rows = slice(DH * m, DH * (m + 1))
                    for blk in range(QB):
                        w = slice(P * blk, P * (blk + 1))
                        nc.tensor.matmul(c_bank[rows, w], gla_vt[c][:, P * blk + DH * m:P * blk + DH * (m + 1)],
                                         gla_w[m][:, w], start=(blk == 0), stop=False, skip_group_check=True)
                    state = gla_s[c][rows, :].rearrange("p (e n) -> p n e", n=CHUNKS)
                    for i in range(1, CHUNKS):
                        w = slice(GLA_CHUNK * i, GLA_CHUNK * (i + 1))
                        last = nc.tensor.matmul(c_bank[rows, w], state[:, i - 1, :], gla_e[c][2][rows, w], start=False,
                                                stop=(i == CHUNKS - 1), skip_group_check=True)
                last.then_inc(g_out, 1)

            chunk_weights(0)
            turn_keys(0)
            chunk_states(0)
            head_squares(1, ml_s, acc[1])
            chunk_weights(1)
            turn_keys(1)
            chunk_outputs(0)
            head_squares(2, gla_e[0][0], acc[1])
            chunk_states(1)

            gate_tile(0, 0, 1)
            chunk_outputs(1)
            head_squares(3, gla_e[1][0], acc[1])

            pe.wait_ge(ln_lo, 2)
            pe.wait_ge(sc_lo, 2)

            def merge_tile(j, m):
                for b in range(2 if isinstance(j, int) and j == 0 else 0, BRANCHES):
                    gate_tile(j, m, b)
                panel_ready(5 * j + (g0 + 4))
                for b in range(BRANCHES):
                    if isinstance(j, int) and j == 0:
                        if b == 0:
                            pe.wait_ge(head_lo, 4)
                    if not (isinstance(j, int) and j == 0):
                        pe.wait_ge(branch_read, 4 * j + (b - 3))
                    products(branch_bank[b][:], m, 2, lambda k: b_hi[1][:, 2 * b + k, :], lambda k: b_lo[1][:, 2 * b + k, :],
                             2 * b * P, P).then_inc(mm_done, 1)

            merge_tile(0, 0)
            merge_tile(1, 1)
            with pe.Fori(1, KT // 2) as jj:
                merge_tile(2 * jj, 0)
                merge_tile(2 * jj + 1, 1)

            pe.wait_ge(branch_read, BRANCHES * (KT - 1) + 1)
            segment("w_o", 0, KT, 2, before_k=lambda k: pe.wait_ge(merge_lo, k + 1))
            sum_squares("mix_y", PREP0["mix_y"] + KT)
            pe.wait_ge(norm_std, NORM["cm"])
            for k in range(KT):
                pe.wait_ge(cm_sq, k + 1)
                last = nc.tensor.matmul(c_bank[:], ones_sq[:], sq[k % 2], start=(k == 0), stop=(k == KT - 1))
                last.then_inc(cm_added if k < KT - 1 else norm_sum, 1)

            for what, c, first in FFN2_STEPS:
                n, at = FFN2_CHUNKS[c], HID0["ffn2"] + HID_AT[c]
                if what == "u":
                    segment("ffn2", first, 2 * n, 0,
                            before_k=(lambda k: pe.wait_ge(h_lo, KT + k + 1)) if c == 0 else None)
                else:
                    segment("ffn2", first, KT, 1 + c % 2, depth=n,
                            before_k=lambda k, at=at: pe.wait_ge(hid_lo, at + k + 1))
            sum_squares("ffn_y", PREP0["ffn_y"] + KT)

        @block.scalar
        def _(act):
            def split(half, slot, width, used):
                act.wait_ge(w_in[slot], 16 * half + 16)
                if used is not None:
                    act.wait_ge(mm_done, used)
                nc.scalar.activation(w_hi[slot][:, 0:width], w_raw[slot][:, 0:width], ACT.Copy).then_inc(w_hi_done, 1)

            def segment(run, first, n, mid, before0, before1, before2=None, fresh=0, width=PANEL, last=1):
                half0, t0 = (PANEL0[run] + first) // 2, TILE0[run] + first
                if fresh < 1:
                    split(half0, 0, width, t0 - last)
                before0()
                if fresh < 2:
                    split(half0, 1, width, t0)
                before1()
                start = 1
                if before2 is not None:
                    split(half0 + 1, 0, width, t0 + 1)
                    before2()
                    mid(0, 0)
                    mid(1, 1)
                    split(half0 + 1, 1, width, t0 + 2)
                    mid(2, 0)
                    start = 2
                else:
                    mid(0, 0)
                with act.Fori(start, n // 2) as half:
                    split(half + half0, 0, width, 2 * half + (t0 - 1))
                    mid(2 * half - 1, 1)
                    split(half + half0, 1, width, 2 * half + t0)
                    mid(2 * half, 0)

            def nothing(*_):
                pass

            def prepare(np, src, tile_free, k, s, gain, dst):
                if tile_free is not None:
                    act.wait_ge(acc_free, tile_free)
                if not (isinstance(np, int) and np < 2):
                    act.wait_ge(prep_lo, np - 1)
                for buf, at, g in zip(dst[0], dst[1], gain):
                    g_col = vec[:, bass.ds(k + VEC[g], 1)]
                    act.activation(b_hi[buf][:, bass.ds(k + at, 1), :].rearrange("p a t -> p (a t)"), src, ACT.Copy,
                                   scale=g_col)
                act.activation(sq[s], src, ACT.Square).then_inc(prep_hi, 1)

            def x_tile(k):
                return x[:, bass.ds(k, 1), :].rearrange("p a t -> p (a t)")

            def prepare_x(norm, t0, gain, dst):
                return lambda j, s: prepare(j + PREP0[norm], x_tile(j), j + (t0 + 1), j, s, gain, dst)

            def root(norm, width, bias=eps):
                if NORM[norm]:
                    act.wait_ge(norm_rstd, NORM[norm])
                act.wait_ge(norm_sum, NORM[norm] + 1)
                dst, src = (std_col, c_bank[:, 0:QB]) if norm in BY_TOKEN else (std, c_bank[:])
                act.activation(dst, src, ACT.Sqrt, bias=bias, scale=1.0 / width).then_inc(norm_std, 1)

            def ready_root():
                act.activation(small[:, 63:64], eps, ACT.Sqrt)

            for i in range(X_PARTS):
                load_x(act, i)
            act.wait_ge(ones_set, 2)
            act.activation(small[:, 63:64], ones_sq[:, 0:1], ACT.Sqrt)
            act.wait_ge(vec_in, 16)
            for k in range(KT):
                if k % (KT // X_PARTS) == 0:
                    act.wait_ge(x_in[k // (KT // X_PARTS)], 16)
                act.activation(b_hi[0][:, k, :], x[:, k, :], ACT.Copy, scale=col("mix_g0", k)).then_inc(prep_hi, 1)
                if k == 1:
                    split(0, 0, PANEL, None)
            act.wait_ge(const_in, 16 * N_CONST)
            act.activation(ws_hi, ws_raw, ACT.Copy).then_inc(ws_hi_done, 1)
            for k in range(KT):
                if k >= 2:
                    act.wait_ge(start_sum, k - 1)
                act.activation(sq[k % 2], x[:, k, :], ACT.Square).then_inc(start_sq, 1)
                if k == 3:
                    split(0, 1, PANEL, None)
            split(1, 0, PANEL, 1)
            root("fox", D)

            def exponentials(n, m):
                for u, rows in enumerate(((3,), (2,), (1, 0))):
                    act.wait_ge(row_min, 3 * n + (u + 1))
                    for qb in rows:
                        w = P * (qb + 1)
                        at = 0 if qb else 2 * P
                        c = 4 * m + qb
                        last = act.activation(probs[m][:, P_AT[qb]:P_AT[qb] + w], s_bank[u][:, at:at + w], ACT.Exp,
                                              bias=rmin[:, c:c + 1], scale=-1.0, accum_out=rsum[:, c:c + 1])
                    last.then_inc(p_exp, 1)

            def read_probs(n, m, c, par):
                if not (isinstance(n, int) and n < 2):
                    act.wait_ge(pv_done, n - 1)
                for u, (at, w) in enumerate(((0, T), (T, T), (2 * T, T // 2))):
                    act.wait_ge(t_ready, c + (u + 1))
                    act.activation(probs_t[m][:, at:at + w], t_bank[(par + u) % 2][:, 0:w], ACT.Copy).then_inc(t_free, 1)

            def read_values(m, c, par):
                act.wait_ge(t_ready, c + 1)
                act.activation(v_tok[m], t_bank[par][:], ACT.Copy).then_inc(t_free, 1)

            def read_context(heads, buf, k):
                act.wait_ge(pv_done, heads)
                act.activation(b_hi[buf][:, bass.ds(k, 1), :].rearrange("p a t -> p (a t)"), c_bank[:], ACT.Copy)\
                   .then_inc(ctx_hi, 1)

            def fox_step(pp, m, project=True, attend=True, late=True):
                p = 2 * pp + m
                c = 7 * p - 6

                def split_next(i):
                    split(3 * pp + (3 * m + i) // 2, (m + i) % 2, PANEL,
                          3 * p + (i - 1))

                if project and attend:
                    split_next(1)
                if not attend:
                    split_next(3)
                    act.wait_ge(f_abs, 1)
                    act.activation(fz[0], fz[3], ACT.Exp, scale=-1.0).then_inc(f_ln, 1)
                    act.wait_ge(f_ln, 1)
                    act.activation(fz[3], fz[0], ACT.Ln, bias=col("one")[0:FOX_HEADS, :]).then_inc(f_ln, 1)
                if late:
                    read_context(2 * p - 2, 1, p - 2)
                if attend:
                    exponentials(2 * p - 2, 0)
                if project and attend:
                    split_next(2)
                if attend:
                    read_probs(2 * p - 2, 0, c, m)
                    exponentials(2 * p - 1, 1)
                if project and attend:
                    split_next(3)
                if attend:
                    read_probs(2 * p - 1, 1, c + 3, 1 - m)
                if project:
                    read_values(m, c + 6 if attend else 0, m)

            fox_step(0, 0, attend=False, late=False)
            fox_step(0, 1, late=False)
            with act.Fori(1, FOX_PAIRS // 2) as pp:
                fox_step(pp, 0)
                fox_step(pp, 1)
            split(PANEL0["fox_out"] // 2, 1, PANEL, TILE0["fox_out"])
            fox_step(FOX_PAIRS // 2, 0, project=False)

            out_a = prepare_x("ff_a", TILE0["fox_out"], ("ff_g0",), ((0,), (0,)))
            segment("fox_out", 0, KT, out_a, nothing, lambda: read_context(2 * FOX_PAIRS, 1, FOX_PAIRS - 1), ready_root,
                    fresh=2)

            def ffn(run, hid, before, norm, last_mid):
                for i, (what, c) in enumerate(FF_ORDER):
                    t0 = TILE0[run] + i * KT

                    def square(j, s, t0=t0, c=c):
                        n = j + (HID0[run] + c * KT)
                        act.wait_ge(acc_free, j + (t0 + 1))
                        if not (isinstance(n, int) and n < 2):
                            act.wait_ge(hid_lo, n - 1)
                        act.activation(ff_s[s], ff_t[s], ACT.Square).then_inc(ff_sq, 1)
                        act.wait_ge(ff_sq, n + 1)
                        act.activation(b_hi[hid[c % 2]][:, bass.ds(j, 1), :].rearrange("p a t -> p (a t)"), ff_s[s],
                                       ACT.Copy).then_inc(sq_hi, 1)

                    mid = square if what == "u" else last_mid if c == FF_CHUNKS - 1 else nothing
                    if i == 0:
                        segment(run, i * KT, KT, mid, lambda: before(KT - 1, 1), nothing, lambda: start(norm))
                    else:
                        segment(run, i * KT, KT, mid, lambda: before(KT - 1, 1), nothing)
                    before = mid
                return before

            def start(norm):
                root(norm, D)
                if norm == "ff_a":
                    act.wait_ge(ada_cin, 16)
                    act.activation(ada_c, ada_c, ACT.Silu).then_inc(ada_silu, 1)
                    ready_root()

            last_a = prepare_x("mla", TILE0["ff_a"] + 7 * KT, ("mix_g1", "kv_g"), ((0, 1), (0, 0)))
            before = ffn("ff_a", (1, 2), out_a, "ff_a", last_a)

            half0, t0 = PANEL0["low"] // 2, TILE0["low"]
            split(half0, 0, PANEL, t0 - 1)
            before(KT - 1, 1)
            split(half0, 1, PANEL, t0)
            split(half0 + 1, 0, PANEL, t0 + 1)
            root("mla", D)

            def prepare_low(norm, n, at, tile0):
                for j in range(n):
                    prepare(PREP0[norm] + j, low[at + j], t0 + tile0 + j + 1, j, (PREP0[norm] + j) % 2,
                            ("kva_g" if norm == "ckv" else "qa_g",), ((2,), (at,)))

            split(half0 + 1, 1, PANEL, t0 + 2)
            split(half0 + 2, 0, PANEL, t0 + 3)
            prepare_low("cq", QKT, 0, 0)
            split(half0 + 2, 1, PANEL, t0 + 4)
            prepare_low("ckv", KVKT, QKT, QKT)
            split(PANEL0["mla"] // 2, 0, Q_COLS, t0 + 5)
            root("cq", Q_RANK)
            split(PANEL0["mla"] // 2, 1, KV_COLS, t0 + 6)
            root("ckv", KV_RANK)

            def mla_step(hh, m, project=True, attend=True, late=True, ahead=True):
                h = 2 * hh + m
                n = h + HEAD0["mla"]
                c = 4 * h + (T0_MLA - 6)
                o = 1 - m
                if late:
                    read_probs(n - 2, m, c if project or attend else c - 1,
                               (T0_MLA if project or attend else T0_MLA - 1) % 2)
                if attend:
                    exponentials(n - 1, o)
                if ahead:
                    split(h + (PANEL0["mla"] // 2 + 1), 0, Q_COLS, 4 * h + (TILE0["mla"] + 2))
                    split(h + (PANEL0["mla"] // 2 + 1), 1, KV_COLS, 4 * h + (TILE0["mla"] + 4))
                if late:
                    read_context(n - 1, 0, h - 2)
                if project:
                    read_values(m, c + 3 if attend else T0_MLA, (T0_MLA - 3) % 2 if attend else T0_MLA % 2)

            mla_step(0, 0, attend=False, late=False)
            mla_step(0, 1, late=False)
            with act.Fori(1, MLA_HEADS // 2 - 1) as hh:
                mla_step(hh, 0)
                mla_step(hh, 1)
            mla_step(MLA_HEADS // 2 - 1, 0)
            mla_step(MLA_HEADS // 2 - 1, 1, ahead=False)
            split(PANEL0["mla_out"] // 2, 0, PANEL, TILE0["mla_out"] - 2)
            split(PANEL0["mla_out"] // 2, 1, PANEL, TILE0["mla_out"])
            mla_step(MLA_HEADS // 2, 0, project=False, ahead=False)
            read_probs(HEAD0["mla"] + MLA_HEADS - 1, 1, T0_MLA + 4 * MLA_HEADS - 3, (T0_MLA - 1) % 2)

            out_b = prepare_x("ff_b", TILE0["mla_out"], ("ff_g1",), ((1,), (0,)))
            segment("mla_out", 0, KT, out_b, nothing,
                    lambda: read_context(HEAD0["mla"] + MLA_HEADS, 0, MLA_HEADS - 1), ready_root, fresh=2)

            def squares_of(norm, src, ready, count):
                def mid(j, s):
                    act.wait_ge(prep_lo, j + (PREP0[norm] - 1))
                    act.wait_ge(ready, j + (count + 1))
                    act.activation(sq[s], src(j), ACT.Square).then_inc(prep_hi, 1)
                return mid

            def y_tile(j):
                return arena[:, bass.ds(j + y_at, 1), :].rearrange("p a t -> p (a t)")

            def last_b(j, s):
                act.wait_ge(prep_lo, j + (PREP0["final"] - 1))
                act.wait_ge(acc_free, j + (TILE0["ff_b"] + 7 * KT + 1))
                act.activation(sq_g[s], x_tile(j), ACT.Square, scale=vec[:, bass.ds(j + VEC["final_g"], 1)])
                act.activation(sq[s], x_tile(j), ACT.Square).then_inc(prep_hi, 1)

            before = ffn("ff_b", (0, 2), out_b, "ff_b", last_b)
            before(KT - 1, 1)
            half0, t0 = PANEL0["mix_in"] // 2, TILE0["mix_in"]
            for s in range(2):
                split(half0, s, PANEL // 2, t0 - 1 + s)
            root("x2", D, col("eps2"))

            act.wait_ge(mod_ready, 1)

            def modulate(n0, shift, scale):
                for k in range(KT):
                    act.wait_ge(h_tmp, n0 + k + 1)
                    if n0 + k >= 4:
                        act.wait_ge(h_lo, n0 + k - 3)
                    by = dict(bias=mod[:, shift * KT + k:shift * KT + k + 1], scale=mod[:, scale * KT + k:scale * KT + k + 1])
                    act.activation(b_hi[0][:, k, :], mod_t[k % 4], ACT.Identity, **by)
                    act.activation(mod_y[k % 4], mod_t[k % 4], ACT.Identity, **by).then_inc(h_hi, 1)

            modulate(0, 0, 1)
            root("final", D)

            def read(i, dst, func, scale=1.0):
                act.wait_ge(mm_done, t0 + i + 1)
                act.activation(dst, acc[i % 2][:], func, scale=scale).then_inc(mix_free, 1)

            def narrow():
                act.wait_ge(mm_done, t0 + 2)
                f, i = slice(F_ROW, F_ROW + HEADS), slice(I_ROW, I_ROW + HEADS)
                act.activation(row_z, s_bank[2][f, :], ACT.Identity, bias=col("ml_bf")[f, :])
                act.activation(row_u, s_bank[2][i, :], ACT.Identity, bias=col("ml_bi")[i, :])
                act.activation(gla_a, s_bank[2][A_ROW:A_ROW + GLA_RANK, :], ACT.Copy).then_inc(rows_in, 1)

            def log_sigmoid(rows, one, ready, done):
                for i, s in enumerate(rows):
                    act.wait_ge(ready, i + 1)
                    act.activation(s, s, ACT.Exp, scale=-1.0).then_inc(done, 1)
                for i, s in enumerate(rows):
                    act.wait_ge(done, i + 1)
                    act.activation(s, s, ACT.Ln, bias=one).then_inc(done, 1)

            one = col("one")
            plan = ([(dst, ACT.Copy, 1.0) for dst in conf_a] + [(dst, ACT.Sigmoid, 1.0) for dst in conf_g]
                    + [(dst, ACT.Copy, 1.0) for dst in sc_b + sc_c + sc_x]
                    + [(dst, ACT.Copy, DH ** -0.5) for dst in ml_q] + [(dst, ACT.Copy, 1.0) for dst in ml_k + ml_v]
                    + [(dst, ACT.Sigmoid, 1.0) for dst in ml_o]
                    + [(dst, ACT.Copy, DH ** -0.5) for dst in gla_q] + [(dst, ACT.Copy, 1.0) for dst in gla_k + gla_v]
                    + [(dst, ACT.Silu, 1.0) for dst in gla_r])
            def conf_squares():
                for i in range(2):
                    act.wait_ge(ln_dev, i + 1)
                    act.activation(ml_v[i], conf_u[i], ACT.Square).then_inc(ln_sq, 1)

            def conf_root():
                act.wait_ge(ln_var, 1)
                act.activation(ml_s_std, c_bank[:], ACT.Sqrt, bias=eps, scale=1.0 / MIX).then_inc(ln_std, 1)

            def conf_high():
                for i in range(2):
                    act.wait_ge(ln_out, i + 1)
                    act.activation(conf_u[i], conf_u[i], ACT.Silu, bias=col("ln_b", i), scale=col("ln_g", i))\
                       .then_inc(ln_act, 1)
                for i in range(2):
                    act.wait_ge(ln_act, i + 1)
                    act.activation(b_hi[1][:, 4 + i, :], conf_u[i], ACT.Copy).then_inc(ln_hi, 1)

            def short_high():
                for j in range(2):
                    act.wait_ge(sc_out, j + 1)
                    act.activation(b_hi[1][:, 6 + j, :], sc_u[j], ACT.Copy).then_inc(sc_hi, 1)

            def values_read(first, dst, src):
                for i in range(2):
                    act.wait_ge(v_turned, first + i + 1)
                    act.activation(dst[i], src[i][:], ACT.Copy).then_inc(v_read, 1)

            def weights(h):
                m = h % 2
                act.wait_ge(d_ready, h + 1)
                if h == 0:
                    act.wait_ge(u_read, 1)
                    act.wait_ge(conv_done, 4)
                if h >= 2:
                    act.wait_ge(head_ctx, h - 1)
                for blk in range(QB):
                    n = T - P * blk
                    last = act.activation(ml_w[m][:, T_AT[blk]:T_AT[blk] + n], s_bank[0][:, P * blk:T], ACT.Exp,
                                          bias=u_col[:, HEADS * blk + h:HEADS * blk + h + 1])
                last.then_inc(w_exp, 1)

            def denominators(c):
                act.wait_ge(head_ctx, 2 * c + 2)
                if c:
                    act.wait_ge(head_h, c)
                else:
                    act.wait_ge(ln_out, 2)
                act.activation(ml_den, s_bank[1][:], ACT.Abs).then_inc(den_abs, 1)

            def squares(i, src, dst, count):
                act.wait_ge(head_h if i < 2 else g_out, count)
                act.activation(dst, src, ACT.Square).then_inc(head_sq, 1)

            def squares_root(i, dst):
                act.wait_ge(head_sum, i + 1)
                src = s_bank[0] if i < 1 else acc[1]
                act.activation(dst, src[:], ACT.Sqrt, bias=eps, scale=1.0 / DH).then_inc(head_std, 1)

            def high(i, src):
                act.wait_ge(head_out, i + 1)
                act.activation(b_hi[1][:, i, :], src, ACT.Copy).then_inc(head_hi, 1)

            def row_floors():
                act.wait_ge(row_floor, 1)
                act.activation(row_b, row_b, ACT.Exp).then_inc(row_em, 1)

            before = {4: lambda: log_sigmoid((row_b,), one[0:HEADS, :], row_abs, row_ln), 6: row_floors}
            beside = {15: short_high,
                      21: lambda: (values_read(0, ml_vt, t_bank), conf_squares()),
                      22: lambda: (conf_root(), weights(0)),
                      23: lambda: weights(1),
                      24: lambda: (weights(2), denominators(0)),
                      25: lambda: weights(3),
                      26: lambda: (conf_high(), squares(0, ml_h, ml_s, 1)),
                      27: lambda: (split(PANEL0["merge"] // 2, 0, PANEL, TILE0["merge"] - 1), squares_root(0, ml_s))}
            for i in range(2, GLA + 8):
                split(half0 + i // 2, i % 2, PANEL, t0 + i - 1)
                if i == 2:
                    narrow()
                    continue
                if i in before:
                    before[i]()
                if i - 1 == GLA:
                    act.wait_ge(pad_ready, 4)
                if i - 1 == GLA + 6:
                    act.wait_ge(sc_out, 2)
                read(i - 1, *plan[i - 3])
                if i in beside:
                    beside[i]()
            denominators(1)

            for c in range(2):
                act.wait_ge(gz_ready, c + 1)
                act.activation(gla_z[c], t_bank[c][:], ACT.Identity, bias=col("gla_b", c))
                act.activation(gla_t[c], t_bank[c][:], ACT.Abs, bias=col("gla_b", c)).then_inc(gz_abs, 1)
            log_sigmoid(gla_t, one, gz_abs, gz_ln)
            high(0, ml_h)

            def decays(c):
                act.wait_ge(gz_sum, c + 1)
                s = 1.0 / GLA_TAU
                b3 = gla_b[c].rearrange("p (n t) -> p n t", t=GLA_CHUNK)
                act.activation(gla_e[c][0], gla_z[c], ACT.Exp, scale=s)
                act.activation(gla_e[c][1], gla_z[c], ACT.Exp, scale=-s)
                act.activation(gla_e[c][2], gla_b[c], ACT.Exp, scale=s)
                act.activation(gla_e[c][3], gla_t[c], ACT.Exp, scale=s)
                act.activation(gla_decay[c], b3[:, :, GLA_CHUNK - 1:GLA_CHUNK].rearrange("p n t -> p (n t)"), ACT.Exp, scale=s)\
                   .then_inc(g_exp, 1)

            decays(0)
            read(GLA + 7, *plan[-1])
            act.wait_ge(ln_lo, 2)
            values_read(2, gla_vt, acc)
            act.wait_ge(mm_done, TILE0["merge"] + 1)
            act.activation(first_gate, s_bank[0][:], ACT.Identity, bias=col("gate_b")).then_inc(gate_early, 1)
            def keys_read(c):
                act.wait_ge(kd_turned, c + 1)
                act.activation(gla_b[c], s_bank[2][:], ACT.Copy).then_inc(kd_read, 1)

            def states_read(c):
                n = P // GLA_CHUNK
                for i in range(n):
                    act.wait_ge(gu_ready, n * c + i + 1)
                    for m in range(2):
                        rows = slice(DH * m, DH * (m + 1))
                        to = gla_u[c][rows, :].rearrange("p (e b n) -> p n b e", b=QB, n=n)
                        src = u_bank[i][rows, :].rearrange("p (b e) -> p b e", b=QB)[:, :, DH * m:DH * (m + 1)]
                        last = act.activation(to[:, i, :, :], src, ACT.Copy)
                last.then_inc(gu_read, 1)

            keys_read(0)
            decays(1)
            states_read(0)
            squares(1, ml_h, ml_s, 2)
            squares_root(1, ml_s)
            half0, t0 = PANEL0["merge"] // 2, TILE0["merge"]
            split(half0, 1, PANEL, t0)
            split(half0 + 1, 0, PANEL, t0 + 1)
            keys_read(1)
            high(1, ml_h)
            squares(2, c_bank[:], gla_e[0][0], 1)
            squares_root(2, gla_e[0][0])
            states_read(1)
            high(2, gla_e[0][1])
            split(half0 + 1, 1, PANEL, t0 + 2)
            squares(3, c_bank[:], gla_e[1][0], 2)
            squares_root(3, gla_e[1][0])
            high(3, gla_e[1][1])

            def gate_of(j, m, b):
                if isinstance(j, int) and j == 0 and b == 0:
                    act.wait_ge(gate_early, 1)
                    act.activation(first_gate, first_gate, ACT.Sigmoid).then_inc(gate_done, 1)
                    return
                act.wait_ge(mm_done, 8 * j + (t0 + b + 1))
                if not (isinstance(j, int) and j < 2):
                    act.wait_ge(branch_read, 4 * j + (b - 7))
                act.activation(gate[m][b], gate_bank[b][:], ACT.Sigmoid,
                               bias=vec[:, bass.ds(j + (VEC["gate_b"] + b * KT), 1)]).then_inc(gate_done, 1)

            def merged_high(j, m):
                act.wait_ge(merge_out, j + 1)
                act.activation(b_hi[2][:, bass.ds(j, 1), :].rearrange("p a t -> p (a t)"), merged[m], ACT.Copy)\
                   .then_inc(merge_hi, 1)

            def panel_used(j, p):
                return 8 * j + (t0 + (p - 1 if p >= 2 else 0 if p == 1 else -BRANCHES))

            def merge_tile(j, jj, m):
                for p in range(5):
                    i = 5 * m + p
                    first = isinstance(j, int) and j == 0
                    if not (first and p < 4):
                        split(5 * jj + (half0 + i // 2), i % 2, PANEL, panel_used(j, p))
                    if p >= 1:
                        gate_of(j, m, p - 1)
                    if p == 1 and not first:
                        merged_high(j - 1, 1 - m)

            merge_tile(0, 0, 0)
            merge_tile(1, 0, 1)
            with act.Fori(1, KT // 2) as jj:
                merge_tile(2 * jj, jj, 0)
                merge_tile(2 * jj + 1, jj, 1)
            ready_root()

            square_y = squares_of("mix_y", y_tile, acc_free, FREE0["w_o"])
            segment("w_o", 0, KT, square_y, nothing, lambda: merged_high(KT - 1, 1), last=BRANCHES)
            square_y(KT - 1, 1)
            half0, t0 = PANEL0["ffn2"] // 2, TILE0["ffn2"]
            for s in range(2):
                split(half0, s, PANEL, t0 - 1 + s)
            root("mix_y", D)
            for k in range(KT):
                if k < 2:
                    act.wait_ge(norm_sum, NORM["mix_y"] + 1)
                else:
                    act.wait_ge(cm_added, k - 1)
                act.wait_ge(x_done, KT + k + 1)
                act.activation(sq[k % 2], x[:, k, :], ACT.Square).then_inc(cm_sq, 1)
            root("cm", D)
            modulate(KT, 3, 4)

            lead0 = lead1 = nothing
            fresh = 2
            for what, c, first in FFN2_STEPS:
                n, f0 = FFN2_CHUNKS[c], FREE0["ffn2"] + first
                hid_buf, hid0 = b_hi[1 + c % 2], HID0["ffn2"] + HID_AT[c]
                half0, t0 = (PANEL0["ffn2"] + first) // 2, TILE0["ffn2"] + first
                if what == "u":
                    def tap(j, is_v, t0=t0, hid_j=hid0 - HID0["ffn2"], last=2 * HID_T):
                        act.wait_ge(mm_done, 2 * j + (t0 + is_v + 1))
                        w_at = VEC["ffn_w"] + 2 * last + is_v * HID_T + hid_j
                        if not (isinstance(j, int) and j == 0 and hid_j == 0):
                            act.wait_ge(hid_lo if is_v else hid_out, j + (hid_j + (HID0["ffn2"] if is_v else 0)))
                        act.activation(hid_v if is_v else hid_a, acc[is_v][:], ACT.Copy,
                                       scale=vec[:, bass.ds(j + w_at, 1)]).then_inc(tap_last, 1)

                    def gate_hidden(j, f0=f0, hid_j=HID_AT[c]):
                        act.wait_ge(acc_free, 2 * j + (f0 + 1))
                        act.activation(hid_a, hid_a, ACT.Silu).then_inc(hid_silu, 1)

                    def hidden_high(j, hid_j=HID_AT[c], buf=hid_buf):
                        act.wait_ge(hid_out, j + (hid_j + 1))
                        act.activation(buf[:, bass.ds(j, 1), :].rearrange("p a t -> p (a t)"), hid_v, ACT.Copy)\
                           .then_inc(hid_hi, 1)

                    if not fresh:
                        split(half0, 0, PANEL, t0 - 1)
                    lead0()
                    if not fresh:
                        split(half0, 1, PANEL, t0)
                    lead1()
                    tap(0, 0)
                    with act.Fori(1, n) as j:
                        split(j + half0, 0, PANEL, 2 * j + (t0 - 1))
                        tap(j - 1, 1)
                        gate_hidden(j - 1)
                        split(j + half0, 1, PANEL, 2 * j + t0)
                        hidden_high(j - 1)
                        tap(j, 0)

                    def lead0(n=n, tap=tap, gate_hidden=gate_hidden):
                        tap(n - 1, 1)
                        gate_hidden(n - 1)

                    def lead1(n=n, hidden_high=hidden_high):
                        hidden_high(n - 1)
                    fresh = 0
                else:
                    mid = squares_of("ffn_y", y_tile, acc_free, f0) if c == len(FFN2_CHUNKS) - 1 else nothing
                    segment("ffn2", first, KT, mid, lead0, lead1, width=n * P)

                    if c == len(FFN2_CHUNKS) - 2:
                        ready_root()

                    def lead0(mid=mid):
                        mid(KT - 1, 1)
                    lead1 = nothing
            lead0()
            root("ffn_y", D)

        @block.vector
        def _(dve):
            steps = Steps(dve_step)

            def own(ins):
                dve.wait_ge(dve_step, steps.mark(ins))

            def split(half, slot, width=PANEL):
                dve.wait_ge(w_hi_done, 2 * half + (slot + 1))
                dve.tensor_tensor(w_lo[slot][:, 0:width], w_raw[slot][:, 0:width], w_hi[slot][:, 0:width].bitcast(F32),
                                  ALU.subtract).then_inc(w_lo_done, 1)

            def segment(run, first, n, evac, post, before0, before1, before2=None, fresh=0, beside=None, width=PANEL):
                half0 = (PANEL0[run] + first) // 2

                def panel(half, s):
                    if not (isinstance(half, int) and half == 0 and s < fresh):
                        split(half + half0, s, width)
                    if beside is not None:
                        beside(2 * half + (first + s), s)

                panel(0, 0)
                before0()
                panel(0, 1)
                before1()
                start = 1
                if before2 is not None:
                    panel(1, 0)
                    before2()
                    evac(0, 0)
                    evac(1, 1)
                    post(0, 0)
                    panel(1, 1)
                    evac(2, 0)
                    post(1, 1)
                    start = 2
                else:
                    evac(0, 0)
                with dve.Fori(start, n // 2) as half:
                    panel(half, 0)
                    evac(2 * half - 1, 1)
                    post(2 * half - 2, 0)
                    panel(half, 1)
                    evac(2 * half, 0)
                    post(2 * half - 1, 1)

            def nothing(*_):
                pass

            def x_tile(k):
                return x[:, bass.ds(k, 1), :].rearrange("p a t -> p (a t)")

            def b_tile(b, k):
                return b[:, bass.ds(k, 1), :].rearrange("p a t -> p (a t)")

            def clear(squares=ssum):
                own(dve.memset(squares, 0.0))

            def prepare(np, src, k, s, gain, dst, squares=ssum):
                dve.wait_ge(prep_hi, np + 1)
                for buf, at, g in zip(dst[0], dst[1], gain):
                    g_col = vec[:, bass.ds(k + VEC[g], 1)]
                    dve.scalar_tensor_tensor(b_tile(b_lo[buf], k + at), src, g_col,
                                             b_tile(b_hi[buf], k + at).bitcast(F32), ALU.mult, ALU.subtract)
                if not (isinstance(np, int) and np == 0):
                    dve.wait_ge(prep_lo, np)
                dve.tensor_tensor(squares, squares, sq[s], ALU.add).then_inc(prep_lo, 1)

            def prepare_x(norm, gain, dst):
                return lambda j, s: prepare(j + PREP0[norm], x_tile(j), j, s, gain, dst)

            def reciprocal_root(norm, dst=rstd):
                dve.wait_ge(norm_std, NORM[norm] + 1)
                dve.reciprocal(dst, std).then_inc(norm_rstd, 1)
                dve.wait_ge(norm_rstd, NORM[norm] + 1)

            def reciprocal_by_token(norm):
                dve.wait_ge(norm_std, NORM[norm] + 1)
                dve.reciprocal(rstd_col, std_col).then_inc(norm_rstd, 1)
                dve.wait_ge(norm_row, BY_TOKEN.index(norm) + 1)
                return c_bank[:]

            def add_to_x(t0):
                def evac(j, s):
                    dve.wait_ge(mm_done, j + (t0 + 1))
                    dve.tensor_tensor(x_tile(j), acc[s][:], x_tile(j), ALU.add).then_inc(acc_free, 1)
                return evac

            dve.wait_ge(vec_in, 16)
            clear()
            for k in range(KT):
                if k % (KT // X_PARTS) == 0:
                    dve.wait_ge(x_in[k // (KT // X_PARTS)], 16)
                dve.wait_ge(prep_hi, k + 1)
                dve.scalar_tensor_tensor(b_lo[0][:, k, :], x[:, k, :], col("mix_g0", k), b_hi[0][:, k, :].bitcast(F32),
                                         ALU.mult, ALU.subtract).then_inc(prep_lo, 1)
                if k == 1:
                    split(0, 0)
            dve.wait_ge(const_in, 16 * N_CONST)
            dve.tensor_copy(ident_b[:], ident[:])
            dve.tensor_copy(mask_b[:], mask_q[:])
            dve.wait_ge(ws_hi_done, 1)
            dve.tensor_tensor(ws_lo, ws_raw, ws_hi.bitcast(F32), ALU.subtract).then_inc(ws_lo_done, 1)
            for k in range(KT):
                dve.wait_ge(start_sq, k + 1)
                if k:
                    dve.wait_ge(start_sum, k)
                dve.tensor_tensor(ssum, ssum, sq[k % 2], ALU.add).then_inc(start_sum, 1)
                if k == 3:
                    split(0, 1)
            split(1, 0)

            def row_minima(n, m):
                for u, rows in enumerate(((3,), (2,), (1, 0))):
                    dve.wait_ge(s_ready, 3 * n + (u + 1))
                    for qb in rows:
                        w = P * (qb + 1)
                        at = 0 if qb else 2 * P
                        c = 4 * m + qb
                        last = dve.tensor_reduce(rmin[:, c:c + 1], s_bank[u][:, at:at + w], AX_X, ALU.min)
                    last.then_inc(row_min, 1)

            def normalise(n, m):
                dve.wait_ge(p_exp, 3 * n + 3)
                own(dve.reciprocal(rinv[:, 4 * m:4 * m + 4], rsum[:, 4 * m:4 * m + 4]))
                for qb in range(QB):
                    part = probs[m][:, P_AT[qb]:P_AT[qb] + P * (qb + 1)]
                    last = dve.tensor_scalar(part, part, rinv[:, 4 * m + qb:4 * m + qb + 1], None, ALU.mult)
                last.then_inc(p_ready, 1)

            def low_context(k, buf, count):
                dve.wait_ge(ctx_hi, count)
                dve.tensor_tensor(b_tile(b_lo[buf], k), c_bank[:], b_tile(b_hi[buf], k).bitcast(F32), ALU.subtract)\
                   .then_inc(ctx_lo, 1)

            def forget_gates():
                dve.wait_ge(f_mm, 1)
                z, s, a = fz[2], fz[3], fz[0]
                own(dve.tensor_tensor(s, s_bank[0][0:FOX_HEADS, :], rstd[0:FOX_HEADS, :], ALU.mult))
                own(dve.tensor_scalar(z, s, col("fox_bf")[0:FOX_HEADS, :], None, ALU.add))
                dve.scalar_tensor_tensor(s, z, -1.0, z, ALU.mult, ALU.max).then_inc(f_abs, 1)

            def sum_forget_gates():
                z, s, a = fz[2], fz[3], fz[0]
                dve.wait_ge(f_ln, 2)
                dve.wait_ge(ones_set, 2)
                own(dve.scalar_tensor_tensor(a, z, 0.0, s, ALU.min, ALU.subtract))
                dve.tensor_tensor_scan(z, fz[1], a, 0.0, ALU.mult, ALU.add).then_inc(f_cum, 1)
                dve.wait_ge(f_cum, 1)
                dve.tensor_scalar(a, z, -1.0, None, ALU.mult).then_inc(f_cum, 1)

            def heads_rows(dst, t, slot, scale):
                dve.wait_ge(mm_done, t + 1)
                for h in range(2):
                    rows = slice(FOX_DH * h, FOX_DH * (h + 1))
                    last = dve.scalar_tensor_tensor(dst[h][0:FOX_DH, :], acc[slot][rows, :], scale, rstd[rows, :],
                                                    ALU.mult, ALU.mult)
                last.then_inc(acc_free, 1)

            def fox_step(pp, m, project=True, attend=True, late=True):
                p = 2 * pp + m
                c = 7 * p - 6
                if project:
                    if not attend:
                        reciprocal_root("fox")
                    else:
                        split(3 * pp + (3 * m + 1) // 2, 1 - m)
                    heads_rows(qa[m], 3 * p, m, -FOX_SCALE)
                    if not attend:
                        clear()
                        split(3 * pp + (3 * m + 3) // 2, 1 - m)
                        forget_gates()
                if late:
                    low_context(p - 2, 1, p - 1)
                if attend:
                    row_minima(2 * p - 2, 0)
                if project and attend:
                    split(3 * pp + (3 * m + 2) // 2, m)
                if attend:
                    normalise(2 * p - 2, 0)
                if project:
                    heads_rows(ka[m], 3 * p + 1, 1 - m, 1.0)
                if attend:
                    row_minima(2 * p - 1, 1)
                if project and attend:
                    split(3 * pp + (3 * m + 3) // 2, 1 - m)
                if attend:
                    normalise(2 * p - 1, 1)
                if project:
                    dve.wait_ge(mm_done, 3 * p + 3)
                    if attend:
                        dve.wait_ge(t_ready, c)
                    dve.tensor_tensor(v_t, acc[m][:], rstd, ALU.mult).then_inc(acc_free, 1)
                if not attend:
                    sum_forget_gates()

            fox_step(0, 0, attend=False, late=False)
            fox_step(0, 1, late=False)
            with dve.Fori(1, FOX_PAIRS // 2) as pp:
                steps.enter(pp - 1, 4)
                fox_step(pp, 0)
                fox_step(pp, 1)
            steps.leave(FOX_PAIRS // 2 - 1)
            split(PANEL0["fox_out"] // 2, 1)
            fox_step(FOX_PAIRS // 2, 0, project=False)

            out_a, post_a = add_to_x(TILE0["fox_out"]), prepare_x("ff_a", ("ff_g0",), ((0,), (0,)))
            segment("fox_out", 0, KT, out_a, post_a, nothing, lambda: low_context(FOX_PAIRS - 1, 1, FOX_PAIRS), nothing,
                    fresh=2)

            def ffn(run, hid, evac, post, norm, last_post, beside):
                for i, (what, c) in enumerate(FF_ORDER):
                    t0 = TILE0[run] + i * KT

                    def relu(j, s, t0=t0, c=c):
                        n = j + (HID0[run] + c * KT)
                        dve.wait_ge(mm_done, j + (t0 + 1))
                        if not (isinstance(n, int) and n < 2):
                            dve.wait_ge(ff_sq, n - 1)
                        dve.scalar_tensor_tensor(ff_t[s], acc[s][:], 0.0, rstd, ALU.max, ALU.mult).then_inc(acc_free, 1)

                    def low(j, s, c=c):
                        n = j + (HID0[run] + c * KT)
                        dve.wait_ge(sq_hi, n + 1)
                        dve.tensor_tensor(b_tile(b_lo[hid[c % 2]], j), ff_s[s],
                                          b_tile(b_hi[hid[c % 2]], j).bitcast(F32), ALU.subtract).then_inc(hid_lo, 1)

                    def lead0():
                        evac(KT - 1, 1)
                        post(KT - 2, 0)

                    def lead1():
                        post(KT - 1, 1)
                        if i == 1:
                            clear()
                            if norm == "ff_b":
                                clear(ssum_g)

                    if what == "u":
                        now = relu, low
                    else:
                        now = add_to_x(t0), last_post if c == FF_CHUNKS - 1 else nothing
                    segment(run, i * KT, KT, *now, lead0, lead1, (lambda: reciprocal_root(norm)) if i == 0 else None,
                            beside=beside if 1 <= i < 7 else None)
                    evac, post = now
                return evac, post

            def conditioning(j, s):
                j = j - KT
                if isinstance(j, int) and j == 0:
                    dve.wait_ge(ada_silu, 1)
                dve.wait_ge(ada_in[s], (j - s) * 8 + 16)
                if not (isinstance(j, int) and j == 0):
                    dve.wait_ge(ada_done, j)
                dve.scalar_tensor_tensor(ada_p, ada_w[s], 1.0, ada_c, ALU.mult, ALU.mult,
                                         accum_out=mod[:, bass.ds(j, 1)]).then_inc(ada_done, 1)

            evac, post = ffn("ff_a", (1, 2), out_a, post_a, "ff_a",
                             prepare_x("mla", ("mix_g1", "kv_g"), ((0, 1), (0, 0))), conditioning)

            half0, t0 = PANEL0["low"] // 2, TILE0["low"]
            split(half0, 0)
            evac(KT - 1, 1)
            post(KT - 2, 0)
            split(half0, 1)
            post(KT - 1, 1)
            split(half0 + 1, 0)
            reciprocal_root("mla")

            def prepare_low(norm, n, at):
                for j in range(n):
                    prepare(PREP0[norm] + j, low[at + j], j, (PREP0[norm] + j) % 2,
                            ("kva_g" if norm == "ckv" else "qa_g",), ((2,), (at,)), low_sum if norm == "ckv" else ssum)

            def low_tile(i):
                dve.wait_ge(mm_done, t0 + i + 1)
                dve.tensor_tensor(low[i], acc[i % 2][:], rstd, ALU.mult).then_inc(acc_free, 1)

            low_tile(0)
            low_tile(1)
            split(half0 + 1, 1)
            low_tile(2)
            clear()
            clear(low_sum)
            split(half0 + 2, 0)
            low_tile(3)
            prepare_low("cq", QKT, 0)
            split(half0 + 2, 1)
            dve.wait_ge(rope_in, 32)
            v = steps.mark(dve.tensor_tensor(kr_tmp, rope, rstd, ALU.mult))
            low_tile(4)
            prepare_low("ckv", KVKT, QKT)
            split(PANEL0["mla"] // 2, 0, Q_COLS)
            dve.wait_ge(mm_done, t0 + QKT + KVKT + 1)
            dve.wait_ge(dve_step, v)
            dve.tensor_tensor(kr_raw, acc[1][:], kr_tmp, ALU.mult).then_inc(acc_free, 1)
            split(PANEL0["mla"] // 2, 1, KV_COLS)
            reciprocal_root("cq", rstd_q)
            v = steps.mark(dve.scalar_tensor_tensor(rope_q, rope, -MLA_SCALE, rstd_q, ALU.mult, ALU.mult))
            dve.wait_ge(kr_mm, 1)
            dve.tensor_copy(k_rope, s_bank[0][:]).then_inc(kr_done, 1)
            dve.wait_ge(dve_step, v)

            def mla_step(hh, m, project=True, attend=True, late=True, ahead=True):
                h = 2 * hh + m
                n = h + HEAD0["mla"]
                t = 4 * h + TILE0["mla"]
                if project:
                    dve.wait_ge(mm_done, t + 1)
                    dve.scalar_tensor_tensor(qa[m][0], acc[0][:], -MLA_SCALE, rstd_q, ALU.mult, ALU.mult).then_inc(acc_free, 1)
                    dve.wait_ge(mm_done, t + 2)
                    dve.tensor_tensor(qa[m][1], acc[1][:], rope_q, ALU.mult).then_inc(acc_free, 1)
                    if not attend:
                        reciprocal_root("ckv", rstd_kv)
                        clear()
                if attend:
                    row_minima(n - 1, 1 - m)
                if project:
                    dve.wait_ge(mm_done, t + 3)
                    dve.tensor_tensor(ka[m][0], acc[0][:], rstd_kv, ALU.mult).then_inc(acc_free, 1)
                    dve.wait_ge(mm_done, t + 4)
                    if attend:
                        dve.wait_ge(t_ready, 4 * h + (T0_MLA - 6) if late else T0_MLA + 1)
                    dve.tensor_tensor(v_t, acc[1][:], rstd_kv, ALU.mult).then_inc(acc_free, 1)
                if ahead:
                    split(h + (PANEL0["mla"] // 2 + 1), 0, Q_COLS)
                if attend:
                    normalise(n - 1, 1 - m)
                if ahead:
                    split(h + (PANEL0["mla"] // 2 + 1), 1, KV_COLS)
                if late:
                    low_context(h - 2, 0, h + (CTX0["mla"] - 1))

            mla_step(0, 0, attend=False, late=False)
            mla_step(0, 1, late=False)
            with dve.Fori(1, MLA_HEADS // 2 - 1) as hh:
                steps.enter(hh - 1, 2)
                mla_step(hh, 0)
                mla_step(hh, 1)
            steps.leave(MLA_HEADS // 2 - 2)
            mla_step(MLA_HEADS // 2 - 1, 0)
            mla_step(MLA_HEADS // 2 - 1, 1, ahead=False)
            split(PANEL0["mla_out"] // 2, 0)
            split(PANEL0["mla_out"] // 2, 1)
            mla_step(MLA_HEADS // 2, 0, project=False, ahead=False)

            out_b, post_b = add_to_x(TILE0["mla_out"]), prepare_x("ff_b", ("ff_g1",), ((1,), (0,)))
            segment("mla_out", 0, KT, out_b, post_b, nothing,
                    lambda: low_context(MLA_HEADS - 1, 0, CTX0["mla"] + MLA_HEADS), nothing, fresh=2)

            def add_squares(norm):
                def post(j, s):
                    dve.wait_ge(prep_hi, j + (PREP0[norm] + 1))
                    dve.wait_ge(prep_lo, j + PREP0[norm])
                    dve.tensor_tensor(ssum, ssum, sq[s], ALU.add).then_inc(prep_lo, 1)
                return post

            def y_tile(j):
                return arena[:, bass.ds(j + y_at, 1), :].rearrange("p a t -> p (a t)")

            def add_both(j, s):
                dve.wait_ge(prep_hi, j + (PREP0["final"] + 1))
                dve.wait_ge(prep_lo, j + PREP0["final"])
                dve.tensor_tensor(ssum, ssum, sq[s], ALU.add)
                dve.tensor_tensor(ssum_g, ssum_g, sq_g[s], ALU.add).then_inc(prep_lo, 1)

            evac, post = ffn("ff_b", (0, 2), out_b, post_b, "ff_b", add_both, None)
            evac(KT - 1, 1)
            post(KT - 2, 0)
            post(KT - 1, 1)
            dve.wait_ge(prep_lo, PREP0["final"] + KT)
            dve.scalar_tensor_tensor(ssum_g, ssum, EPS, ssum_g, ALU.mult, ALU.add).then_inc(both_sum, 1)
            half0, t0 = PANEL0["mix_in"] // 2, TILE0["mix_in"]
            for s in range(2):
                split(half0, s, PANEL // 2)

            dve.wait_ge(ada_done, 6 * KT)
            own(dve.tensor_tensor(mod[:], mod[:], vec[:, VEC["ada_b"]:VEC["ada_b"] + 6 * KT], ALU.add))
            for i, gain, plus in ((1, "tm_pre_g", 1.0), (2, "tm_post_g", 0.0), (4, "cm_pre_g", 1.0), (5, "cm_post_g", 0.0)):
                part = mod[:, i * KT:(i + 1) * KT]
                last = dve.scalar_tensor_tensor(part, part, plus, vec[:, VEC[gain]:VEC[gain] + KT], ALU.add, ALU.mult)
            own(last)
            part = mod[:, KT:2 * KT]
            dve.tensor_tensor(part, part, vec[:, VEC["final_g"]:VEC["final_g"] + KT], ALU.mult).then_inc(mod_ready, 1)
            row = reciprocal_by_token("x2")

            def modulate(n0, row):
                def normed(k):
                    if n0 + k >= 4:
                        dve.wait_ge(h_hi, n0 + k - 3)
                    dve.tensor_tensor(mod_t[k % 4], x[:, k, :], row, ALU.mult).then_inc(h_tmp, 1)

                for k in range(2):
                    normed(k)
                for k in range(KT):
                    if k + 2 < KT:
                        normed(k + 2)
                    dve.wait_ge(h_hi, n0 + k + 1)
                    dve.tensor_tensor(b_lo[0][:, k, :], mod_y[k % 4], b_hi[0][:, k, :].bitcast(F32), ALU.subtract)\
                       .then_inc(h_lo, 1)

            modulate(0, row)

            def head_gates():
                dve.wait_ge(rows_in, 1)
                dve.scalar_tensor_tensor(row_b, row_z, -1.0, row_z, ALU.mult, ALU.max).then_inc(row_abs, 1)

            def gate_sums():
                dve.wait_ge(row_ln, 2)
                own(dve.scalar_tensor_tensor(row_z, row_z, 0.0, row_b, ALU.min, ALU.subtract))
                own(dve.tensor_tensor_scan(row_b, row_z, row_z, 0.0, ALU.add, ALU.min))
                dve.tensor_tensor(row_u, row_u, row_b, ALU.subtract).then_inc(row_u_done, 1)

            def gate_maxima():
                dve.wait_ge(row_u_done, 1)
                own(dve.tensor_tensor_scan(row_z, row_u, row_u, 0.0, ALU.max, ALU.max))
                dve.tensor_scalar(row_z, row_z, -1.0, None, ALU.mult).then_inc(row_max, 1)
                dve.wait_ge(row_max, 1)
                dve.tensor_tensor(row_b, row_z, row_b, ALU.subtract).then_inc(row_floor, 1)

            def gated(i):
                dve.wait_ge(mix_free, CONF + 2 + i - 1)
                if i == 0:
                    dve.wait_ge(pads_set, 5)
                at = i * CONF_PAD + CONF_W - 1
                dve.tensor_tensor(conf_pad[:, at:at + T], conf_a[i], conf_g[i], ALU.mult).then_inc(pad_ready, 1)
                dve.wait_ge(pad_ready, i + 1)
                own(dve.tensor_scalar(conf_u[i], conf_pad[:, i * CONF_PAD:i * CONF_PAD + T], col("conf_w", i),
                                      col("conf_b", i), ALU.mult, ALU.add))

            def short(i):
                dve.wait_ge(mix_free, SC + 4 + i - 1)
                at = i * SC_PAD
                dve.tensor_tensor(sc_pad[:, at + SC_W - 1:at + SC_W - 1 + T], sc_c[i], sc_x[i], ALU.mult).then_inc(pad_ready, 1)
                dve.wait_ge(pad_ready, 3 + i)
                own(dve.tensor_scalar(sc_u[i], sc_pad[:, at:at + T], col("sc_w", i), None, ALU.mult))
                for tap in range(1, SC_W):
                    ins = dve.scalar_tensor_tensor(sc_u[i], sc_pad[:, at + tap:at + tap + T], col("sc_w", 2 * tap + i),
                                                   sc_u[i], ALU.mult, ALU.add)
                    if tap < SC_W - 1:
                        own(ins)
                ins.then_inc(conv_done, 1)
                dve.wait_ge(conv_done, i + 1)
                dve.tensor_tensor(sc_u[i], sc_u[i], sc_b[i], ALU.mult).then_inc(sc_out, 1)

            def sc_low(i):
                dve.wait_ge(sc_hi, i + 1)
                dve.tensor_tensor(b_lo[1][:, 6 + i, :], sc_u[i], b_hi[1][:, 6 + i, :].bitcast(F32), ALU.subtract)\
                   .then_inc(sc_lo, 1)

            def finish_x(first):
                for k in (first, first + 1):
                    dve.scalar_tensor_tensor(x[:, k, :], x[:, k, :], col("final_g", k), rstd_f, ALU.mult, ALU.mult)\
                       .then_inc(x_done, 1)

            TAPS = 3

            def long_taps(first, turns, tap0):
                with dve.Fori(0, turns) as half:
                    steps.enter(half, 4 * TAPS)
                    for s in range(2):
                        split(half + (half0 + first // 2), s)
                        for t in range(TAPS):
                            for i in range(2):
                                dve.wait_ge(dve_step, steps.moved + steps.count - 1)
                                at = half * (2 * TAPS) + (tap0 + TAPS * s + t + i * CONF_PAD)
                                w = half * (4 * TAPS) + (VEC["conf_w"] + 2 * (tap0 + TAPS * s + t) + i)
                                steps.mark(dve.scalar_tensor_tensor(conf_u[i], conf_pad[:, bass.ds(at, T)],
                                                                    vec[:, bass.ds(w, 1)], conf_u[i], ALU.mult, ALU.add))
                steps.leave(turns)

            def conf_deviations():
                dve.wait_ge(ln_mean, 1)
                for i in range(2):
                    dve.scalar_tensor_tensor(conf_u[i], c_bank[:], -1.0 / MIX, conf_u[i], ALU.mult, ALU.add)\
                       .then_inc(ln_dev, 1)

            def conf_normed():
                for i in range(2):
                    dve.tensor_tensor(conf_u[i], conf_u[i], ml_s_std, ALU.mult).then_inc(ln_out, 1)

            def conf_low():
                for i in range(2):
                    dve.wait_ge(ln_hi, i + 1)
                    dve.tensor_tensor(b_lo[1][:, 4 + i, :], conf_u[i], b_hi[1][:, 4 + i, :].bitcast(F32), ALU.subtract)\
                       .then_inc(ln_lo, 1)

            def conf_reciprocal():
                dve.wait_ge(ln_std, 1)
                own(dve.reciprocal(ml_s_std, ml_s_std))

            def gates_by_key():
                dve.wait_ge(u_turned, 1)
                dve.tensor_copy(u_col, s_bank[2][:, 0:QB * HEADS]).then_inc(u_read, 1)

            def weigh(h):
                w = ml_w[h % 2]
                dve.wait_ge(qk_ready, h + 1)
                dve.wait_ge(w_exp, h + 1)
                if h == 0:
                    dve.wait_ge(const2_in, 16 * N_CONST2)
                for at, src, n in ((0, t_bank[0], T), (T, t_bank[1], T), (2 * T, s_bank[2], 2 * P)):
                    last = dve.tensor_tensor(w[:, at:at + n], src[:, 0:n], w[:, at:at + n], ALU.mult)
                own(last)
                for at, step in ((T_AT[0], T_AT[1] - T_AT[0]), (T_AT[3], T_AT[2] - T_AT[3])):
                    blocks = w[:, at:at + 2 * step].rearrange("p (b t) -> p b t", b=2)[:, :, 0:P]
                    mask, none = (x_.rearrange("p (b t) -> p b t", b=1).to_broadcast([P, 2, P]) for x_ in (mask_low[:], zeros))
                    last = dve.copy_predicated(blocks, mask, none)
                last.then_inc(a_ready, 1)

            def quotient(c):
                dve.wait_ge(floor_ready, c + 1)
                own(dve.tensor_tensor(ml_den, ml_den, s_bank[1][:], ALU.max))
                own(dve.reciprocal(ml_den, ml_den))
                dve.tensor_tensor(ml_h, c_bank[:], ml_den, ALU.mult).then_inc(head_h, 1)

            def head_norm(i, src, root, dst, gain, gates):
                dve.wait_ge(head_std, i + 1)
                own(dve.reciprocal(root, root))
                if i < 2:
                    own(dve.tensor_tensor(dst, src, root, ALU.mult))
                else:
                    dve.tensor_tensor(dst, src, root, ALU.mult).then_inc(head_h, 1)
                    dve.wait_ge(head_h, i + 1)
                dve.scalar_tensor_tensor(dst, dst, gain, gates, ALU.mult, ALU.mult).then_inc(head_out, 1)

            def head_low(i, src):
                dve.wait_ge(head_hi, i + 1)
                dve.tensor_tensor(b_lo[1][:, i, :], src, b_hi[1][:, i, :].bitcast(F32), ALU.subtract).then_inc(head_lo, 1)

            beside = {2: lambda: reciprocal_root("final", rstd_f), 3: head_gates,
                      4: gate_sums, 5: lambda: (gate_maxima(), finish_x(0)),
                      6: lambda: (gated(0), finish_x(2)), 7: lambda: (gated(1), finish_x(4)),
                      12: lambda: short(0), 13: lambda: short(1),
                      20: lambda: (finish_x(6), sc_low(0), sc_low(1)),
                      21: lambda: (gates_by_key(), conf_deviations()),
                      22: lambda: (weigh(0), conf_reciprocal()),
                      23: lambda: (weigh(1), conf_normed()),
                      24: lambda: weigh(2),
                      25: lambda: quotient(0),
                      26: lambda: (weigh(3), conf_low()),
                      27: lambda: (split(PANEL0["merge"] // 2, 0), head_norm(0, ml_h, ml_s, ml_h, col("ml_g", 0), ml_o[0]))}

            def panels(first, last):
                for i in range(first, last):
                    split(half0 + i // 2, i % 2)
                    if i in beside:
                        beside[i]()

            panels(2, 8)
            long_taps(8, 2, 1)
            panels(12, 14)
            long_taps(14, 3, 1 + 4 * TAPS)
            dve.wait_ge(dve_step, steps.count)
            dve.sem_inc(conv_done, 2)
            panels(GLA, GLA + 8)

            def decay_sums(c):
                dve.wait_ge(gz_ln, c + 3)
                if c:
                    dve.wait_ge(v_turned, 4)
                own(dve.scalar_tensor_tensor(gla_z[c], gla_z[c], 0.0, gla_t[c], ALU.min, ALU.subtract))
                own(dve.tensor_tensor_scan(gla_b[c], chunk_start, gla_z[c], 0.0, ALU.mult, ALU.add))
                b3, z3, t3 = (x_.rearrange("p (n t) -> p n t", t=GLA_CHUNK) for x_ in (gla_b[c], gla_z[c], gla_t[c]))
                half = GLA_CHUNK // 2
                shape = [P, CHUNKS, GLA_CHUNK]
                dve.tensor_tensor(z3, b3, b3[:, :, half - 1:half].to_broadcast(shape), ALU.subtract)
                dve.tensor_tensor(t3, b3[:, :, GLA_CHUNK - 1:GLA_CHUNK].to_broadcast(shape), b3, ALU.subtract)\
                   .then_inc(gz_sum, 1)

            decay_sums(0)
            head_low(0, ml_h)

            def scaled(c):
                dve.wait_ge(g_exp, c + 1)
                dve.memset(gla_decay[c][:, 0:1], 0.0)
                for e, src in zip(gla_e[c], (gla_q[c], gla_k[c], gla_q[c], gla_k[c])):
                    last = dve.tensor_tensor(e, e, src, ALU.mult)
                last.then_inc(g_scaled, 1)

            def masked(c):
                dve.wait_ge(gs_ready, c + 1)
                dve.wait_ge(gw_set, 2)
                if c:
                    dve.wait_ge(g_out, c)
                for m in range(2):
                    w3, s3 = (x_.rearrange("p (b t) -> p b t", b=QB) for x_ in (gla_w[m], t_bank[m][:]))
                    mask = mask_gla[:].rearrange("p (b t) -> p b t", b=1).to_broadcast([P, QB, P])
                    last = dve.copy_predicated(w3, mask, s3)
                last.then_inc(gs_read, 1)

            def states(c):
                dve.wait_ge(g_scaled, c + 1)
                decay = gla_decay[c].rearrange("p (e n) -> p e n", e=1).to_broadcast([P, DH, CHUNKS])
                own(dve.tensor_copy(gla_s[c].rearrange("p (e n) -> p e n", n=CHUNKS), decay))
                dve.wait_ge(gu_read, c + 1)
                last = dve.tensor_tensor_scan(gla_s[c], gla_s[c], gla_u[c], 0.0, ALU.mult, ALU.add)
                last.then_inc(g_state, 1)

            def gla_norm(c):
                head_norm(2 + c, c_bank[:], gla_e[c][0], gla_e[c][1], col("gla_g", c), gla_r[c])
                head_low(2 + c, gla_e[c][1])

            scaled(0)
            decay_sums(1)
            quotient(1)
            masked(0)
            scaled(1)
            states(0)
            head_norm(1, ml_h, ml_s, ml_h, col("ml_g", 1), ml_o[1])
            half0, t0 = PANEL0["merge"] // 2, TILE0["merge"]
            split(half0, 1)
            split(half0 + 1, 0)
            masked(1)
            head_low(1, ml_h)
            gla_norm(0)
            states(1)
            split(half0 + 1, 1)
            gla_norm(1)

            def branches(j, m):
                for b in range(BRANCHES):
                    g = gate_at(j, m, b)
                    dve.wait_ge(mm_done, 8 * j + (t0 + BRANCHES + b + 1))
                    dve.wait_ge(gate_done, 4 * j + (b + 1))
                    if b == 2:
                        bias = vec[:, bass.ds(j + VEC["conf_out_b"], 1)]
                        ins = dve.scalar_tensor_tensor(g, branch_bank[b][:], bias, g, ALU.add, ALU.mult)
                    else:
                        ins = dve.tensor_tensor(g, branch_bank[b][:], g, ALU.mult)
                    ins.then_inc(branch_read, 1)
                if not (isinstance(j, int) and j < 2):
                    dve.wait_ge(merge_hi, j - 1)
                dve.wait_ge(branch_read, 4 * j + BRANCHES)
                own(dve.tensor_tensor(merged[m], gate_at(j, m, 0), gate[m][1], ALU.add))
                own(dve.tensor_tensor(merged[m], merged[m], gate[m][2], ALU.add))
                dve.tensor_tensor(merged[m], merged[m], gate[m][3], ALU.add).then_inc(merge_out, 1)

            def merged_low(j, m):
                dve.wait_ge(merge_hi, j + 1)
                dve.tensor_tensor(b_tile(b_lo[2], j), merged[m], b_tile(b_hi[2], j).bitcast(F32), ALU.subtract)\
                   .then_inc(merge_lo, 1)

            def merge_tile(j, jj, m):
                first = isinstance(j, int) and j == 0
                for p in range(5):
                    i = 5 * m + p
                    if not (first and p < 4):
                        split(5 * jj + (half0 + i // 2), i % 2)
                    if not first and p == 0:
                        branches(j - 1, 1 - m)
                    if not first and p == 1:
                        merged_low(j - 1, 1 - m)

            merge_tile(0, 0, 0)
            merge_tile(1, 0, 1)
            with dve.Fori(1, KT // 2) as jj:
                steps.enter(jj - 1, 4)
                merge_tile(2 * jj, jj, 0)
                merge_tile(2 * jj + 1, jj, 1)
            steps.leave(KT // 2 - 1)

            def keep(t0):
                def evac(j, s):
                    dve.wait_ge(mm_done, j + (t0 + 1))
                    dve.tensor_copy(y_tile(j), acc[s][:]).then_inc(acc_free, 1)
                return evac

            def start_y():
                merged_low(KT - 1, 1)
                clear()

            evac, post = keep(TILE0["w_o"]), add_squares("mix_y")
            segment("w_o", 0, KT, evac, post, lambda: branches(KT - 1, 1), start_y)
            evac(KT - 1, 1)
            post(KT - 2, 0)
            post(KT - 1, 1)
            half0, t0 = PANEL0["ffn2"] // 2, TILE0["ffn2"]
            for s in range(2):
                split(half0, s)
            row = reciprocal_by_token("mix_y")

            def add_normed(n0, scale, row):
                dve.tensor_copy(rstd, row).then_inc(rstd_set, 1)
                dve.wait_ge(rstd_set, n0 // (KT // 2) + 1)

                def scaled(k):
                    return steps.mark(dve.tensor_tensor(y[k], y[k], rstd, ALU.mult))

                y = [ar(y_at + k) for k in range(KT)]
                v = scaled(0)
                for k in range(KT):
                    if k % 2 == 0:
                        now, v = v, scaled(k + 2) if k + 2 < KT else None
                        dve.wait_ge(dve_step, now)
                    else:
                        dve.wait_ge(y_normed, n0 + k // 2 + 1)
                    dve.scalar_tensor_tensor(x[:, k, :], y[k], mod[:, scale * KT + k:scale * KT + k + 1], x[:, k, :],
                                             ALU.mult, ALU.add).then_inc(x_done, 1)

            add_normed(0, 2, row)
            reciprocal_root("cm")
            modulate(KT, rstd)

            lead0 = lead1 = nothing
            fresh = 2
            for what, c, first in FFN2_STEPS:
                n, f0 = FFN2_CHUNKS[c], FREE0["ffn2"] + first
                half0, t0 = (PANEL0["ffn2"] + first) // 2, TILE0["ffn2"] + first
                if what == "u":
                    def taps(j, is_v, f0=f0, hid_j=HID_AT[c]):
                        dst = hid_v if is_v else hid_a
                        dve.wait_ge(tap_last, 2 * j + (2 * hid_j + is_v + 1))
                        for tap in (1, 0):
                            back = FFN_W - 1 - tap
                            w = vec[:, bass.ds(j + (VEC["ffn_w"] + tap * 2 * HID_T + is_v * HID_T + hid_j), 1)]
                            ins = dve.scalar_tensor_tensor(dst[:, back:T], acc[is_v][:, 0:T - back], w, dst[:, back:T],
                                                           ALU.mult, ALU.add)
                            if tap:
                                own(ins)
                        ins.then_inc(acc_free, 1)

                    def product(j, f0=f0, hid_j=HID_AT[c]):
                        dve.wait_ge(hid_silu, j + (hid_j + 1))
                        dve.wait_ge(acc_free, 2 * j + (f0 + 2))
                        dve.tensor_tensor(hid_v, hid_a, hid_v, ALU.mult).then_inc(hid_out, 1)

                    def hidden_low(j, hid_j=HID_AT[c], buf=1 + c % 2):
                        dve.wait_ge(hid_hi, j + (hid_j + 1))
                        dve.tensor_tensor(b_tile(b_lo[buf], j), hid_v, b_tile(b_hi[buf], j).bitcast(F32), ALU.subtract)\
                           .then_inc(hid_lo, 1)

                    if not fresh:
                        split(half0, 0)
                    lead0()
                    if not fresh:
                        split(half0, 1)
                    lead1()
                    taps(0, 0)
                    with dve.Fori(1, n) as j:
                        steps.enter(j - 1, 2)
                        split(j + half0, 0)
                        taps(j - 1, 1)
                        product(j - 1)
                        split(j + half0, 1)
                        hidden_low(j - 1)
                        taps(j, 0)
                    steps.leave(n - 1)

                    def lead0(n=n, taps=taps, product=product):
                        taps(n - 1, 1)
                        product(n - 1)

                    def lead1(n=n, hidden_low=hidden_low):
                        hidden_low(n - 1)
                    fresh = 0
                else:
                    def add_to_y(j, s, t0=t0):
                        dve.wait_ge(mm_done, j + (t0 + 1))
                        dve.tensor_tensor(y_tile(j), acc[s][:], y_tile(j), ALU.add).then_inc(acc_free, 1)

                    evac = add_to_y if c else keep(t0)
                    post = add_squares("ffn_y") if c == len(FFN2_CHUNKS) - 1 else nothing

                    def start_down(lead1=lead1, c=c):
                        lead1()
                        if c == len(FFN2_CHUNKS) - 1:
                            clear()

                    segment("ffn2", first, KT, evac, post, lead0, start_down, width=n * P)

                    def lead0(evac=evac, post=post):
                        evac(KT - 1, 1)
                        post(KT - 2, 0)

                    def lead1(post=post):
                        post(KT - 1, 1)
            lead0()
            lead1()
            add_normed(KT // 2, 5, reciprocal_by_token("ffn_y"))


def kernel(**inputs):
    import concourse.bacc as _bacc
    from concourse.bass_utils import run_bass_kernel_spmd as _run

    laid = lay_out(inputs)
    nc = _bacc.Bacc("TRN2", target_bir_lowering=False, num_devices=1)
    d = {}
    for name, a in laid.items():
        d[name] = nc.dram_tensor(f"in_{name}", a.shape, mybir.dt.from_np(a.dtype), kind="ExternalInput").ap()
    out = nc.dram_tensor("out_xT", (P, KT * T), F32, kind="ExternalOutput").ap()
    crow = nc.dram_tensor("crow", (FOX_HEADS, 4, T), F32, kind="Internal").ap()
    program(nc, d, out, crow)
    r = _run(nc, [{f"in_{name}": a for name, a in laid.items()}], core_ids=[0])
    got = r.results[0]["out_xT"]
    return got.reshape(P, KT, T).transpose(1, 0, 2).reshape(D, T).T.reshape(1, T, D)
```
